# Optimizing a Trainium2 kernel written in Bass

```python
import jax, jax.numpy as jnp
from jax import lax
import numpy as np

D_MODEL = 1024
BATCH = 1
SEQ = 1024
DEPTH = 1
DEC_BATCH = 8
DEC_SEQ = 8
PAST_LEN = 1024
PAGE_SIZE = 128

HEAD_DIM = 64
N_ATT_HEADS = 8
ATT_WIDTH = N_ATT_HEADS * HEAD_DIM
N_ML_HEADS = 8
ML_WIDTH = N_ML_HEADS * HEAD_DIM
DIL_GROUPS = ((128, 1), (512, 4), (2048, 16))
W_MAX = max(w for w, _ in DIL_GROUPS)
ML_CHUNK = 64
CONV_W = 4
N_MEM = 256
N_X_HEADS = 4
X_HEAD_DIM = D_MODEL // N_X_HEADS
D_FF = -(-8 * D_MODEL // (3 * 256)) * 256
RMS_EPS = 1e-6
NEG_INIT = -1e30
PROJ_SPLITS = (ATT_WIDTH, ATT_WIDTH, ATT_WIDTH, 2 * ML_WIDTH, ML_WIDTH, ML_WIDTH, N_ML_HEADS, N_ML_HEADS)
N_IN = sum(PROJ_SPLITS)

kernel_name = 'hybrid_dilated_attn_mlstm_decoder_step'

def rmsnorm(x, g):
    xf = x.astype(jnp.float32)
    y = xf * lax.rsqrt(jnp.mean(xf * xf, axis=-1, keepdims=True) + RMS_EPS)
    return (y * g.astype(jnp.float32)).astype(x.dtype)

def heads(t, n):
    return t.reshape(t.shape[:-1] + (n, t.shape[-1] // n))

def split_proj(z):
    parts, o = [], 0
    for w in PROJ_SPLITS:
        parts.append(z[..., o:o + w])
        o += w
    return parts

def alibi_slopes(n):
    return jnp.exp2(-8.0 * (jnp.arange(n, dtype=jnp.float32) + 1.0) / n)

def dilated_prompt(q, k, v, window, dil, slopes):
    B, S, H, Dh = q.shape
    band = window // dil
    L = S // dil
    nb = -(-L // band)
    Lp = nb * band

    def to_res(t):
        t = t.reshape(B, L, dil, H, Dh).transpose(0, 2, 1, 3, 4).reshape(B * dil, L, H, Dh)
        t = jnp.pad(t, ((0, 0), (0, Lp - L), (0, 0), (0, 0)))
        return t.reshape(B * dil, nb, band, H, Dh)

    def with_prev(t):
        prev = jnp.pad(t, ((0, 0), (1, 0), (0, 0), (0, 0), (0, 0)))[:, :-1]
        return jnp.concatenate([prev, t], axis=2)

    qb = to_res(q)
    ke, ve = with_prev(to_res(k)), with_prev(to_res(v))
    s = jnp.einsum('bnqhd,bnkhd->bnhqk', qb, ke).astype(jnp.float32) * (Dh ** -0.5)
    qi = jnp.arange(band)[:, None]
    kj = jnp.arange(2 * band)[None, :]
    delta = band + qi - kj
    key_m = (jnp.arange(nb)[:, None, None] - 1) * band + kj[None]
    valid = ((delta >= 0) & (delta <= band))[None] & (key_m >= 0)
    bias = -slopes[:, None, None] * (delta * dil).astype(jnp.float32)[None]
    s = jnp.where(valid[None, :, None], s + bias[None, None], -jnp.inf)
    lse = jax.nn.logsumexp(s, axis=-1)
    p = jnp.exp(s - lse[..., None])
    o = jnp.einsum('bnhqk,bnkhd->bnqhd', p.astype(v.dtype), ve).astype(jnp.float32)

    def from_res(t):
        t = t.reshape((B, dil, Lp) + t.shape[3:])[:, :, :L]
        t = jnp.moveaxis(t, 1, 2)
        return t.reshape((B, S) + t.shape[3:])

    return from_res(o), from_res(lse.transpose(0, 1, 3, 2))

def dilated_sample(q, kk, vv, wb, window, dil, slopes):
    T, Dh = q.shape[1], q.shape[3]
    n_keys = window // dil + 1
    kidx = jnp.arange(n_keys)
    idx = wb + jnp.arange(T)[:, None] - kidx[None, :] * dil
    valid = idx >= 0
    idx_c = jnp.clip(idx, 0)
    kg = jnp.take(kk, idx_c, axis=1)
    vg = jnp.take(vv, idx_c, axis=1)
    s = jnp.einsum('bthd,btkhd->bthk', q, kg).astype(jnp.float32) * (Dh ** -0.5)
    bias = -slopes[:, None] * (kidx * dil).astype(jnp.float32)[None]
    s = jnp.where(valid[None, :, None, :], s + bias[None, None], -jnp.inf)
    lse = jax.nn.logsumexp(s, axis=-1)
    p = jnp.exp(s - lse[..., None])
    o = jnp.einsum('bthk,btkhd->bthd', p.astype(vv.dtype), vg).astype(jnp.float32)
    return o, lse

def combine_groups(outs, lses):
    w = jax.nn.softmax(jnp.stack(lses), axis=0)
    return jnp.einsum('gbth,gbthd->bthd', w, jnp.stack(outs))

def causal_conv(xp, w, b):
    T = xp.shape[1] - CONV_W + 1
    out = b.astype(xp.dtype)
    for j in range(CONV_W):
        out = out + xp[:, j:j + T] * w[j].astype(xp.dtype)
    return out

def mlstm_inputs(qk_conv, mv, mi, mf, b_ig, b_fg):
    qk = jax.nn.silu(qk_conv.astype(jnp.float32))
    q = heads(qk[..., :ML_WIDTH], N_ML_HEADS)
    k = heads(qk[..., ML_WIDTH:], N_ML_HEADS) * (HEAD_DIM ** -0.5)
    v = heads(mv.astype(jnp.float32), N_ML_HEADS)
    ig = mi.astype(jnp.float32) + b_ig.astype(jnp.float32)
    lf = jax.nn.log_sigmoid(mf.astype(jnp.float32) + b_fg.astype(jnp.float32))
    return q, k, v, ig, lf

def mlstm_chunk(carry, xs):
    C, n, m = carry
    q, k, v, ig, lf = xs
    L = q.shape[1]
    b = jnp.cumsum(lf, axis=1)
    causal = jnp.tril(jnp.ones((L, L), dtype=bool))
    log_d = b[:, :, None, :] - b[:, None, :, :] + ig[:, None, :, :]
    log_d = jnp.where(causal[None, :, :, None], log_d, -jnp.inf)
    log_inter = b + m[:, None, :]
    m_t = jnp.maximum(log_inter, jnp.max(log_d, axis=2))
    d_w = jnp.exp(log_d - m_t[:, :, None, :])
    inter_w = jnp.exp(log_inter - m_t)
    a = jnp.einsum('bthd,bshd->btsh', q, k) * d_w
    num = jnp.einsum('btsh,bshd->bthd', a, v) + inter_w[..., None] * jnp.einsum('bthk,bhkv->bthv', q, C)
    den = jnp.sum(a, axis=2) + inter_w * jnp.einsum('bthk,bhk->bth', q, n)
    h = num / jnp.maximum(jnp.abs(den), jnp.exp(-m_t))[..., None]
    m_new = m_t[:, -1]
    w_s = jnp.exp(b[:, -1:, :] - b + ig - m_new[:, None, :])
    decay = jnp.exp(b[:, -1] + m - m_new)
    C_new = decay[..., None, None] * C + jnp.einsum('bsh,bshk,bshv->bhkv', w_s, k, v)
    n_new = decay[..., None] * n + jnp.einsum('bsh,bshk->bhk', w_s, k)
    return (C_new, n_new, m_new), h

def merge_mixers(att, ml_h, mo, p, dtype):
    B, T = att.shape[:2]
    att = att.reshape(B, T, ATT_WIDTH).astype(dtype)
    ml = (jax.nn.sigmoid(mo.astype(jnp.float32) + p['b_og'].astype(jnp.float32)) * ml_h).astype(dtype)
    cat = jnp.concatenate([rmsnorm(att, p['g_attn_out']), rmsnorm(ml, p['g_mlstm_out'])], axis=-1)
    return cat @ p['w_out']

def cross_attn(hn, mem_k, mem_v, w_cq, w_co):
    B, T, _ = hn.shape
    q = heads(hn @ w_cq, N_X_HEADS)
    s = jnp.einsum('bthd,bmhd->bhtm', q, mem_k.astype(q.dtype)).astype(jnp.float32) * (X_HEAD_DIM ** -0.5)
    pr = jax.nn.softmax(s, axis=-1).astype(hn.dtype)
    o = jnp.einsum('bhtm,bmhd->bthd', pr, mem_v.astype(hn.dtype)).reshape(B, T, N_X_HEADS * X_HEAD_DIM)
    return o @ w_co

def tail(h1, mem_k, mem_v, p):
    h2 = h1 + cross_attn(rmsnorm(h1, p['g_cross']), mem_k, mem_v, p['w_cq'], p['w_co'])
    hn = rmsnorm(h2, p['g_ffn'])
    return h2 + (jax.nn.silu(hn @ p['w_gate']) * (hn @ p['w_up'])) @ p['w_down']

def prompt_layer(x, mem, p):
    B, S, _ = x.shape
    z = rmsnorm(x, p['g_mix']) @ p['w_in']
    aq, ak, av, qk_pre, mv, mo, mi, mf = split_proj(z)
    aq, ak, av = heads(aq, N_ATT_HEADS), heads(ak, N_ATT_HEADS), heads(av, N_ATT_HEADS)
    slopes = alibi_slopes(N_ATT_HEADS)
    outs, lses = [], []
    for window, dil in DIL_GROUPS:
        o, l = dilated_prompt(aq, ak, av, window, dil, slopes)
        outs.append(o)
        lses.append(l)
    att = combine_groups(outs, lses)
    xp = jnp.pad(qk_pre, ((0, 0), (CONV_W - 1, 0), (0, 0)))
    q, k, v, ig, lf = mlstm_inputs(causal_conv(xp, p['conv_w'], p['conv_b']), mv, mi, mf, p['b_ig'], p['b_fg'])
    nc = S // ML_CHUNK

    def to_chunks(t):
        return jnp.moveaxis(t.reshape((B, nc, ML_CHUNK) + t.shape[2:]), 1, 0)

    init = (jnp.zeros((B, N_ML_HEADS, HEAD_DIM, HEAD_DIM), jnp.float32),
            jnp.zeros((B, N_ML_HEADS, HEAD_DIM), jnp.float32),
            jnp.full((B, N_ML_HEADS), NEG_INIT, jnp.float32))
    (C, n, m), hs = lax.scan(mlstm_chunk, init, (to_chunks(q), to_chunks(k), to_chunks(v), to_chunks(ig), to_chunks(lf)))
    ml_h = jnp.moveaxis(hs, 0, 1).reshape(B, S, ML_WIDTH)
    h1 = x + merge_mixers(att, ml_h, mo, p, x.dtype)
    mem_n = rmsnorm(mem, p['g_mem'])
    mem_k = heads(mem_n @ p['w_ck'], N_X_HEADS)
    mem_v = heads(mem_n @ p['w_cv'], N_X_HEADS)
    h = tail(h1, mem_k, mem_v, p)
    keep = min(W_MAX, S)
    return h, (ak[:, S - keep:], av[:, S - keep:], xp[:, -(CONV_W - 1):], C, n, m, mem_k, mem_v)

def sample_layer(x, win_k, win_v, mem_k, mem_v, conv_buf, C0, n0, m0, p):
    B, T, _ = x.shape
    z = rmsnorm(x, p['g_mix']) @ p['w_in']
    aq, ak, av, qk_pre, mv, mo, mi, mf = split_proj(z)
    aq, ak, av = heads(aq, N_ATT_HEADS), heads(ak, N_ATT_HEADS), heads(av, N_ATT_HEADS)
    wb = win_k.shape[1]
    kk = jnp.concatenate([win_k.astype(ak.dtype), ak], axis=1)
    vv = jnp.concatenate([win_v.astype(av.dtype), av], axis=1)
    slopes = alibi_slopes(N_ATT_HEADS)
    outs, lses = [], []
    for window, dil in DIL_GROUPS:
        o, l = dilated_sample(aq, kk, vv, wb, window, dil, slopes)
        outs.append(o)
        lses.append(l)
    att = combine_groups(outs, lses)
    xp = jnp.concatenate([conv_buf.astype(qk_pre.dtype), qk_pre], axis=1)
    q, k, v, ig, lf = mlstm_inputs(causal_conv(xp, p['conv_w'], p['conv_b']), mv, mi, mf, p['b_ig'], p['b_fg'])
    carry = (C0.astype(jnp.float32), n0.astype(jnp.float32), m0.astype(jnp.float32))
    (C, n, m), hch = mlstm_chunk(carry, (q, k, v, ig, lf))
    ml_h = hch.reshape(B, T, ML_WIDTH)
    h1 = x + merge_mixers(att, ml_h, mo, p, x.dtype)
    h = tail(h1, mem_k, mem_v, p)
    keep = min(W_MAX, kk.shape[1])
    return h, (kk[:, kk.shape[1] - keep:], vv[:, vv.shape[1] - keep:], xp[:, -(CONV_W - 1):], C, n, m)

def setup_inputs(seed: int = 0) -> dict:
    key = jax.random.key(seed)
    ks = jax.random.split(key, 40)
    f = jnp.float32

    def nrm(k, shape, scale):
        return jax.random.normal(k, shape, f) * scale

    def gain(k, n):
        return 1.0 + 0.02 * jax.random.normal(k, (n,), f)

    win_len = min(W_MAX, PAST_LEN)
    return {
        'x_prompt': nrm(ks[0], (BATCH, SEQ, D_MODEL), 1.0),
        'x_sample': nrm(ks[1], (DEC_BATCH, DEC_SEQ, D_MODEL), 1.0),
        'mem_prompt': nrm(ks[2], (BATCH, N_MEM, D_MODEL), 1.0),
        'cache_win_k': nrm(ks[3], (DEC_BATCH, win_len, N_ATT_HEADS, HEAD_DIM), 1.0),
        'cache_win_v': nrm(ks[4], (DEC_BATCH, win_len, N_ATT_HEADS, HEAD_DIM), 1.0),
        'cache_mem_k': nrm(ks[5], (DEC_BATCH, N_MEM, N_X_HEADS, X_HEAD_DIM), 1.0),
        'cache_mem_v': nrm(ks[6], (DEC_BATCH, N_MEM, N_X_HEADS, X_HEAD_DIM), 1.0),
        'state_conv': nrm(ks[7], (DEC_BATCH, CONV_W - 1, 2 * ML_WIDTH), 1.0),
        'state_mlstm_C': nrm(ks[8], (DEC_BATCH, N_ML_HEADS, HEAD_DIM, HEAD_DIM), 0.1),
        'state_mlstm_n': nrm(ks[9], (DEC_BATCH, N_ML_HEADS, HEAD_DIM), 0.1),
        'state_mlstm_m': nrm(ks[10], (DEC_BATCH, N_ML_HEADS), 1.0),
        'g_mix': gain(ks[11], D_MODEL),
        'w_in': nrm(ks[12], (D_MODEL, N_IN), D_MODEL ** -0.5),
        'conv_w': nrm(ks[13], (CONV_W, 2 * ML_WIDTH), CONV_W ** -0.5),
        'conv_b': nrm(ks[14], (2 * ML_WIDTH,), 0.02),
        'b_ig': nrm(ks[15], (N_ML_HEADS,), 0.1),
        'b_fg': jnp.linspace(3.0, 6.0, N_ML_HEADS, dtype=f) + nrm(ks[16], (N_ML_HEADS,), 0.01),
        'b_og': nrm(ks[17], (ML_WIDTH,), 0.02),
        'g_attn_out': gain(ks[18], ATT_WIDTH),
        'g_mlstm_out': gain(ks[19], ML_WIDTH),
        'w_out': nrm(ks[20], (ATT_WIDTH + ML_WIDTH, D_MODEL), (ATT_WIDTH + ML_WIDTH) ** -0.5),
        'g_cross': gain(ks[21], D_MODEL),
        'g_mem': gain(ks[22], D_MODEL),
        'w_cq': nrm(ks[23], (D_MODEL, N_X_HEADS * X_HEAD_DIM), D_MODEL ** -0.5),
        'w_ck': nrm(ks[24], (D_MODEL, N_X_HEADS * X_HEAD_DIM), D_MODEL ** -0.5),
        'w_cv': nrm(ks[25], (D_MODEL, N_X_HEADS * X_HEAD_DIM), D_MODEL ** -0.5),
        'w_co': nrm(ks[26], (N_X_HEADS * X_HEAD_DIM, D_MODEL), (N_X_HEADS * X_HEAD_DIM) ** -0.5),
        'g_ffn': gain(ks[27], D_MODEL),
        'w_gate': nrm(ks[28], (D_MODEL, D_FF), D_MODEL ** -0.5),
        'w_up': nrm(ks[29], (D_MODEL, D_FF), D_MODEL ** -0.5),
        'w_down': nrm(ks[30], (D_FF, D_MODEL), D_FF ** -0.5),
        'g_final': gain(ks[31], D_MODEL),
    }

def reference(x_prompt, x_sample, mem_prompt, cache_win_k, cache_win_v, cache_mem_k, cache_mem_v,
              state_conv, state_mlstm_C, state_mlstm_n, state_mlstm_m,
              g_mix, w_in, conv_w, conv_b, b_ig, b_fg, b_og, g_attn_out, g_mlstm_out, w_out,
              g_cross, g_mem, w_cq, w_ck, w_cv, w_co, g_ffn, w_gate, w_up, w_down, g_final):
    p = dict(g_mix=g_mix, w_in=w_in, conv_w=conv_w, conv_b=conv_b, b_ig=b_ig, b_fg=b_fg, b_og=b_og,
             g_attn_out=g_attn_out, g_mlstm_out=g_mlstm_out, w_out=w_out, g_cross=g_cross, g_mem=g_mem,
             w_cq=w_cq, w_ck=w_ck, w_cv=w_cv, w_co=w_co, g_ffn=g_ffn, w_gate=w_gate, w_up=w_up, w_down=w_down)
    h_p, h_s = x_prompt, x_sample
    for _ in range(DEPTH):
        h_p, st_p = prompt_layer(h_p, mem_prompt, p)
        h_s, st_s = sample_layer(h_s, cache_win_k, cache_win_v, cache_mem_k, cache_mem_v,
                                 state_conv, state_mlstm_C, state_mlstm_n, state_mlstm_m, p)
    y_prompt = rmsnorm(h_p, g_final)
    y_sample = rmsnorm(h_s, g_final)
    win_k_p, win_v_p, conv_p, C_p, n_p, m_p, mem_k_p, mem_v_p = st_p
    win_k_s, win_v_s, conv_s, C_s, n_s, m_s = st_s
    return (y_prompt, y_sample, win_k_p, win_v_p, conv_p, C_p, n_p, m_p, mem_k_p, mem_v_p,
            win_k_s, win_v_s, conv_s, C_s, n_s, m_s)


_drawn_inputs = setup_inputs


def setup_inputs(seed=0):
    import zlib

    import numpy as np

    out = dict(_drawn_inputs(seed))
    spreads = {}
    factors = {'b_og': 8.0,
     'g_attn_out': 5.672,
     'g_mlstm_out': 5.506,
     'g_cross': 8.0,
     'g_mem': 2.829,
     'g_ffn': 5.596,
     'g_final': 2.899}
    for name, (base, spread) in spreads.items():
        noise = np.random.default_rng([zlib.crc32(name.encode()), seed]).standard_normal(out[name].shape)
        drawn = base * np.exp(spread * noise) if base else spread * noise
        out[name] = __import__('jax').numpy.asarray(drawn.astype(out[name].dtype))
    for name, factor in factors.items():
        out[name] = (out[name] * factor).astype(out[name].dtype)
    return out
```

```python
from contextlib import ExitStack

import numpy as np

import concourse.bass as bass
from concourse import mybir

F32 = mybir.dt.float32
ALU = mybir.AluOpType
ACT = mybir.ActivationFunctionType
AX_X = mybir.AxisListType.X

P = 128
D = 1024
KB = D // P
SEQ = 1024
DB, DT = 8, 8
NS = DB * DT
N = SEQ + NS
TT = 9
PAST = 1024
H, HD = 8, 64
NP = H // 2
AW = H * HD
NMEM, XH, XD = 256, 4, 256
FB = 22
D_FF = FB * P
EPS = 1e-6
NEG = -1e30
CHUNKS = ((0, 384), (384, 384), (768, 320))
NC = SEQ // P
G_MIX, G_CROSS, G_MEM, G_FFN, G_FINAL = 0, 8, 16, 24, 32
G_ATT, G_ML, CONV_W, CONV_B, B_OG, N_PAR = 40, 44, 48, 80, 88, 92


def constants():
    slopes = np.exp2(-8.0 * (np.arange(H) + 1.0) / H)

    def bias(delta):
        count = ((delta <= 128).astype(int) + ((delta <= 512) & (delta % 4 == 0))
                 + ((delta <= 2048) & (delta % 16 == 0))) * (delta >= 0)
        log_count = np.where(count > 0, np.log(np.maximum(count, 1)), 0.0)
        return [np.where(count > 0, -s * delta + log_count, NEG) for s in slopes]

    delta = np.arange(P)[:, None] + (SEQ - P) - np.arange(SEQ)[None]
    prompt_bias = np.stack(bias(delta))
    t = np.arange(DT)
    cache = np.stack(bias(PAST + t[:, None] - np.arange(PAST)[None])).reshape(AW // DT, PAST)
    new = np.stack(bias(t[:, None] - t[None])).reshape(H * DT, DT)
    sample_new = np.full((2, H * DT, DB // 2, DB, DT), NEG)
    for pair in range(DB // 2):
        for e in range(2):
            sample_new[e, :, pair, 2 * pair + e] = new
    s = np.arange(P)
    causal = np.where(s[:, None] <= s[None], 0.0, NEG)
    r = np.arange(NS)
    sample_causal = np.where((r[:, None] <= r[None]) & (r[:, None] // DT == r[None] // DT), 0.0, NEG)
    restart = np.ones((H, N))
    restart[:, 0:SEQ:P] = 0
    restart[:, SEQ::DT] = 0
    head = np.arange(H)
    c = {
        "ident": np.eye(P),
        "prompt_bias": prompt_bias,
        "sample_bias": np.concatenate([cache, cache]),
        "sample_new_bias": sample_new.reshape(P, DB // 2 * NS),
        "causal": causal,
        "sample_causal": sample_causal,
        "restart": restart,
        "head_sel": np.repeat(np.eye(H), P, axis=1),
        "pair_sel": (head[:, None] == (2 * np.arange(NP)[:, None] + np.arange(P)[None] // HD).reshape(1, -1)),
        "batch_sel": r[:, None] // DT == np.arange(DB)[None],
    }
    return {k: np.ascontiguousarray(v, dtype=np.float32) for k, v in c.items()}


def build(nc, A, O):
    with ExitStack() as ctx:
        def sb(name, *shape):
            return ctx.enter_context(nc.sbuf_tensor(name, list(shape), F32))

        def sem(name):
            return ctx.enter_context(nc.semaphore(name))

        PS = ctx.enter_context(nc.psum_tensor("psum", [P, 8, 512], F32))
        XT = sb("residual_T", P, KB, N)
        XN = sb("normed_T", P, KB * N)
        HB = sb("wide", P, FB * N)
        WRT = sb("weights", P, 4224)
        SC = sb("scratch", P, 4352)
        IDENT = sb("ident", P, P)
        ONES = sb("ones", P, P)
        PAR = sb("params_T", P, N_PAR)
        EPSC = sb("eps", P, 1)
        QX = sb("sample_q_wide", P, NP, DB, NS)
        KNEW = sb("sample_k_new", P, NP, NS)
        VNEW = sb("sample_v_new", NS, AW)
        SMALL = sb("small", P, 96)

        def cut(t, start, *shape):
            n = int(np.prod(shape))
            v = t[:, start:start + n]
            if len(shape) == 2:
                return v.rearrange("p (a b) -> p a b", b=shape[1])
            if len(shape) == 3:
                return v.rearrange("p (a b c) -> p a b c", b=shape[1], c=shape[2])
            return v

        xn = cut(XN, 0, KB, N)
        cat = cut(HB, 0, KB, N)
        BIG = KB * N
        hid = cut(HB, 0, FB, N)
        ring = cut(WRT, 0, 4, KB, P)
        nsq = cut(SC, 0, 2, N)
        nacc = cut(SC, 2 * N, N)
        nr = cut(SC, 3 * N, N)
        silu_g = cut(SC, 0, 2, N)

        phase_done = sem("phase_done")
        act_step, dve_step, pool_step = sem("act_step"), sem("dve_step"), sem("pool_step")
        w_landed = [sem(f"w_landed{i}") for i in range(4)]
        z_ready, z_taken = sem("z_ready"), sem("z_taken")
        sq_ready, sq_summed, sum_ready, bcast_ready, rnorm_ready, norm_done = (
            sem("sq_ready"), sem("sq_summed"), sem("sum_ready"), sem("bcast_ready"), sem("rnorm_ready"),
            sem("norm_done"))
        x_landed, par_landed, x_turned, x_taken = sem("x_landed"), sem("par_landed"), sem("x_turned"), sem("x_taken")
        out_stored = sem("out_stored")
        stores = [0]

        def stored(ins):
            ins.then_inc(out_stored, 16)
            stores[0] += 1

        class Chain:

            def __init__(self, eng, s):
                self.eng, self.sem, self.n, self.phase = eng, s, 0, 0

            def __call__(self, ins):
                self.n += 1
                ins.then_inc(self.sem, 1)
                self.eng.wait_ge(self.sem, self.n)

            def meet(self):
                self.phase += 1
                self.eng.drain().then_inc(phase_done, 1)
                self.eng.wait_ge(phase_done, 4 * self.phase)

        def w_view(w, c0=0):
            return w.rearrange("(k p) n -> p k n", p=P)[:, :, c0:]

        def proj_load(sp, views, blocks, n0):
            m = len(views)

            def block(i, s):
                v = views[s % m]
                sp.dma_start(ring[:, s], v[:, :, bass.ds((i * (4 // m) + s // m) * P, P)]).then_inc(w_landed[s], 16)
            if n0 == 0:
                for s in range(4):
                    block(0, s)
                return
            with sp.Fori(0, blocks // 4) as i:
                for s in range(4):
                    sp.wait_ge(z_ready, i * 4 + (n0 + s - 3))
                    block(i, s)

        def proj_tensor(pe, x, blocks, n0, chunks=CHUNKS):
            def block(i, s):
                pe.wait_ge(w_landed[s], i * 16 + (16 * (n0 // 4) + 16))
                for c, (t0, w) in enumerate(chunks):
                    for k in range(KB):
                        mm = nc.tensor.matmul(PS[:, 3 * (s % 2) + c, 0:w], ring[:, s, k], x[:, k, t0:t0 + w],
                                              start=(k == 0), stop=(k == KB - 1))
                mm.then_inc(z_ready, 1)
            if n0 == 0:
                for s in range(4):
                    if s >= 2:
                        pe.wait_ge(z_taken, s - 1)
                    block(0, s)
                return
            with pe.Fori(0, blocks // 4) as i:
                for s in range(4):
                    pe.wait_ge(z_taken, i * 4 + (n0 + s - 1))
                    block(i, s)

        def proj_evac(eng, dst, blocks, n0, put, chunks=CHUNKS):
            with eng.Fori(0, blocks // 4) as i:
                for s in range(4):
                    eng.wait_ge(z_ready, i * 4 + (n0 + s + 1))
                    for c, (t0, w) in enumerate(chunks):
                        last = put(dst[:, bass.ds(i * 4 + s, 1), t0:t0 + w], PS[:, 3 * (s % 2) + c:3 * (s % 2) + c + 1, 0:w])
                    last.then_inc(z_taken, 1)

        def act_copy(scale=1.0):
            return lambda out, ps: nc.scalar.activation(out, ps, ACT.Copy, scale=scale)

        def add_residual(out, ps):
            return nc.vector.tensor_tensor(out, ps, out, ALU.add)

        def norm_scalar(act, src, nb, cols, j0, r0):
            for k in range(nb):
                if j0 + k >= 2:
                    act.wait_ge(sq_summed, j0 + k - 1)
                nc.scalar.activation(nsq[:, (j0 + k) % 2, 0:cols], src[:, k, 0:cols], ACT.Square).then_inc(sq_ready, 1)
            act.wait_ge(bcast_ready, r0 + 1)
            if r0:
                act.wait_ge(norm_done, r0)
            chain = chains["act"]
            for c, (t0, w) in enumerate(CHUNKS):
                w = min(w, cols - t0)
                if w > 0:
                    last = nc.scalar.activation(nr[:, t0:t0 + w], PS[:, c, 0:w], ACT.Ln, bias=EPSC[:, 0:1],
                                                scale=1.0 / (nb * P))
            chain(last)
            nc.scalar.activation(nr[:, 0:cols], nr[:, 0:cols], ACT.Exp, scale=-0.5).then_inc(rnorm_ready, 1)

        def norm_vector(dve, src, dst, nb, cols, gain, j0, r0):
            for k in range(nb):
                dve.wait_ge(sq_ready, j0 + k + 1)
                if k:
                    dve.wait_ge(sq_summed, j0 + k)
                    nc.vector.tensor_tensor(nacc[:, 0:cols], nacc[:, 0:cols], nsq[:, (j0 + k) % 2, 0:cols],
                                            ALU.add).then_inc(sq_summed, 1)
                else:
                    nc.vector.tensor_copy(nacc[:, 0:cols], nsq[:, (j0 + k) % 2, 0:cols]).then_inc(sq_summed, 1)
            dve.wait_ge(rnorm_ready, r0 + 1)
            for k in range(nb):
                last = nc.vector.scalar_tensor_tensor(out=dst[:, k, 0:cols], in0=src[:, k, 0:cols],
                                                      scalar=PAR[:, gain + k:gain + k + 1], in1=nr[:, 0:cols],
                                                      op0=ALU.mult, op1=ALU.mult)
            last.then_inc(norm_done, 1)

        def norm_tensor(pe, nb, cols, j0, r0):
            pe.wait_ge(sq_summed, j0 + nb)
            if r0:
                pe.wait_ge(rnorm_ready, r0)
            for c, (t0, w) in enumerate(CHUNKS):
                w = min(w, cols - t0)
                if w > 0:
                    mm = nc.tensor.matmul(PS[:, c, 0:w], ONES[:, :], nacc[:, t0:t0 + w], start=True, stop=True)
            mm.then_inc(bcast_ready, 1)

        xs = cut(HB, BIG, TT, D)
        par_rows = cut(SC, 0, P)

        def load_inputs(sp):
            row = lambda a: a.rearrange("(k p) -> k p", p=P)
            for a, r, n in (("g_mix", G_MIX, 8), ("g_cross", G_CROSS, 8), ("g_mem", G_MEM, 8), ("g_ffn", G_FFN, 8),
                            ("g_final", G_FINAL, 8), ("g_attn_out", G_ATT, 4), ("g_mlstm_out", G_ML, 4),
                            ("conv_b", CONV_B, 8), ("b_og", B_OG, 4)):
                sp.dma_start(par_rows[r:r + n, :], row(A[a])).then_inc(par_landed, 16)
            sp.dma_start(par_rows[CONV_W:CONV_W + 32, :], A["conv_w"].rearrange("j (k p) -> (j k) p", p=P)).then_inc(par_landed, 16)
            sp.dma_start(IDENT[:, :], A["ident"]).then_inc(par_landed, 16)
            xp = A["x_prompt"][0].rearrange("(t p) d -> p t d", p=P)
            for t in range(TT - 1):
                sp.dma_start(xs[:, t, :], xp[:, t, :]).then_inc(x_landed, 16)
            sp.dma_start(xs[0:NS, TT - 1, :], A["x_sample"].rearrange("b t d -> (b t) d")).then_inc(x_landed, 16)

        def turn_tensor(pe):
            pe.wait_ge(par_landed, 16 * 11)
            nc.tensor.transpose(PS[:, 4, 0:N_PAR], par_rows[0:N_PAR, :], IDENT[0:N_PAR, 0:N_PAR]).then_inc(x_turned, 1)
            pe.wait_ge(x_landed, 16 * TT)
            for g in range(2 * TT):
                t, half = g // 2, g % 2
                n = P if t < TT - 1 else NS
                if g >= 4:
                    pe.wait_ge(x_taken, g - 2)
                for j in range(4):
                    mm = nc.tensor.transpose(PS[:, g % 4, j * P:j * P + n], xs[0:n, t, (4 * half + j) * P:(4 * half + j + 1) * P],
                                             IDENT[0:n, 0:n])
                mm.then_inc(x_turned, 1)

        def turn_vector(dve):
            chains["dve"](nc.vector.memset(EPSC[:, :], EPS))
            nc.vector.memset(ONES[:, :], 1.0)
            dve.wait_ge(x_turned, 1)
            nc.vector.tensor_copy(PAR[:, :], PS[:, 4, 0:N_PAR]).then_inc(x_taken, 1)
            for g in range(2 * TT):
                t, half = g // 2, g % 2
                n = P if t < TT - 1 else NS
                dve.wait_ge(x_turned, g + 2)
                nc.vector.tensor_copy(XT[:, 4 * half:4 * half + 4, t * P:t * P + n],
                                      PS[:, g % 4, :].rearrange("p (j n) -> p j n", j=4)[:, :, 0:n]).then_inc(x_taken, 1)

        aq, ak, av = (cut(HB, BIG + j * NP * N, NP, N) for j in range(3))
        akv = cut(HB, BIG + NP * N, 2 * NP, N)
        vtok = cut(HB, NP * N, TT - 1, AW)
        AW0 = BIG + 2 * NP * N
        att_tok = cut(HB, AW0, NC, AW)
        bias_tab = cut(HB, AW0 + NC * AW, 2, SEQ)
        logit = cut(SC, 0, 3, SEQ)
        prob_T = cut(SC, 3 * SEQ, SEQ), cut(WRT, 2048, SEQ)
        k_stage = cut(WRT, 0, 4, AW)
        kv_turned, kv_taken, q_wide = sem("kv_turned"), sem("kv_taken"), sem("q_wide")
        k_stored = [sem(f"k_stored{i}") for i in range(4)]

        def kv_turn_tensor(pe):
            for g in range(2 * TT):
                t, which = g // 2, g % 2
                n = P if t < TT - 1 else NS
                if g >= 4:
                    pe.wait_ge(kv_taken, g - 3)
                for j in range(NP):
                    mm = nc.tensor.transpose(PS[0:n, g % 4, j * P:(j + 1) * P], akv[:, NP * which + j, t * P:t * P + n], IDENT[:, :])
                mm.then_inc(kv_turned, 1)

        def kv_turn_scalar(act):
            for g in range(2 * TT):
                t, which = g // 2, g % 2
                n = P if t < TT - 1 else NS
                act.wait_ge(kv_turned, g + 1)
                if which == 0:
                    if t >= 4:
                        act.wait_ge(k_stored[t % 4], 16 * (t // 4))
                    out = k_stage[0:n, t % 4, :]
                else:
                    out = vtok[:, t, :] if t < TT - 1 else VNEW[:, :]
                nc.scalar.activation(out, PS[0:n, g % 4, :], ACT.Copy).then_inc(kv_taken, 1)

        def kv_store(sp):
            wk, wv = (O[n][0].rearrange("(t p) h d -> p t (h d)", p=P) for n in ("win_k_p", "win_v_p"))
            for t in range(TT):
                sp.wait_ge(kv_taken, 2 * t + 1)
                if t < TT - 1:
                    sp.dma_start(wk[:, t, :], k_stage[:, t % 4, :]).then_inc(k_stored[t % 4], 16)
                    sp.wait_ge(kv_taken, 2 * t + 2)
                    stored(sp.dma_start(wv[:, t, :], vtok[:, t, :]))
                else:
                    sp.wait_ge(kv_taken, 2 * t + 2)
                    for b in range(DB):
                        rows = slice(b * DT, (b + 1) * DT)
                        sp.dma_start(O["win_k_s"][b, PAST:PAST + DT].rearrange("t h d -> t (h d)"),
                                     k_stage[rows, t % 4, :]).then_inc(k_stored[t % 4], 16)
                        stored(sp.dma_start(O["win_v_s"][b, PAST:PAST + DT].rearrange("t h d -> t (h d)"), VNEW[rows, :]))
            for i in range(4):
                sp.wait_ge(k_stored[i], 16 * (len(range(i, TT - 1, 4)) + (DB if i == (TT - 1) % 4 else 0)))

        def q_wide_pool(pool):
            chains["pool"](nc.gpsimd.memset(QX[:, :, :, :], 0.0))
            for e in range(2):
                rows = slice(HD * e, HD * e + HD)
                for p in range(NP):
                    h = 2 * p + e
                    chains["pool"](nc.gpsimd.tensor_copy(QX[rows, p, :, h * DT:(h + 1) * DT],
                                                         aq[rows, p, SEQ:N].rearrange("p (b t) -> p b t", t=DT)))
            nc.gpsimd.tensor_copy(KNEW[:, :, :], ak[:, :, SEQ:N])

        tab_landed = [sem(f"tab_landed{i}") for i in range(2)]
        s_ready, logit_ready, prob_ready, pt_ready, pt_taken, o_ready, o_taken = (
            sem("s_ready"), sem("logit_ready"), sem("prob_ready"), sem("pt_ready"),
            sem("pt_taken"), sem("o_ready"), sem("o_taken"))
        UNITS = [(h, qb) for h in range(H) for qb in range(NC)]
        GROUPS = [(u, g) for u, (h, qb) in enumerate(UNITS) for g in range((qb + 4) // 4)]
        after = {u: sum(1 for v, _ in GROUPS if v <= u) for u in range(len(UNITS))}

        def att_load(sp):
            for h in range(H):
                if h >= 2:
                    sp.wait_ge(logit_ready, (h - 1) * NC)
                sp.dma_start(bias_tab[:, h % 2, :], A["prompt_bias"][h]).then_inc(tab_landed[h % 2], 16)

        def att_tensor(pe):
            def scores(u):
                h, qb = UNITS[u]
                rows = slice(HD * (h % 2), HD * (h % 2) + HD)
                if u >= 2:
                    pe.wait_ge(logit_ready, u - 1)
                for g in range((qb + 4) // 4):
                    w = min(4, qb + 1 - 4 * g) * P
                    mm = nc.tensor.matmul(PS[:, 2 * (u % 2) + g, 0:w], aq[rows, h // 2, qb * P:(qb + 1) * P],
                                          ak[rows, h // 2, 512 * g:512 * g + w], start=True, stop=True)
                mm.then_inc(s_ready, 1)

            def turn(u):
                h, qb = UNITS[u]
                pe.wait_ge(prob_ready, u + 1)
                for g in range((qb + 4) // 4):
                    n = after[u - 1] + g if u else g
                    if n >= 2:
                        pe.wait_ge(pt_taken, n - 1)
                    for j in range(min(4, qb + 1 - 4 * g)):
                        mm = nc.tensor.transpose(PS[:, 4 + n % 2, j * P:(j + 1) * P],
                                                 logit[:, u % 3, (4 * g + j) * P:(4 * g + j + 1) * P], IDENT[:, :])
                    mm.then_inc(pt_ready, 1)

            def values(u):
                h, qb = UNITS[u]
                pe.wait_ge(pt_taken, after[u])
                if u >= 2:
                    pe.wait_ge(o_taken, u - 1)
                for j in range(qb + 1):
                    mm = nc.tensor.matmul(PS[:, 6 + u % 2, 0:HD], prob_T[u % 2][:, j * P:(j + 1) * P],
                                          vtok[:, j, h * HD:(h + 1) * HD], start=(j == 0), stop=(j == qb))
                mm.then_inc(o_ready, 1)

            for u in range(len(UNITS) + 2):
                if u < len(UNITS):
                    scores(u)
                if 1 <= u <= len(UNITS):
                    turn(u - 1)
                if u >= 2:
                    values(u - 2)

        amax, asum, arec, negm = (SMALL[:, 4 * i:4 * i + 4] for i in range(4))

        def att_vector(dve):
            def finish(u):
                h, qb = UNITS[u]
                i = u % 4
                dve.wait_ge(prob_ready, u + 1)
                chains["dve"](nc.vector.reciprocal(arec[:, i:i + 1], asum[:, i:i + 1]))
                dve.wait_ge(o_ready, u + 1)
                nc.vector.tensor_scalar(att_tok[:, qb, h * HD:(h + 1) * HD], PS[:, 6 + u % 2, 0:HD],
                                        arec[:, i:i + 1], None, ALU.mult).then_inc(o_taken, 1)
            for u, (h, qb) in enumerate(UNITS):
                w, i = (qb + 1) * P, u % 4
                dve.wait_ge(s_ready, u + 1)
                dve.wait_ge(tab_landed[h % 2], 16 * (h // 2 + 1))
                if u >= 3:
                    dve.wait_ge(pt_ready, after[u - 3])
                chains["dve"](nc.vector.tensor_tensor_reduce(
                    logit[:, u % 3, 0:w], PS[:, 2 * (u % 2):2 * (u % 2) + 2, :].rearrange("p a b -> p (a b)")[:, 0:w],
                    bias_tab[:, h % 2, SEQ - w:SEQ], 1.0, 3 * NEG, ALU.add, ALU.max, amax[:, i:i + 1]))
                nc.vector.tensor_scalar(negm[:, i:i + 1], amax[:, i:i + 1], -1.0, None, ALU.mult).then_inc(logit_ready, 1)
                if u >= 2:
                    finish(u - 2)
            finish(len(UNITS) - 2)
            finish(len(UNITS) - 1)

        def att_scalar(act):
            def take(u):
                h, qb = UNITS[u]
                for g in range((qb + 4) // 4):
                    n = after[u - 1] + g if u else g
                    w = min(4, qb + 1 - 4 * g) * P
                    act.wait_ge(pt_ready, n + 1)
                    if g == 0 and u >= 2:
                        act.wait_ge(o_ready, u - 1)
                    nc.scalar.activation(prob_T[u % 2][:, 512 * g:512 * g + w], PS[:, 4 + n % 2, 0:w], ACT.Copy).then_inc(pt_taken, 1)
            for u, (h, qb) in enumerate(UNITS):
                w, i = (qb + 1) * P, u % 4
                act.wait_ge(logit_ready, u + 1)
                if u >= 4:
                    act.wait_ge(o_taken, u - 3)
                nc.scalar.activation(logit[:, u % 3, 0:w], logit[:, u % 3, 0:w], ACT.Exp, bias=negm[:, i:i + 1],
                                     accum_out=asum[:, i:i + 1]).then_inc(prob_ready, 1)
                if u >= 1:
                    take(u - 1)
            take(len(UNITS) - 1)

        at_turned, at_taken = sem("at_turned"), sem("at_taken")

        def att_turn_tensor(pe):
            for t in range(NC):
                if t >= 4:
                    pe.wait_ge(at_taken, t - 3)
                for j in range(NP):
                    mm = nc.tensor.transpose(PS[:, t % 4, j * P:(j + 1) * P], att_tok[:, t, j * P:(j + 1) * P], IDENT[:, :])
                mm.then_inc(at_turned, 1)

        def att_turn_scalar(act):
            for t in range(NC):
                act.wait_ge(at_turned, t + 1)
                nc.scalar.activation(cat[:, 0:NP, t * P:(t + 1) * P], PS[:, t % 4, :].rearrange("p (j n) -> p j n", j=NP),
                                     ACT.Copy).then_inc(at_taken, 1)

        qk = cut(HB, BIG, 2 * NP, N)
        mv = cut(HB, BIG + 2 * NP * N, NP, N)
        sig_o = cat[:, NP:2 * NP, :]
        V1W = HD + 1
        v1 = cut(XN, 0, TT, H * V1W)
        ML0 = TT * H * V1W
        head_sel = cut(XN, ML0, H, P)
        pair_sel = cut(XN, ML0 + 1024, NP, P)
        causal = cut(XN, ML0 + 1536, P)
        sample_causal = cut(XN, ML0 + 1664, NS)
        restart = cut(XN, ML0 + 1728, N)
        batch_sel = cut(XN, ML0 + 2816, DB)
        cols = cut(XN, ML0 + 2824, TT, 4, H)
        colx = cut(XN, ML0 + 3112, TT, 3, H)
        dec = cut(XN, ML0 + 3328, NP, NC + DB)
        bgate = cut(XN, ML0 + 3392, 2)
        wgate = cut(XN, ML0 + 3400, 1)
        mrow = cut(XN, ML0 + 3404, NC + DB)
        dkrow = cut(XN, ML0 + 3420, NC + DB)
        m_out = cut(XN, ML0 + 3436, DB + 1)
        ktok = cut(HB, BIG + 2 * NP * N, TT, AW)
        gate_w = cut(SC, 0, KB, 40)
        g_raw = [cut(HB, BIG + (12 + j) * N, N) for j in range(2)]
        gb, gm, gw = (cut(SC, j * N, N) for j in range(3))
        gu = cut(HB, BIG + 2 * NP * N + TT * AW, N)
        rows4 = cut(WRT, 0, N)
        gi, gf = cut(WRT, N, N), cut(WRT, 2 * N, N)
        conv_acc = cut(SC, 0, 2, N)
        conv_x = cut(SC, 2 * N, KB, DB, 11)
        state_rows = cut(SC, 2 * N + 704, D)
        mrows_stage = cut(WRT, 0, D)

        gw_landed, gate_ready, ml_landed, gate_rows = sem("gw_landed"), sem("gate_ready"), sem("ml_landed"), sem("gate_rows")

        def ml_loads(sp):
            sp.wait_ge(phase_done, 4 * PH["att"])
            sp.wait_ge(gw_zeroed, 1)
            wv = A["w_in"].rearrange("(k p) n -> p k n", p=P)
            with nc.allow_non_contiguous_dma(reason="sixteen gate columns"):
                sp.dma_start(gate_w[:, :, 0:8], wv[:, :, 3584:3592]).then_inc(gw_landed, 16)
                sp.dma_start(gate_w[:, :, 32:40], wv[:, :, 3592:3600]).then_inc(gw_landed, 16)

        def ml_tables(sp):
            sp.wait_ge(phase_done, 4 * PH["ml_proj"])
            with nc.allow_non_contiguous_dma(reason="small tables and columns"):
                for dst, src in ((head_sel[0:H].rearrange("p a b -> p (a b)"), A["head_sel"]),
                                 (pair_sel[0:H].rearrange("p a b -> p (a b)"), A["pair_sel"]),
                                 (causal, A["causal"]), (sample_causal[0:NS], A["sample_causal"]),
                                 (restart[0:H], A["restart"]), (batch_sel[0:NS], A["batch_sel"]),
                                 (bgate[0:H, 0:1], A["b_ig"].rearrange("(a b) -> a b", b=1)),
                                 (bgate[0:H, 1:2], A["b_fg"].rearrange("(a b) -> a b", b=1)),
                                 (mrow[0:H, NC:NC + DB], A["state_mlstm_m"].rearrange("b h -> h b")),
                                 (state_rows[0:DB * 3], A["state_conv"].rearrange("b j c -> (b j) c"))):
                    sp.dma_start(dst, src).then_inc(ml_landed, 16)

        gw_zeroed = sem("gw_zeroed")

        def gates_tensor(pe):
            pe.wait_ge(gw_landed, 32)
            for c, (t0, w) in enumerate(CHUNKS):
                for k in range(KB):
                    mm = nc.tensor.matmul(PS[0:40, c, 0:w], gate_w[:, k, :], xn[:, k, t0:t0 + w],
                                          start=(k == 0), stop=(k == KB - 1))
            mm.then_inc(gate_ready, 1)

        def gates_vector(dve):
            dve.wait_ge(gate_ready, 1)
            for c, (t0, w) in enumerate(CHUNKS):
                nc.vector.tensor_copy(g_raw[0][0:H, t0:t0 + w], PS[0:H, c, 0:w])
                last = nc.vector.tensor_copy(g_raw[1][0:H, t0:t0 + w], PS[32:32 + H, c, 0:w])
            last.then_inc(gates_read, 1)

        gates_read = sem("gates_read")

        def gate_bias_vector(dve):
            dve.wait_ge(ml_landed, 160)
            for j, g in enumerate((gi, gf)):
                nc.vector.tensor_scalar(g[0:H], g_raw[j][0:H], bgate[0:H, j:j + 1], None, ALU.add)

        ct_turned, ct_taken = sem("ct_turned"), sem("ct_taken")

        def conv_state_tensor(pe):
            pe.wait_ge(ml_landed, 160)
            for g in range(TT + 3):
                if g >= 4:
                    pe.wait_ge(ct_taken, g - 3)
                n = P if g != TT - 1 else NS
                for j in range(NP):
                    if g < TT:
                        mm = nc.tensor.transpose(PS[0:n, g % 4, j * P:(j + 1) * P], mv[:, j, g * P:g * P + n], IDENT[:, :])
                    elif g < TT + 2:
                        mm = nc.tensor.transpose(PS[:, g % 4, j * P:(j + 1) * P], qk[:, 4 * (g - TT) + j, N - P:N], IDENT[:, :])
                    else:
                        for i in (j, j + 4):
                            mm = nc.tensor.transpose(PS[:, g % 4, i * 24:(i + 1) * 24], state_rows[0:24, i * P:(i + 1) * P],
                                                     IDENT[0:24, 0:24])
                mm.then_inc(ct_turned, 1)

        def conv_state_scalar(act):
            for k in range(NP):
                nc.scalar.activation(sig_o[:, k, :], sig_o[:, k, :], ACT.Sigmoid, bias=PAR[:, B_OG + k:B_OG + k + 1])
            for g in range(TT + 3):
                n = P if g != TT - 1 else NS
                act.wait_ge(ct_turned, g + 1)
                if g < TT:
                    last = nc.scalar.activation(v1[0:n, g, :].rearrange("p (h d) -> p h d", h=H)[:, :, 0:HD],
                                                PS[0:n, g % 4, :].rearrange("p (h d) -> p h d", h=H), ACT.Copy)
                elif g < TT + 2:
                    last = nc.scalar.activation(mrows_stage[:, 512 * (g - TT):512 * (g - TT) + 512], PS[:, g % 4, :], ACT.Copy)
                else:
                    last = nc.scalar.activation(conv_x[:, :, :, 0:3],
                                                PS[:, g % 4, 0:192].rearrange("p (k b j) -> p k b j", k=KB, b=DB), ACT.Copy)
                last.then_inc(ct_taken, 1)

        def conv_state_pool(pool):
            nc.gpsimd.memset(v1[:, :, :].rearrange("p t (h d) -> p (t h) d", h=H)[:, :, HD:V1W], 1.0)
            nc.gpsimd.tensor_copy(conv_x[:, :, :, 3:11], qk[:, :, SEQ:N].rearrange("p k (b t) -> p k b t", t=DT))

        def conv_store(sp):
            sp.wait_ge(ct_taken, TT + 2)
            first = P - NS - 3
            stored(sp.dma_start(O["conv_p"][0], mrows_stage[first:first + 3, :]))
            for b in range(DB):
                r = P - NS + b * DT + DT - 3
                stored(sp.dma_start(O["conv_s"][b], mrows_stage[r:r + 3, :]))
            mark["conv_rows"] = stores[0]

        mark = {}

        conv_ready, conv_used, scan_ready = sem("conv_ready"), sem("conv_used"), sem("scan_ready")

        def conv_vector(dve):
            chain = chains["dve"]
            for k in range(2 * NP):
                if k >= 2:
                    dve.wait_ge(conv_used, k - 1)
                acc = conv_acc[:, k % 2, :]
                w = [PAR[:, CONV_W + 8 * j + k:CONV_W + 8 * j + k + 1] for j in range(4)]
                sacc = acc[:, SEQ:N].rearrange("p (b t) -> p b t", t=DT)
                nc.vector.tensor_scalar(acc[:, 0:SEQ], qk[:, k, 0:SEQ], w[3], PAR[:, CONV_B + k:CONV_B + k + 1], ALU.mult, ALU.add)
                chain(nc.vector.tensor_scalar(sacc, conv_x[:, k, :, 3:11], w[3], PAR[:, CONV_B + k:CONV_B + k + 1], ALU.mult, ALU.add))
                for j in (2, 1, 0):
                    s = 3 - j
                    nc.vector.scalar_tensor_tensor(out=acc[:, s:SEQ], in0=qk[:, k, 0:SEQ - s], scalar=w[j], in1=acc[:, s:SEQ],
                                                   op0=ALU.mult, op1=ALU.add)
                    last = nc.vector.scalar_tensor_tensor(out=sacc, in0=conv_x[:, k, :, j:j + DT], scalar=w[j], in1=sacc,
                                                          op0=ALU.mult, op1=ALU.add)
                    if j:
                        chain(last)
                last.then_inc(conv_ready, 1)

        def conv_scalar(act):
            for k in range(2 * NP):
                act.wait_ge(conv_ready, k + 1)
                nc.scalar.activation(qk[:, k, :], conv_acc[:, k % 2, :], ACT.Silu).then_inc(conv_used, 1)

        kt_turned, kt_taken = sem("kt_turned"), sem("kt_taken")

        def k_turn_tensor(pe):
            for g in range(TT):
                if g >= 4:
                    pe.wait_ge(kt_taken, g - 3)
                n = P if g != TT - 1 else NS
                for j in range(NP):
                    mm = nc.tensor.transpose(PS[0:n, g % 4, j * P:(j + 1) * P], qk[:, NP + j, g * P:g * P + n], IDENT[:, :])
                mm.then_inc(kt_turned, 1)

        def k_turn_vector(dve):
            for g in range(TT):
                n = P if g != TT - 1 else NS
                dve.wait_ge(kt_turned, g + 1)
                nc.vector.tensor_copy(ktok[0:n, g, :], PS[0:n, g % 4, :]).then_inc(kt_taken, 1)

        gexp, rows_ready, cols_turned, dec_ready, cols_taken = (
            sem("gate_softplus"), sem("rows_ready"), sem("cols_turned"), sem("dec_ready"),
            sem("cols_taken"))

        def gate_scalar(act):
            chain = chains["act"]
            chain(nc.scalar.activation(gm[0:H], gf[0:H], ACT.Abs))
            chain(nc.scalar.activation(gm[0:H], gm[0:H], ACT.Exp, scale=-1.0))
            nc.scalar.activation(gm[0:H], gm[0:H], ACT.Ln, bias=1.0).then_inc(gexp, 1)
            act.wait_ge(cols_taken, TT)
            nc.scalar.activation(colx[:, :, 0, :], cols[:, :, 0, :], ACT.Exp)
            nc.scalar.activation(colx[:, :, 1, :], cols[:, :, 1, :], ACT.Exp, scale=-1.0)
            chain(nc.scalar.activation(colx[:, :, 2, :], cols[:, :, 3, :], ACT.Exp))
            nc.scalar.activation(colx[:, :, 2, :], colx[:, :, 2, :], ACT.Copy, scale=HD ** -0.5)
            act.wait_ge(dec_ready, 1)
            nc.scalar.activation(dec[:, :, :], PS[:, 5, 0:64].rearrange("p (a b) -> p a b", a=NP), ACT.Exp)

        def gate_vector(dve):
            chain = chains["dve"]
            dve.wait_ge(out_stored, 16 * mark["conv_rows"])
            nc.vector.memset(rows4[:, :], 0.0)
            nc.vector.memset(cols[:, :, :, :], 0.0)
            nc.vector.memset(cst[:, :, :], 0.0)
            chain(nc.vector.memset(mrow[0:H, 0:1], NEG))
            dve.wait_ge(gexp, 1)
            chain(nc.vector.scalar_tensor_tensor(out=gf[0:H], in0=gf[0:H], scalar=0.0, in1=gm[0:H],
                                                 op0=ALU.min, op1=ALU.subtract))
            nc.vector.tensor_tensor_scan(gb[0:H], restart[0:H], gf[0:H], 0.0, ALU.mult, ALU.add)
            nc.vector.tensor_tensor_scan(gm[0:H, 0:SEQ], gf[0:H, 0:SEQ], gi[0:H, 0:SEQ], NEG, ALU.add, ALU.max)
            for b in range(DB):
                t = slice(SEQ + b * DT, SEQ + (b + 1) * DT)
                last = nc.vector.tensor_tensor_scan(gm[0:H, t], gf[0:H, t], gi[0:H, t], mrow[0:H, NC + b:NC + b + 1],
                                                    ALU.add, ALU.max)
            chain(last)
            chunk3 = lambda r: r[:, 0:SEQ].rearrange("p (c t) -> p c t", t=P)
            batch3 = lambda r: r[:, SEQ:N].rearrange("p (c t) -> p c t", t=DT)
            nc.vector.tensor_copy(mrow[0:H, 1:NC], gm[0:H, P - 1:SEQ - P:P])
            nc.vector.tensor_copy(m_out[0:H, 1:1 + DB], gm[0:H, SEQ + DT - 1:N:DT])
            nc.vector.tensor_tensor(gu[0:H], gb[0:H], gm[0:H], ALU.subtract)
            nc.vector.tensor_copy(rows4[32:32 + H, :], gm[0:H])
            nc.vector.tensor_tensor(gw[0:H], gi[0:H], gb[0:H], ALU.subtract)
            chain(nc.vector.tensor_copy(m_out[0:H, 0:1], gm[0:H, SEQ - 1:SEQ]))
            g8, m8 = gu[0:H], mrow[0:H]
            nc.vector.tensor_tensor(chunk3(rows4[0:H]), chunk3(g8), m8[:, 0:NC].unsqueeze(2).to_broadcast([H, NC, P]), ALU.add)
            nc.vector.tensor_tensor(batch3(rows4[0:H]), batch3(g8), m8[:, NC:].unsqueeze(2).to_broadcast([H, DB, DT]), ALU.add)
            nc.vector.tensor_copy(rows4[64:64 + H, :], gw[0:H])
            nc.vector.tensor_tensor(chunk3(rows4[96:96 + H]), chunk3(gw[0:H]),
                                    chunk3(g8)[:, :, P - 1:P].to_broadcast([H, NC, P]), ALU.add)
            chain(nc.vector.tensor_tensor(batch3(rows4[96:96 + H]), batch3(gw[0:H]),
                                          batch3(g8)[:, :, DT - 1:DT].to_broadcast([H, DB, DT]), ALU.add))
            nc.vector.tensor_copy(dkrow[0:H, 0:NC], rows4[0:H, P - 1:SEQ:P])
            nc.vector.tensor_copy(dkrow[0:H, NC:], rows4[0:H, SEQ + DT - 1:N:DT]).then_inc(rows_ready, 1)
            for g in range(TT):
                n = P if g != TT - 1 else NS
                dve.wait_ge(cols_turned, g + 1)
                nc.vector.tensor_copy(cols[0:n, g, :, :], PS[0:n, g % 4, 0:P].rearrange("p (a b) -> p a b", a=4)[:, :, 0:H])\
                    .then_inc(cols_taken, 1)

        def gate_tensor(pe):
            pe.wait_ge(rows_ready, 1)
            for g in range(TT):
                n = P if g != TT - 1 else NS
                if g >= 4:
                    pe.wait_ge(cols_taken, g - 3)
                nc.tensor.transpose(PS[0:n, g % 4, 0:P], rows4[:, g * P:g * P + n], IDENT[:, :]).then_inc(cols_turned, 1)
            for p in range(NP):
                mm = nc.tensor.matmul(PS[:, 5, 16 * p:16 * p + 16], pair_sel[0:H, p, :], dkrow[0:H, :], start=True, stop=True)
            mm.then_inc(dec_ready, 1)

        def m_store(sp):
            sp.wait_ge(rows_ready, 1)
            with nc.allow_non_contiguous_dma(reason="one value per head"):
                stored(sp.dma_start(O["m_p"].rearrange("a h -> h a"), m_out[0:H, 0:1]))
                stored(sp.dma_start(O["m_s"].rearrange("b h -> h b"), m_out[0:H, 1:1 + DB]))

        lb = cut(SC, 0, H, P)
        la2 = cut(SC, 1024, H, P), cut(SC, 2048, H, P)
        mnum = cut(SC, 3072, H, V1W)
        hout = cut(SC, 3592, H, HD)
        kw = cut(HB, BIG + 2 * NP * N + TT * AW + N, AW)
        cst = cut(XN, ML0 + 3448, NP, 2 * V1W)
        den = SMALL[:, 16:24]
        rden = SMALL[:, 24:32]
        sample_c = cut(WRT, 0, DB, NP * 2 * V1W)
        q_mask = cut(HB, BIG + 2 * NP * N, DB, NP * NS)
        kwm = cut(SC, 2048, 2, AW)
        n_rows = cut(HB, BIG + 2 * NP * N + DB * NP * NS, P)
        n_stage = cut(HB, BIG + 2 * NP * N + DB * NP * NS + P, 40)
        n_out = cut(HB, BIG + 2 * NP * N + DB * NP * NS + 2 * P, P)

        c_ready, c_l, c_e, c_a, c_num, c_h, c_ht, c_cat, c_kw, c_upd, c_state = (
            sem(n) for n in ("chunk_scores", "chunk_logits", "chunk_weights", "chunk_a", "chunk_num", "chunk_h",
                             "chunk_h_turned", "chunk_done", "chunk_kw", "chunk_update", "chunk_state"))

        def slot(h):
            return (h % 2) * (H // 2) + h // 2

        def scores_tensor(pe, t0, n):
            for h in range(H):
                rows = slice(HD * (h % 2), HD * (h % 2) + HD)
                nc.tensor.matmul(PS[0:n, h % 2, (h // 2) * P:(h // 2) * P + n], qk[rows, NP + h // 2, t0:t0 + n],
                                 qk[rows, h // 2, t0:t0 + n], start=True, stop=True)
                mm = nc.tensor.matmul(PS[0:n, 2 + h % 2, (h // 2) * P:(h // 2) * P + n], head_sel[0:H, h, 0:n],
                                      gu[0:H, t0:t0 + n], start=True, stop=True)
            mm.then_inc(c_ready, 1)

        def num_tensor(pe, c, n):
            pe.wait_ge(c_a, c + 1)
            for h in range(H):
                mm = nc.tensor.matmul(PS[0:n, 4 + h // 4, (h % 4) * V1W:(h % 4 + 1) * V1W], la2[c % 2][0:n, slot(h), 0:n],
                                      v1[0:n, c, h * V1W:(h + 1) * V1W], start=True, stop=True)
            mm.then_inc(c_num, 1)

        def turn_h_tensor(pe, c, n):
            pe.wait_ge(c_h, c + 1)
            for j in range(NP):
                mm = nc.tensor.transpose(PS[:, 4, j * P:j * P + n], hout[0:n, 2 * j:2 * j + 2, :].rearrange("p a b -> p (a b)"),
                                         IDENT[0:n, 0:n])
            mm.then_inc(c_ht, 1)

        def chunk_tensor(pe):
            scores_tensor(pe, 0, P)
            for c in range(NC):
                if c:
                    pe.wait_ge(c_state, c)
                for p in range(NP):
                    nc.tensor.matmul(PS[:, 6 + p // 2, (p % 2) * 2 * V1W:(p % 2 + 1) * 2 * V1W], qk[:, p, c * P:(c + 1) * P],
                                     cst[:, p, :], start=True, stop=True)
                if c:
                    pe.wait_ge(c_cat, c)
                num_tensor(pe, c, P)
                if c + 1 < NC:
                    scores_tensor(pe, (c + 1) * P, P)
                pe.wait_ge(c_kw, c + 1)
                pe.wait_ge(c_h, c + 1)
                for p in range(NP):
                    mm = nc.tensor.matmul(PS[:, 6 + p // 2, (p % 2) * 2 * V1W:(p % 2 + 1) * 2 * V1W], kw[:, p * P:(p + 1) * P],
                                          v1[:, c, p * 2 * V1W:(p + 1) * 2 * V1W], start=True, stop=True)
                mm.then_inc(c_upd, 1)
                turn_h_tensor(pe, c, P)

        def chunk_scalar(act, chunks):
            for c in chunks:
                n = P if c < NC else NS
                act.wait_ge(c_l, c + 1)
                for h in range(H):
                    last = nc.scalar.activation(lb[0:n, slot(h), 0:n], lb[0:n, slot(h), 0:n], ACT.Exp, bias=cols[0:n, c, 2, h:h + 1])
                last.then_inc(c_e, 1)

        def chunk_pool(pool, chunks):
            for c in chunks:
                n = P if c < NC else NS
                if 0 < c < NC:
                    pool.wait_ge(c_upd, c)
                nc.gpsimd.tensor_tensor(kw[0:n, :].rearrange("p (h d) -> p h d", h=H),
                                        ktok[0:n, c, :].rearrange("p (h d) -> p h d", h=H),
                                        colx[0:n, c, 2, :].unsqueeze(2).to_broadcast([n, H, HD]), ALU.mult).then_inc(c_kw, 1)

        def chunk_logits(dve, c, n, mask):
            dve.wait_ge(c_ready, c + 1)
            if c and c < NC:
                dve.wait_ge(c_a, c)
            nc.vector.tensor_tensor(lb[0:n, :, 0:n], bank2(n, 2), mask.unsqueeze(1).to_broadcast([n, H, n]), ALU.add).then_inc(c_l, 1)

        def bank2(n, b):
            return PS[0:n, b:b + 2, :].rearrange("p a (h t) -> p (a h) t", h=4)[:, :, 0:n]

        def chunk_weights(dve, c, n):
            dve.wait_ge(c_e, c + 1)
            nc.vector.scalar_tensor_tensor(out=la2[c % 2][0:n, :, 0:n], in0=bank2(n, 0), scalar=HD ** -0.5, in1=lb[0:n, :, 0:n],
                                           op0=ALU.mult, op1=ALU.mult).then_inc(c_a, 1)

        def chunk_output(dve, c, n):
            chain = chains["dve"]
            dve.wait_ge(c_num, c + 1)
            iw = colx[0:n, c, 0, :].rearrange("p (a h) -> p a h", a=2)
            m4 = mnum[0:n].rearrange("p (a h) d -> p a h d", a=2)
            part = lambda b: PS[0:n, b, 0:4 * V1W].rearrange("p (h d) -> p h d", h=4)
            for a in range(2):
                last = nc.vector.tensor_tensor(m4[:, a], part(6 + a), iw[:, a].unsqueeze(2).to_broadcast([n, 4, V1W]), ALU.mult)
            chain(last)
            for a in range(2):
                last = nc.vector.tensor_tensor(m4[:, a], part(4 + a), m4[:, a], ALU.add)
            chain(last)
            chain(nc.vector.tensor_scalar(den[0:n], mnum[0:n, :, HD], -1.0, None, ALU.mult))
            chain(nc.vector.tensor_tensor(den[0:n], den[0:n], mnum[0:n, :, HD], ALU.max))
            chain(nc.vector.tensor_tensor(den[0:n], den[0:n], colx[0:n, c, 1, :], ALU.max))
            chain(nc.vector.reciprocal(rden[0:n], den[0:n]))
            nc.vector.tensor_tensor(hout[0:n], mnum[0:n, :, 0:HD], rden[0:n].unsqueeze(2).to_broadcast([n, H, HD]), ALU.mult)\
                .then_inc(c_h, 1)

        def chunk_place(dve, c, n, t0):
            dve.wait_ge(c_ht, c + 1)
            nc.vector.tensor_tensor(sig_o[:, :, t0:t0 + n], PS[:, 4, :].rearrange("p (j t) -> p j t", j=NP)[:, :, 0:n],
                                    sig_o[:, :, t0:t0 + n], ALU.mult).then_inc(c_cat, 1)

        def state_update(state, c, banks, signal):
            chain = chains["dve"]
            for e in range(2):
                rows, cs = slice(HD * e, HD * e + HD), slice(V1W * e, V1W * e + V1W)
                last = nc.vector.tensor_tensor(state[rows, :, cs], state[rows, :, cs],
                                               dec[rows, :, c:c + 1].to_broadcast([HD, NP, V1W]), ALU.mult)
            chain(last)
            for e in range(2):
                rows, cs = slice(HD * e, HD * e + HD), slice(V1W * e, V1W * e + V1W)
                for a in range(2):
                    upd = PS[rows, banks + a, 0:4 * V1W].rearrange("p (j d) -> p j d", j=2)
                    last = nc.vector.tensor_tensor(state[rows, 2 * a:2 * a + 2, cs], upd[:, :, cs], state[rows, 2 * a:2 * a + 2, cs], ALU.add)
            last.then_inc(signal, 1)

        def chunk_vector(dve):
            chunk_logits(dve, 0, P, causal[:, :])
            chunk_weights(dve, 0, P)
            for c in range(NC):
                chunk_output(dve, c, P)
                if c + 1 < NC:
                    chunk_logits(dve, c + 1, P, causal[:, :])
                dve.wait_ge(c_upd, c + 1)
                if c:
                    dve.wait_ge(c_state, c)
                state_update(cst, c, 6, c_state)
                if c + 1 < NC:
                    chunk_weights(dve, c + 1, P)
                chunk_place(dve, c, P, c * P)
            dve.wait_ge(c_state, NC)

        sc_zeroed, sc_landed, n_turned, n_put, qm_ready, kwm_ready, su_ready, su_done, n_ready, n_rows_ready = (
            sem(n) for n in ("sc_zeroed", "sc_landed", "n_turned", "n_put", "q_mask_ready", "kwm_ready", "sample_update",
                             "sample_state", "n_ready", "n_rows_ready"))
        sc4 = sample_c[:, :, :].rearrange("p b (j d) -> p b j d", j=NP)

        def sample_state_load(sp):
            sp.wait_ge(sc_zeroed, 1)
            src = A["state_mlstm_C"].rearrange("b (j e) k v -> e k b j v", e=2)
            with nc.allow_non_contiguous_dma(reason="rows of 64 floats"):
                for e in range(2):
                    for b in range(DB):
                        sp.dma_start(sc4[HD * e:HD * e + HD, b, :, V1W * e:V1W * e + HD], src[e, :, b]).then_inc(sc_landed, 16)
            sp.wait_ge(phase_done, 4 * PH["chunks"])
            sp.dma_start(n_rows[0:DB * NP, :], A["state_mlstm_n"].rearrange("b (j e) k -> (b j) (e k)", e=2)).then_inc(n_landed, 16)

        n_landed = sem("n_landed")

        def sample_pool(pool):
            chains["pool"](nc.gpsimd.memset(sample_c[:, :, :], 0.0))
            nc.gpsimd.memset(SMALL[:, 40:41], 0.0).then_inc(sc_zeroed, 1)

        def q_mask_pool(pool):
            chains["pool"](nc.gpsimd.memset(q_mask[:, :, :], 0.0))
            for b in range(DB):
                qm = q_mask[:, b, :].rearrange("p (j t) -> p j t", j=NP)
                last = nc.gpsimd.tensor_copy(qm[:, :, b * DT:(b + 1) * DT], qk[:, 0:NP, SEQ + b * DT:SEQ + (b + 1) * DT])
            last.then_inc(qm_ready, 1)

        def sample_tensor(pe):
            pe.wait_ge(n_landed, 16)
            nc.tensor.transpose(PS[:, 7, 480:512], n_rows[0:DB * NP, :], IDENT[0:DB * NP, 0:DB * NP]).then_inc(n_turned, 1)
            scores_tensor(pe, SEQ, NS)
            pe.wait_ge(n_put, 1)
            pe.wait_ge(qm_ready, 1)
            for p in range(NP):
                for b in range(DB):
                    mm = nc.tensor.matmul(PS[0:NS, 6 + p // 2, (p % 2) * 2 * V1W:(p % 2 + 1) * 2 * V1W],
                                          q_mask[:, b, p * NS:(p + 1) * NS], sc4[:, b, p, :], start=(b == 0), stop=(b == DB - 1))
            num_tensor(pe, NC, NS)
            turn_h_tensor(pe, NC, NS)
            for b in range(DB):
                pe.wait_ge(kwm_ready, b + 1)
                bank = 4 + 2 * (b % 2)
                if b == 0:
                    pe.wait_ge(c_cat, NC + 1)
                if b >= 2:
                    pe.wait_ge(su_done, b - 1)
                for p in range(NP):
                    mm = nc.tensor.matmul(PS[:, bank + p // 2, (p % 2) * 2 * V1W:(p % 2 + 1) * 2 * V1W],
                                          kwm[0:NS, b % 2, p * P:(p + 1) * P], v1[0:NS, NC, p * 2 * V1W:(p + 1) * 2 * V1W],
                                          start=True, stop=True)
                mm.then_inc(su_ready, 1)
            pe.wait_ge(n_ready, 1)
            nc.tensor.transpose(PS[0:(DB + 1) * NP, 0, 0:P], n_stage[:, 0:(DB + 1) * NP], IDENT[:, :]).then_inc(n_rows_ready, 1)

        def sample_vector(dve):
            chain = chains["dve"]
            dve.wait_ge(n_turned, 1)
            dve.wait_ge(sc_landed, 16 * 16)
            for e in range(2):
                rows = slice(HD * e, HD * e + HD)
                last = nc.vector.tensor_copy(sc4[rows, :, :, V1W * e + HD], PS[rows, 7, 480:512].rearrange("p (b j) -> p b j", b=DB))
            last.then_inc(n_put, 1)
            chunk_logits(dve, NC, NS, sample_causal[0:NS])
            chunk_weights(dve, NC, NS)
            chunk_output(dve, NC, NS)
            chunk_place(dve, NC, NS, SEQ)
            dve.wait_ge(c_kw, NC + 1)

            def masked(b):
                if b >= 2:
                    dve.wait_ge(su_ready, b - 1)
                nc.vector.tensor_scalar(kwm[0:NS, b % 2, :], kw[0:NS, :], batch_sel[0:NS, b:b + 1], None, ALU.mult).then_inc(kwm_ready, 1)
            masked(0)
            for b in range(DB):
                if b + 1 < DB:
                    masked(b + 1)
                dve.wait_ge(su_ready, b + 1)
                state_update(sc4[:, b], NC + b, 4 + 2 * (b % 2), su_done)
            dve.wait_ge(su_done, DB)
            for e in range(2):
                rows = slice(HD * e, HD * e + HD)
                nc.vector.tensor_copy(n_stage[rows, 0:DB * NP].rearrange("p (b j) -> p b j", b=DB), sc4[rows, :, :, V1W * e + HD])
                last = nc.vector.tensor_copy(n_stage[rows, DB * NP:(DB + 1) * NP], cst[rows, :, V1W * e + HD])
            last.then_inc(n_ready, 1)
            dve.wait_ge(n_rows_ready, 1)
            nc.vector.tensor_copy(n_out[0:(DB + 1) * NP, :], PS[0:(DB + 1) * NP, 0, 0:P]).then_inc(n_out_ready, 1)

        n_out_ready = sem("n_out_ready")

        def state_store(sp):
            sp.wait_ge(n_out_ready, 1)
            cs, cp = (O[n].rearrange("b (j e) k v -> e k b j v", e=2) for n in ("C_s", "C_p"))
            with nc.allow_non_contiguous_dma(reason="rows of 64 floats"):
                for e in range(2):
                    rows, c64 = slice(HD * e, HD * e + HD), slice(V1W * e, V1W * e + HD)
                    stored(sp.dma_start(cp[e, :, 0], cst[rows, :, c64]))
                    for b in range(DB):
                        stored(sp.dma_start(cs[e, :, b], sc4[rows, b, :, c64]))
            stored(sp.dma_start(O["n_s"].rearrange("b (j e) k -> (b j) (e k)", e=2), n_out[0:DB * NP, :]))
            stored(sp.dma_start(O["n_p"].rearrange("b (j e) k -> (b j) (e k)", e=2), n_out[DB * NP:(DB + 1) * NP, :]))
            sp.wait_ge(out_stored, 16 * stores[0])

        KT = PAST // P
        kc = cut(HB, BIG, 2, KT * AW)
        kT = cut(HB, BIG + 2 * KT * AW, NP, PAST), cut(WRT, 0, NP, PAST)
        vc = cut(XN, 0, 2, KT * AW)
        wl = cut(SC, 0, PAST + NS)
        wbias = cut(SC, PAST + NS, PAST)
        wnew = cut(SC, 2 * PAST + NS, DB // 2 * NS)
        wpt = cut(SC, 2 * PAST + NS + DB // 2 * NS, 9, P)
        kc_landed = [sem(f"kc_landed{i}") for i in range(2)]
        vc_landed = [sem(f"vc_landed{i}") for i in range(2)]
        wb_landed = sem("wb_landed")
        wk_taken = [sem(f"wk_taken{i}") for i in range(2)]
        wk_turned, ws_ready, wl_ready, wp_ready, wp_turned, wp_taken, wo_ready, wo_taken, wl_free = (
            sem(n) for n in ("wk_turned", "ws_ready", "wl_ready", "wp_ready", "wp_turned", "wp_taken",
                             "wo_ready", "wo_taken", "wl_free"))

        def win_load(sp):
            sp.wait_ge(phase_done, 4 * PH["sample"])
            sp.dma_start(wbias, A["sample_bias"]).then_inc(wb_landed, 16)
            sp.dma_start(wnew, A["sample_new_bias"]).then_inc(wb_landed, 16)
            kd, vd = (A[n].rearrange("b (t p) h d -> b p t (h d)", p=P) for n in ("cache_win_k", "cache_win_v"))
            def load_k(b):
                if b >= 2:
                    sp.wait_ge(wk_turned, NP * 2 * (b - 1))
                sp.dma_start(kc[:, b % 2, :].rearrange("p (t n) -> p t n", n=AW), kd[b]).then_inc(kc_landed[b % 2], 16)

            def load_v(b):
                if b >= 2:
                    sp.wait_ge(wo_ready, b - 1)
                sp.dma_start(vc[:, b % 2, :].rearrange("p (t n) -> p t n", n=AW), vd[b]).then_inc(vc_landed[b % 2], 16)
            load_k(0)
            load_k(1)
            for pair in range(DB // 2):
                if pair + 1 < DB // 2:
                    load_k(2 * pair + 2)
                if pair == 0:
                    load_v(0)
                    load_v(1)
                if pair + 1 < DB // 2:
                    load_k(2 * pair + 3)
                if pair:
                    load_v(2 * pair)
                    load_v(2 * pair + 1)

        def win_tensor(pe):
            def turn_k(b):
                pe.wait_ge(kc_landed[b % 2], 16 * (b // 2 + 1))
                kb = kc[:, b % 2, :].rearrange("p (t n) -> p t n", n=AW)
                for p in range(NP):
                    for half in range(2):
                        if b or p:
                            pe.wait_ge(wk_taken[half], NP * b + p)
                        for j in range(4):
                            mm = nc.tensor.transpose(PS[:, half, j * P:(j + 1) * P], kb[:, 4 * half + j, p * P:(p + 1) * P],
                                                     IDENT[:, :])
                        mm.then_inc(wk_turned, 1)

            def scores(b):
                e, pair = b % 2, b // 2
                for half in range(2):
                    pe.wait_ge(wk_taken[half], NP * (b + 1))
                if e == 0 and pair:
                    pe.wait_ge(wl_ready, pair)
                x = kT[b % 2]
                for c, (w, x) in enumerate(((512, x[:, :, 0:512]), (512, x[:, :, 512:PAST]), (NS, KNEW[:, :, :]))):
                    for p in range(NP):
                        mm = nc.tensor.matmul(PS[HD * e:HD * e + HD, 2 + c, 0:w], QX[:, p, b, :], x[:, p, :],
                                              start=(p == 0), stop=(p == NP - 1))
                mm.then_inc(ws_ready, 1)

            def turn_p(pair):
                pe.wait_ge(wp_ready, pair + 1)
                for q in range(3):
                    n = 3 * pair + q
                    if n >= 2:
                        pe.wait_ge(wp_taken, n - 1)
                    if q < 2:
                        for j in range(4):
                            mm = nc.tensor.transpose(PS[:, 5 + n % 2, j * P:(j + 1) * P], wl[:, (4 * q + j) * P:(4 * q + j + 1) * P],
                                                     IDENT[:, :])
                    else:
                        mm = nc.tensor.transpose(PS[0:NS, 5 + n % 2, 0:P], wl[:, PAST:PAST + NS], IDENT[:, :])
                    mm.then_inc(wp_turned, 1)

            def values(pair):
                pe.wait_ge(wp_taken, 3 * pair + 3)
                if pair:
                    pe.wait_ge(wo_taken, 2 * pair)
                for e in range(2):
                    pe.wait_ge(vc_landed[e], 16 * (pair + 1))
                    vb = vc[:, e, :].rearrange("p (t n) -> p t n", n=AW)
                    for p in range(NP):
                        cs = slice(HD * e + 2 * DT * p, HD * e + 2 * DT * (p + 1))
                        for t in range(KT + 1):
                            v = vb[:, t, p * P:(p + 1) * P] if t < KT else VNEW[:, p * P:(p + 1) * P]
                            x = wpt[:, t, cs] if t < KT else wpt[0:NS, t, cs]
                            mm = nc.tensor.matmul(PS[:, 7, (4 * e + p) * 16:(4 * e + p + 1) * 16], v, x, start=(t == 0), stop=(t == KT))
                    mm.then_inc(wo_ready, 1)

            turn_k(0)
            for b in range(DB):
                if b + 1 < DB:
                    turn_k(b + 1)
                scores(b)
                if b >= 2:
                    (turn_p if b % 2 == 0 else values)(b // 2 - 1)
            turn_p(DB // 2 - 1)
            values(DB // 2 - 1)

        def take_k(eng, half, b):
            for p in range(NP):
                eng.wait_ge(wk_turned, 2 * (NP * b + p) + half + 1)
                if p == 0 and b >= 2:
                    eng.wait_ge(ws_ready, b - 1)
                out, src = kT[b % 2][:, p, 512 * half:512 * half + 512], PS[:, half, :]
                ins = nc.vector.tensor_copy(out, src) if half else nc.scalar.activation(out, src, ACT.Copy)
                ins.then_inc(wk_taken[half], 1)

        def win_scalar(act):
            def take_p(pair):
                for q in range(3):
                    n = 3 * pair + q
                    act.wait_ge(wp_turned, n + 1)
                    if q == 0 and pair:
                        act.wait_ge(wo_ready, 2 * pair)
                    if q < 2:
                        last = nc.scalar.activation(wpt[:, 4 * q:4 * q + 4, :], PS[:, 5 + n % 2, :].rearrange("p (a b) -> p a b", a=4), ACT.Copy)
                    else:
                        last = nc.scalar.activation(wpt[0:NS, KT, :], PS[0:NS, 5 + n % 2, 0:P], ACT.Copy)
                    last.then_inc(wp_taken, 1)
            take_k(act, 0, 0)
            for b in range(DB):
                if b + 1 < DB:
                    take_k(act, 0, b + 1)
                if b % 2:
                    act.wait_ge(wl_ready, b // 2 + 1)
                    nc.scalar.activation(wl[:, :], wl[:, :], ACT.Exp, bias=negm[:, 0:1], accum_out=asum[:, 0:1]).then_inc(wl_free, 1)
                elif b:
                    take_p(b // 2 - 1)
            take_p(DB // 2 - 1)

        def win_vector(dve):
            chain = chains["dve"]

            def softmax(pair):
                dve.wait_ge(ws_ready, 2 * pair + 2)
                if pair:
                    dve.wait_ge(wp_turned, 3 * pair)
                nc.vector.tensor_tensor_reduce(wl[:, 0:PAST], PS[:, 2:4, :].rearrange("p a b -> p (a b)"), wbias, 1.0, 3 * NEG,
                                               ALU.add, ALU.max, amax[:, 0:1])
                chain(nc.vector.tensor_tensor_reduce(wl[:, PAST:PAST + NS], PS[:, 4, 0:NS], wnew[:, pair * NS:(pair + 1) * NS],
                                                     1.0, 3 * NEG, ALU.add, ALU.max, amax[:, 1:2]))
                chain(nc.vector.tensor_tensor(amax[:, 0:1], amax[:, 0:1], amax[:, 1:2], ALU.max))
                nc.vector.tensor_scalar(negm[:, 0:1], amax[:, 0:1], -1.0, None, ALU.mult).then_inc(wl_ready, 1)
                dve.wait_ge(wl_free, pair + 1)
                chain(nc.vector.reciprocal(arec[:, 0:1], asum[:, 0:1]))
                nc.vector.tensor_scalar(wl[:, :], wl[:, :], arec[:, 0:1], None, ALU.mult).then_inc(wp_ready, 1)

            def output(pair):
                dve.wait_ge(wo_ready, 2 * pair + 2)
                for e in range(2):
                    b = 2 * pair + e
                    for r in range(2):
                        rows = slice(HD * r, HD * r + HD)
                        src = PS[rows, 7, 64 * e:64 * e + 64].rearrange("p (j t) -> p j t", j=NP)[:, :, DT * r:DT * r + DT]
                        last = nc.vector.tensor_copy(cat[rows, 0:NP, SEQ + b * DT:SEQ + (b + 1) * DT], src)
                    last.then_inc(wo_taken, 1)

            dve.wait_ge(wb_landed, 32)
            take_k(dve, 1, 0)
            for b in range(DB):
                if b + 1 < DB:
                    take_k(dve, 1, b + 1)
                if b % 2:
                    softmax(b // 2)
                    if b >= 3:
                        output(b // 2 - 1)
            output(DB // 2 - 1)

        mem_tok = cut(HB, BIG, 2, D)
        mem_T = cut(HB, BIG + 2048, KB, NMEM)
        mem_n = cut(HB, BIG + 4096, KB, NMEM)
        mkT = cut(HB, BIG + 6144, KB, NMEM)
        mvT = cut(HB, BIG + 8192, KB, NMEM)
        mk_tok = cut(HB, BIG + 10240, 2, D)
        mv_tok = cut(HB, BIG + 12288, 2, D)
        mem_landed, mem_turned, mem_taken, mkv_turned, mkv_taken = (
            sem(n) for n in ("mem_landed", "mem_turned", "mem_taken", "mkv_turned", "mkv_taken"))

        def mem_load(sp):
            sp.wait_ge(phase_done, 4 * PH["win"])
            sp.dma_start(mem_tok[:, :, :], A["mem_prompt"][0].rearrange("(t p) d -> p t d", p=P)).then_inc(mem_landed, 16)

        def mem_turn_tensor(pe):
            pe.wait_ge(mem_landed, 16)
            for g in range(4):
                t, half = g // 2, g % 2
                for j in range(4):
                    mm = nc.tensor.transpose(PS[:, g, j * P:(j + 1) * P], mem_tok[:, t, (4 * half + j) * P:(4 * half + j + 1) * P], IDENT[:, :])
                mm.then_inc(mem_turned, 1)

        def mem_turn_vector(dve):
            for g in range(4):
                t, half = g // 2, g % 2
                dve.wait_ge(mem_turned, g + 1)
                nc.vector.tensor_copy(mem_T[:, 4 * half:4 * half + 4, t * P:(t + 1) * P], PS[:, g, :].rearrange("p (j n) -> p j n", j=4))

        def mkv_turn_tensor(pe):
            for g in range(8):
                src, t, half = (mkT, mvT)[g // 4], g % 4 // 2, g % 2
                for j in range(4):
                    mm = nc.tensor.transpose(PS[:, g, j * P:(j + 1) * P], src[:, 4 * half + j, t * P:(t + 1) * P], IDENT[:, :])
                mm.then_inc(mkv_turned, 1)

        def mkv_turn_scalar(act):
            for g in range(8):
                dst, t, half = (mk_tok, mv_tok)[g // 4], g % 4 // 2, g % 2
                act.wait_ge(mkv_turned, g + 1)
                nc.scalar.activation(dst[:, t, 512 * half:512 * half + 512], PS[:, g, :], ACT.Copy).then_inc(mkv_taken, 1)

        def mkv_store(sp):
            sp.wait_ge(mkv_taken, 8)
            for name, src in (("mem_k", mk_tok), ("mem_v", mv_tok)):
                stored(sp.dma_start(O[name][0].rearrange("(t p) h d -> p t (h d)", p=P), src[:, :, :]))

        cq = cat
        co = xn
        xl = cut(SC, 0, 2, XH * NMEM)
        xpt = cut(SC, 2048, 2, 8 * P)
        xmax, xsum, xrec = SMALL[:, 48:56], SMALL[:, 56:64], SMALL[:, 64:72]
        xs_ready, xm_ready, xp_ready, xn_ready, xt_ready, xt_taken, xo_ready, xo_taken = (
            sem(n) for n in ("xs_ready", "xm_ready", "xp_ready", "xn_ready", "xt_ready", "xt_taken", "xo_ready", "xo_taken"))

        def cross_tensor(pe):
            def scores(t):
                if t >= 2:
                    pe.wait_ge(xp_ready, t - 1)
                b0 = 2 * (t % 2)
                for h in range(XH):
                    for k in range(2):
                        mm = nc.tensor.matmul(PS[:, b0 + h // 2, (h % 2) * NMEM:(h % 2 + 1) * NMEM], cq[:, 2 * h + k, t * P:(t + 1) * P],
                                              mkT[:, 2 * h + k, :], start=(k == 0), stop=(k == 1))
                mm.then_inc(xs_ready, 1)
            scores(0)
            for t in range(NC):
                if t + 1 < NC:
                    scores(t + 1)
                pe.wait_ge(xn_ready, t + 1)
                if t:
                    pe.wait_ge(xt_taken, t)
                for i in range(8):
                    mm = nc.tensor.transpose(PS[:, 4 + i // 4, (i % 4) * P:(i % 4 + 1) * P], xl[:, t % 2, i * P:(i + 1) * P], IDENT[:, :])
                mm.then_inc(xt_ready, 1)
                pe.wait_ge(xt_taken, t + 1)
                if t:
                    pe.wait_ge(xo_taken, t)
                for h in range(XH):
                    for db in range(2):
                        i = 2 * h + db
                        for m in range(2):
                            mm = nc.tensor.matmul(PS[:, 6 + i // 4, (i % 4) * P:(i % 4 + 1) * P], mv_tok[:, m, i * P:(i + 1) * P],
                                                  xpt[:, t % 2, (2 * h + m) * P:(2 * h + m + 1) * P], start=(m == 0), stop=(m == 1))
                mm.then_inc(xo_ready, 1)

        def cross_scalar(act):
            for t in range(NC):
                act.wait_ge(xm_ready, t + 1)
                b0, s4 = 2 * (t % 2), 4 * (t % 2)
                for h in range(XH):
                    last = nc.scalar.activation(xl[:, t % 2, h * NMEM:(h + 1) * NMEM],
                                                PS[:, b0 + h // 2, (h % 2) * NMEM:(h % 2 + 1) * NMEM], ACT.Exp,
                                                bias=xmax[:, s4 + h:s4 + h + 1], accum_out=xsum[:, s4 + h:s4 + h + 1])
                last.then_inc(xp_ready, 1)
                act.wait_ge(xt_ready, t + 1)
                if t >= 2:
                    act.wait_ge(xo_ready, t - 1)
                nc.scalar.activation(xpt[:, t % 2, :], PS[:, 4:6, :].rearrange("p a b -> p (a b)"), ACT.Copy).then_inc(xt_taken, 1)

        def cross_vector(dve):
            chain = chains["dve"]

            def maxima(t):
                b0, s4 = 2 * (t % 2), 4 * (t % 2)
                dve.wait_ge(xs_ready, t + 1)
                if t >= 2:
                    dve.wait_ge(xp_ready, t - 1)
                    dve.wait_ge(xt_ready, t - 1)
                nc.vector.tensor_reduce(xmax[:, s4:s4 + 4], PS[:, b0:b0 + 2, :].rearrange("p a (h m) -> p (a h) m", h=2), AX_X, ALU.max,
                                        negate=True).then_inc(xm_ready, 1)
            maxima(0)
            for t in range(NC):
                if t + 1 < NC:
                    maxima(t + 1)
                s4 = 4 * (t % 2)
                dve.wait_ge(xp_ready, t + 1)
                chain(nc.vector.reciprocal(xrec[:, s4:s4 + 4], xsum[:, s4:s4 + 4]))
                x3 = xl[:, t % 2, :].rearrange("p (h m) -> p h m", h=XH)
                nc.vector.tensor_tensor(x3, x3, xrec[:, s4:s4 + 4].unsqueeze(2).to_broadcast([P, XH, NMEM]), ALU.mult).then_inc(xn_ready, 1)
                dve.wait_ge(xo_ready, t + 1)
                nc.vector.tensor_copy(co[:, :, t * P:(t + 1) * P], PS[:, 6:8, :].rearrange("p a (j n) -> p (a j) n", j=4)).then_inc(xo_taken, 1)

        ck = cut(HB, BIG, 2, 2 * D)
        cv = cut(HB, BIG + 4096, 4, 2 * D)
        ckT = cut(HB, BIG + 12288, KB, NMEM), cut(WRT, 0, KB, NMEM)
        cqx = cut(SC, 0, KB, DB, XH * DT)
        yl = cut(SC, 2048, NMEM)
        ypt = cut(SC, 2304, 2, P)
        ck_landed = [sem(f"ck_landed{i}") for i in range(2)]
        cv_landed = [sem(f"cv_landed{i}") for i in range(2)]
        cqx_ready, yk_turned, yk_taken, ys_ready, ym_ready, yp_ready, yn_ready, yt_ready, yt_taken, yo_ready, yo_taken = (
            sem(n) for n in ("cqx_ready", "yk_turned", "yk_taken", "ys_ready", "ym_ready", "yp_ready", "yn_ready", "yt_ready",
                             "yt_taken", "yo_ready", "yo_taken"))

        def xsample_load(sp):
            sp.wait_ge(phase_done, 4 * PH["mkv"])
            kd, vd = (A[n].rearrange("b (t p) h d -> b p t (h d)", p=P) for n in ("cache_mem_k", "cache_mem_v"))
            for b in range(DB):
                if b >= 2:
                    sp.wait_ge(yk_turned, 4 * (b - 1))
                sp.dma_start(ck[:, b % 2, :].rearrange("p (t n) -> p t n", n=D), kd[b]).then_inc(ck_landed[b % 2], 16)
                if b == 1:
                    sp.wait_ge(phase_done, 4 * PH["cross"])
                    for v in range(4):
                        sp.dma_start(cv[:, v, :].rearrange("p (t n) -> p t n", n=D), vd[v]).then_inc(cv_landed[0], 16)
            for b in range(4, DB):
                sp.wait_ge(yo_ready, b - 3)
                sp.dma_start(cv[:, b % 4, :].rearrange("p (t n) -> p t n", n=D), vd[b]).then_inc(cv_landed[1], 16)
            sp.wait_ge(ys_ready, DB)

        def xsample_pool(pool):
            chains["pool"](nc.gpsimd.memset(cqx[:, :, :, :], 0.0))
            for h in range(XH):
                for k in (2 * h, 2 * h + 1):
                    last = nc.gpsimd.tensor_copy(cqx[:, k, :, h * DT:(h + 1) * DT], cq[:, k, SEQ:N].rearrange("p (b t) -> p b t", t=DT))
            last.then_inc(cqx_ready, 1)

        def xsample_tensor(pe):
            pe.wait_ge(cqx_ready, 1)
            def turn_k(b):
                pe.wait_ge(ck_landed[b % 2], 16 * (b // 2 + 1))
                kb = ck[:, b % 2, :].rearrange("p (t n) -> p t n", n=D)
                for q in range(4):
                    g = 4 * b + q
                    if g >= 2:
                        pe.wait_ge(yk_taken, g - 1)
                    for j in range(4):
                        mm = nc.tensor.transpose(PS[:, g % 2, j * P:(j + 1) * P], kb[:, j % 2, (2 * q + j // 2) * P:(2 * q + j // 2 + 1) * P],
                                                 IDENT[:, :])
                    mm.then_inc(yk_turned, 1)
            turn_k(0)
            for quad in range(2):
                for i in range(4):
                    b = 4 * quad + i
                    if b + 1 < DB:
                        turn_k(b + 1)
                    pe.wait_ge(yk_taken, 4 * (b + 1))
                    if i == 0 and quad:
                        pe.wait_ge(yp_ready, quad)
                    for k in range(KB):
                        mm = nc.tensor.matmul(PS[32 * i:32 * i + 32, 2, 0:NMEM], cqx[:, k, b, :], ckT[b % 2][:, k, :],
                                              start=(k == 0), stop=(k == KB - 1), tile_position=(0, 32 * i))
                    mm.then_inc(ys_ready, 1)
                pe.wait_ge(yn_ready, quad + 1)
                if quad:
                    pe.wait_ge(yt_taken, quad)
                for m in range(2):
                    mm = nc.tensor.transpose(PS[:, 3, m * P:(m + 1) * P], yl[:, m * P:(m + 1) * P], IDENT[:, :])
                mm.then_inc(yt_ready, 1)
                pe.wait_ge(yt_taken, quad + 1)
                pe.wait_ge(cv_landed[quad], 64)
                for i in range(4):
                    b = 4 * quad + i
                    if b >= 2:
                        pe.wait_ge(yo_taken, b - 1)
                    vb = cv[:, i, :].rearrange("p (t n) -> p t n", n=D)
                    for k in range(KB):
                        c0 = 32 * i + DT * (k // 2)
                        for m in range(2):
                            mm = nc.tensor.matmul(PS[:, 4 + b % 2, k * DT:(k + 1) * DT], vb[:, m, k * P:(k + 1) * P], ypt[:, m, c0:c0 + DT],
                                                  start=(m == 0), stop=(m == 1))
                    mm.then_inc(yo_ready, 1)

        def xsample_scalar(act):
            def take_k(b):
                for q in range(4):
                    g = 4 * b + q
                    act.wait_ge(yk_turned, g + 1)
                    if q == 0 and b >= 2:
                        act.wait_ge(ys_ready, b - 1)
                    nc.scalar.activation(ckT[b % 2][:, 2 * q:2 * q + 2, :], PS[:, g % 2, :].rearrange("p (a b) -> p a b", a=2), ACT.Copy)\
                        .then_inc(yk_taken, 1)
            take_k(0)
            for quad in range(2):
                for i in range(4):
                    if 4 * quad + i + 1 < DB:
                        take_k(4 * quad + i + 1)
                act.wait_ge(ym_ready, quad + 1)
                nc.scalar.activation(yl[:, :], PS[:, 2, 0:NMEM], ACT.Exp, bias=xmax[:, 0:1], accum_out=xsum[:, 0:1]).then_inc(yp_ready, 1)
                act.wait_ge(yt_ready, quad + 1)
                if quad:
                    act.wait_ge(yo_ready, 4 * quad)
                nc.scalar.activation(ypt[:, :, :], PS[:, 3, 0:2 * P].rearrange("p (a b) -> p a b", a=2), ACT.Copy).then_inc(yt_taken, 1)

        def xsample_vector(dve):
            for quad in range(2):
                dve.wait_ge(ys_ready, 4 * quad + 4)
                if quad:
                    dve.wait_ge(yt_ready, quad)
                nc.vector.tensor_reduce(xmax[:, 0:1], PS[:, 2, 0:NMEM], AX_X, ALU.max, negate=True).then_inc(ym_ready, 1)
                dve.wait_ge(yp_ready, quad + 1)
                chains["dve"](nc.vector.reciprocal(xrec[:, 0:1], xsum[:, 0:1]))
                nc.vector.tensor_scalar(yl[:, :], yl[:, :], xrec[:, 0:1], None, ALU.mult).then_inc(yn_ready, 1)
                for i in range(4):
                    b = 4 * quad + i
                    dve.wait_ge(yo_ready, b + 1)
                    nc.vector.tensor_copy(co[:, :, SEQ + b * DT:SEQ + (b + 1) * DT],
                                          PS[:, 4 + b % 2, 0:KB * DT].rearrange("p (k t) -> p k t", k=KB)).then_inc(yo_taken, 1)

        gate_taken, up_taken, d_ready, d_taken = sem("gate_taken"), sem("up_taken"), sem("d_ready"), sem("d_taken")

        def ffn_tensor(pe, n0):
            def block(i, s, first):
                pe.wait_ge(w_landed[s], i * 16 + (16 * (n0 // 4) + 16))
                if not first:
                    pe.wait_ge((gate_taken, up_taken)[s % 2], i * 2 + s // 2)
                for c, (t0, w) in enumerate(CHUNKS):
                    for k in range(KB):
                        mm = nc.tensor.matmul(PS[:, 3 * (s % 2) + c, 0:w], ring[:, s, k], xn[:, k, t0:t0 + w],
                                              start=(k == 0), stop=(k == KB - 1))
                mm.then_inc(z_ready, 1)
            for s in range(4):
                block(0, s, s < 2)
            with pe.Fori(1, FB // 2) as i:
                for s in range(4):
                    block(i, s, False)

        def ffn_scalar(act, n0):
            def pair(i, s, first):
                act.wait_ge(z_ready, i * 4 + (n0 + 2 * s + 1))
                if not first:
                    act.wait_ge(up_taken, i * 2 + (s - 1))
                for c, (t0, w) in enumerate(CHUNKS):
                    last = nc.scalar.activation(silu_g[:, s, t0:t0 + w], PS[:, c, 0:w], ACT.Silu)
                last.then_inc(gate_taken, 1)
            pair(0, 0, True)
            pair(0, 1, True)
            with act.Fori(1, FB // 2) as i:
                pair(i, 0, False)
                pair(i, 1, False)

        def ffn_vector(dve, n0):
            with dve.Fori(0, FB // 2) as i:
                for s in range(2):
                    dve.wait_ge(z_ready, i * 4 + (n0 + 2 * s + 2))
                    dve.wait_ge(gate_taken, i * 2 + (s + 1))
                    for c, (t0, w) in enumerate(CHUNKS):
                        last = nc.vector.tensor_tensor(hid[:, bass.ds(i * 2 + s, 1), t0:t0 + w], PS[:, 3 + c:4 + c, 0:w],
                                                       silu_g[:, s:s + 1, t0:t0 + w], ALU.mult)
                    last.then_inc(up_taken, 1)

        wd = cut(XN, 0, 2, FB * P)
        wd_landed = [sem(f"wd_landed{i}") for i in range(2)]

        def down_load(sp, n0):
            wv = A["w_down"].rearrange("(k p) n -> p k n", p=P)
            sp.wait_ge(z_ready, n0)
            for j in range(KB):
                if j >= 2:
                    sp.wait_ge(d_ready, j - 1)
                sp.dma_start(wd[:, j % 2, :].rearrange("p (k n) -> p k n", n=P), wv[:, :, j * P:(j + 1) * P]).then_inc(wd_landed[j % 2], 16)

        def down_tensor(pe):
            def block(i, s, first):
                pe.wait_ge(wd_landed[s], i * 16 + 16)
                if not first:
                    pe.wait_ge(d_taken, i * 2 + (s - 1))
                for c, (t0, w) in enumerate(CHUNKS):
                    for k in range(FB):
                        mm = nc.tensor.matmul(PS[:, 3 * s + c, 0:w], wd[:, s, k * P:(k + 1) * P], hid[:, k, t0:t0 + w],
                                              start=(k == 0), stop=(k == FB - 1))
                mm.then_inc(d_ready, 1)
            block(0, 0, True)
            block(0, 1, True)
            with pe.Fori(1, KB // 2) as i:
                block(i, 0, False)
                block(i, 1, False)

        def down_vector(dve):
            with dve.Fori(0, KB // 2) as i:
                for s in range(2):
                    dve.wait_ge(d_ready, i * 2 + (s + 1))
                    for c, (t0, w) in enumerate(CHUNKS):
                        last = add_residual(XT[:, bass.ds(i * 2 + s, 1), t0:t0 + w], PS[:, 3 * s + c:3 * s + c + 1, 0:w])
                    last.then_inc(d_taken, 1)

        yst = cut(HB, 0, 4, D)
        y_turned, y_taken = sem("y_turned"), sem("y_taken")
        y_stored = [sem(f"y_stored{i}") for i in range(4)]

        def out_tensor(pe):
            for g in range(2 * TT):
                t, half = g // 2, g % 2
                n = P if t < TT - 1 else NS
                if g >= 4:
                    pe.wait_ge(y_taken, g - 3)
                for j in range(4):
                    mm = nc.tensor.transpose(PS[0:n, g % 4, j * P:(j + 1) * P], xn[:, 4 * half + j, t * P:t * P + n], IDENT[:, :])
                mm.then_inc(y_turned, 1)

        def out_scalar(act):
            for g in range(2 * TT):
                t, half = g // 2, g % 2
                n = P if t < TT - 1 else NS
                act.wait_ge(y_turned, g + 1)
                if t >= 4:
                    act.wait_ge(y_stored[t % 4], 16 * (t // 4))
                nc.scalar.activation(yst[0:n, t % 4, 512 * half:512 * half + 512], PS[0:n, g % 4, :], ACT.Copy).then_inc(y_taken, 1)

        def out_store(sp):
            yp = O["y_p"][0].rearrange("(t p) d -> p t d", p=P)
            for t in range(TT):
                sp.wait_ge(y_taken, 2 * t + 2)
                if t < TT - 1:
                    sp.dma_start(yp[:, t, :], yst[:, t % 4, :]).then_inc(y_stored[t % 4], 16)
                else:
                    sp.dma_start(O["y_s"].rearrange("b t d -> (b t) d"), yst[0:NS, t % 4, :]).then_inc(y_stored[t % 4], 16)
            for s in range(4):
                sp.wait_ge(y_stored[s], 16 * len(range(s, TT, 4)))

        cache_stored = sem("cache_stored")

        def cache_copy(act):
            for b in range(DB):
                for o, a in (("win_k_s", "cache_win_k"), ("win_v_s", "cache_win_v")):
                    act.dma_start(O[o][b, 0:PAST].rearrange("(p r) h d -> p (r h d)", p=P),
                                  A[a][b].rearrange("(p r) h d -> p (r h d)", p=P)).then_inc(cache_stored, 16)

        order = ["turn", "norm_x", "att_proj", "kv", "att", "ml_proj", "conv_state", "conv", "gates", "chunks", "sample",
                 "win", "mix_norm", "out", "mem_turn", "mem_norm", "mem_proj", "cq_norm", "cq", "mkv", "cross", "xsample", "co", "ffn_norm",
                 "ffn", "down", "final_norm", "end"]
        PH = {name: i + 1 for i, name in enumerate(order)}
        NB = {}
        count = 0
        for name, blocks in (("aq", 4), ("akv", 8), ("qk", 8), ("mv", 4), ("mo", 4), ("out", 8), ("mk", 8), ("mv2", 8), ("cq", 8),
                             ("co", 8), ("ffn", 2 * FB), ("down", KB)):
            NB[name] = count
            count += blocks
        MCH = ((0, NMEM),)
        J = {}
        j = 0
        for r, (name, nb) in enumerate((("x", 8), ("att", 4), ("ml", 4), ("mem", 8), ("cross", 8), ("ffn", 8), ("final", 8))):
            J[name] = (j, r)
            j += nb
        chains = {}

        block = ctx.enter_context(nc.Block())

        @block.sync
        def _(sp):
            load_inputs(sp)
            win = A["w_in"]
            proj_load(sp, [w_view(win, 0)], 4, NB["aq"])
            proj_load(sp, [w_view(win, AW)], 8, NB["akv"])
            sp.wait_ge(phase_done, 4 * PH["att_proj"])
            kv_store(sp)
            sp.wait_ge(phase_done, 4 * PH["kv"])
            att_load(sp)
            ml_loads(sp)
            sp.wait_ge(phase_done, 4 * PH["att"])
            proj_load(sp, [w_view(win, 3 * AW)], 8, NB["qk"])
            proj_load(sp, [w_view(win, 5 * AW)], 4, NB["mv"])
            proj_load(sp, [w_view(win, 6 * AW)], 4, NB["mo"])
            ml_tables(sp)
            conv_store(sp)
            m_store(sp)
            sp.wait_ge(phase_done, 4 * PH["gates"])
            sample_state_load(sp)
            state_store(sp)
            win_load(sp)
            mem_load(sp)
            proj_load(sp, [w_view(A["w_out"])], 8, NB["out"])
            proj_load(sp, [w_view(A["w_ck"])], 8, NB["mk"])
            proj_load(sp, [w_view(A["w_cv"])], 8, NB["mv2"])
            proj_load(sp, [w_view(A["w_cq"])], 8, NB["cq"])
            mkv_store(sp)
            xsample_load(sp)
            proj_load(sp, [w_view(A["w_co"])], 8, NB["co"])
            proj_load(sp, [w_view(A["w_gate"]), w_view(A["w_up"])], 2 * FB, NB["ffn"])
            down_load(sp, NB["down"])
            out_store(sp)
            sp.wait_ge(out_stored, 16 * stores[0])
            sp.wait_ge(cache_stored, 16 * 2 * DB)

        @block.tensor
        def _(pe):
            c = chains["pe"] = Chain(pe, None)
            turn_tensor(pe)
            c.meet()
            norm_tensor(pe, KB, N, *J["x"])
            c.meet()
            proj_tensor(pe, xn, 4, NB["aq"])
            proj_tensor(pe, xn, 8, NB["akv"])
            c.meet()
            kv_turn_tensor(pe)
            c.meet()
            att_tensor(pe)
            pe.wait_ge(o_taken, len(UNITS))
            att_turn_tensor(pe)
            c.meet()
            gates_tensor(pe)
            pe.wait_ge(gates_read, 1)
            proj_tensor(pe, xn, 8, NB["qk"])
            proj_tensor(pe, xn, 4, NB["mv"])
            proj_tensor(pe, xn, 4, NB["mo"])
            c.meet()
            conv_state_tensor(pe)
            c.meet()
            c.meet()
            k_turn_tensor(pe)
            pe.wait_ge(kt_taken, TT)
            gate_tensor(pe)
            c.meet()
            chunk_tensor(pe)
            c.meet()
            sample_tensor(pe)
            c.meet()
            win_tensor(pe)
            c.meet()
            norm_tensor(pe, 4, N, *J["att"])
            norm_tensor(pe, 4, N, *J["ml"])
            c.meet()
            proj_tensor(pe, cat, 8, NB["out"])
            c.meet()
            mem_turn_tensor(pe)
            c.meet()
            norm_tensor(pe, KB, NMEM, *J["mem"])
            c.meet()
            proj_tensor(pe, mem_n, 8, NB["mk"], MCH)
            proj_tensor(pe, mem_n, 8, NB["mv2"], MCH)
            c.meet()
            norm_tensor(pe, KB, N, *J["cross"])
            c.meet()
            proj_tensor(pe, xn, 8, NB["cq"])
            c.meet()
            mkv_turn_tensor(pe)
            c.meet()
            cross_tensor(pe)
            c.meet()
            xsample_tensor(pe)
            c.meet()
            proj_tensor(pe, co, 8, NB["co"])
            c.meet()
            norm_tensor(pe, KB, N, *J["ffn"])
            c.meet()
            ffn_tensor(pe, NB["ffn"])
            c.meet()
            down_tensor(pe)
            c.meet()
            norm_tensor(pe, KB, N, *J["final"])
            c.meet()
            out_tensor(pe)
            c.meet()

        @block.scalar
        def _(act):
            c = chains["act"] = Chain(act, act_step)
            c.meet()
            norm_scalar(act, XT, KB, N, *J["x"])
            c.meet()
            proj_evac(act, aq, 4, NB["aq"], act_copy(HD ** -0.5))
            proj_evac(act, akv, 8, NB["akv"], act_copy())
            c.meet()
            kv_turn_scalar(act)
            c.meet()
            att_scalar(act)
            att_turn_scalar(act)
            c.meet()
            proj_evac(act, qk, 8, NB["qk"], act_copy())
            proj_evac(act, mv, 4, NB["mv"], act_copy())
            proj_evac(act, sig_o, 4, NB["mo"], act_copy())
            c.meet()
            conv_state_scalar(act)
            c.meet()
            conv_scalar(act)
            c.meet()
            gate_scalar(act)
            c.meet()
            chunk_scalar(act, range(NC))
            c.meet()
            chunk_scalar(act, [NC])
            c.meet()
            win_scalar(act)
            c.meet()
            norm_scalar(act, cat, 4, N, *J["att"])
            norm_scalar(act, cat[:, NP:, :], 4, N, *J["ml"])
            c.meet()
            c.meet()
            c.meet()
            norm_scalar(act, mem_T, KB, NMEM, *J["mem"])
            c.meet()
            proj_evac(act, mkT, 8, NB["mk"], act_copy(), MCH)
            proj_evac(act, mvT, 8, NB["mv2"], act_copy(), MCH)
            c.meet()
            norm_scalar(act, XT, KB, N, *J["cross"])
            c.meet()
            proj_evac(act, cq, 8, NB["cq"], act_copy(XD ** -0.5))
            c.meet()
            mkv_turn_scalar(act)
            c.meet()
            cross_scalar(act)
            c.meet()
            xsample_scalar(act)
            c.meet()
            c.meet()
            norm_scalar(act, XT, KB, N, *J["ffn"])
            c.meet()
            cache_copy(act)
            ffn_scalar(act, NB["ffn"])
            c.meet()
            c.meet()
            norm_scalar(act, XT, KB, N, *J["final"])
            c.meet()
            out_scalar(act)
            c.meet()

        @block.vector
        def _(dve):
            c = chains["dve"] = Chain(dve, dve_step)
            turn_vector(dve)
            c.meet()
            norm_vector(dve, XT, xn, KB, N, G_MIX, *J["x"])
            c.meet()
            c.meet()
            c.meet()
            att_vector(dve)
            c.meet()
            nc.vector.memset(gate_w[:, :, :], 0.0).then_inc(gw_zeroed, 1)
            gates_vector(dve)
            c.meet()
            gate_bias_vector(dve)
            c.meet()
            conv_vector(dve)
            c.meet()
            k_turn_vector(dve)
            gate_vector(dve)
            c.meet()
            chunk_vector(dve)
            c.meet()
            sample_vector(dve)
            c.meet()
            win_vector(dve)
            c.meet()
            norm_vector(dve, cat, cat, 4, N, G_ATT, *J["att"])
            norm_vector(dve, cat[:, NP:, :], cat[:, NP:, :], 4, N, G_ML, *J["ml"])
            c.meet()
            proj_evac(dve, XT, 8, NB["out"], add_residual)
            c.meet()
            mem_turn_vector(dve)
            c.meet()
            norm_vector(dve, mem_T, mem_n, KB, NMEM, G_MEM, *J["mem"])
            c.meet()
            c.meet()
            norm_vector(dve, XT, xn, KB, N, G_CROSS, *J["cross"])
            c.meet()
            c.meet()
            c.meet()
            cross_vector(dve)
            c.meet()
            xsample_vector(dve)
            c.meet()
            proj_evac(dve, XT, 8, NB["co"], add_residual)
            c.meet()
            norm_vector(dve, XT, xn, KB, N, G_FFN, *J["ffn"])
            c.meet()
            ffn_vector(dve, NB["ffn"])
            c.meet()
            down_vector(dve)
            c.meet()
            norm_vector(dve, XT, xn, KB, N, G_FINAL, *J["final"])
            c.meet()
            c.meet()

        @block.gpsimd
        def _(pool):
            c = chains["pool"] = Chain(pool, pool_step)
            for name in order:
                if name == "kv":
                    q_wide_pool(pool)
                elif name == "conv_state":
                    conv_state_pool(pool)
                elif name == "chunks":
                    sample_pool(pool)
                    chunk_pool(pool, range(NC))
                elif name == "sample":
                    q_mask_pool(pool)
                    chunk_pool(pool, [NC])
                elif name == "xsample":
                    xsample_pool(pool)
                c.meet()


_INS = ['x_prompt', 'x_sample', 'mem_prompt', 'cache_win_k', 'cache_win_v', 'cache_mem_k', 'cache_mem_v', 'state_conv',
        'state_mlstm_C', 'state_mlstm_n', 'state_mlstm_m', 'g_mix', 'w_in', 'conv_w', 'conv_b', 'b_ig', 'b_fg', 'b_og',
        'g_attn_out', 'g_mlstm_out', 'w_out', 'g_cross', 'g_mem', 'w_cq', 'w_ck', 'w_cv', 'w_co', 'g_ffn', 'w_gate', 'w_up',
        'w_down', 'g_final']
_OUTS = [('y_p', (1, SEQ, D)), ('y_s', (DB, DT, D)), ('win_k_p', (1, SEQ, H, HD)), ('win_v_p', (1, SEQ, H, HD)),
         ('conv_p', (1, 3, D)), ('C_p', (1, H, HD, HD)), ('n_p', (1, H, HD)), ('m_p', (1, H)),
         ('mem_k', (1, NMEM, XH, XD)), ('mem_v', (1, NMEM, XH, XD)), ('win_k_s', (DB, PAST + DT, H, HD)),
         ('win_v_s', (DB, PAST + DT, H, HD)), ('conv_s', (DB, 3, D)), ('C_s', (DB, H, HD, HD)), ('n_s', (DB, H, HD)),
         ('m_s', (DB, H))]


def kernel(**inputs):
    import concourse.bacc as _bacc
    from concourse.bass_utils import run_bass_kernel_spmd as _run

    nc = _bacc.Bacc("TRN2", target_bir_lowering=False, num_devices=1)
    arrays, ins, outs = {}, {}, {}
    given = {name: np.ascontiguousarray(inputs[name]) for name in _INS}
    given.update(constants())
    for name, a in given.items():
        arrays[f"in_{name}_dram"] = a
        ins[name] = nc.dram_tensor(f"in_{name}_dram", a.shape, F32, kind="ExternalInput").ap()
    for name, shape in _OUTS:
        outs[name] = nc.dram_tensor(f"out_{name}_dram", shape, F32, kind="ExternalOutput").ap()
    build(nc, ins, outs)
    r = _run(nc, [arrays], core_ids=[0])
    return tuple(r.results[0][f"out_{name}_dram"] for name, _ in _OUTS)
```

```python
from contextlib import ExitStack

import numpy as np

import concourse.bass as bass
from concourse import mybir

F32 = mybir.dt.float32
F32R = mybir.dt.float32r
ALU = mybir.AluOpType
ACT = mybir.ActivationFunctionType
AX_X = mybir.AxisListType.X

P = 128
D = 1024
KB = D // P
SEQ = 1024
DB, DT = 8, 8
NS = DB * DT
N = SEQ + NS
TT = 9
PAST = 1024
H, HD = 8, 64
NP = H // 2
AW = H * HD
NMEM, XH, XD = 256, 4, 256
FB = 22
FGROUPS = (6, 6, 6, 4)
D_FF = FB * P
EPS = 1e-6
NEG = -1e30
CHUNKS = ((0, 384), (384, 384), (768, 320))
NC = SEQ // P
G_MIX, G_CROSS, G_MEM, G_FFN, G_FINAL = 0, 8, 16, 24, 32
G_ATT, G_ML, CONV_W, CONV_B, B_OG, N_PAR = 40, 44, 48, 80, 88, 92


def constants():
    slopes = np.exp2(-8.0 * (np.arange(H) + 1.0) / H)

    def bias(delta):
        count = ((delta <= 128).astype(int) + ((delta <= 512) & (delta % 4 == 0))
                 + ((delta <= 2048) & (delta % 16 == 0))) * (delta >= 0)
        log_count = np.where(count > 0, np.log(np.maximum(count, 1)), 0.0)
        return [np.where(count > 0, -s * delta + log_count, NEG) for s in slopes]

    delta = np.arange(P)[:, None] + (SEQ - P) - np.arange(SEQ)[None]
    prompt_bias = np.stack(bias(delta))
    t = np.arange(DT)
    cache = np.stack(bias(PAST + t[:, None] - np.arange(PAST)[None])).reshape(AW // DT, PAST)
    new = np.stack(bias(t[:, None] - t[None])).reshape(H * DT, DT)
    sample_new = np.full((2, H * DT, DB // 2, DB, DT), NEG)
    for pair in range(DB // 2):
        for e in range(2):
            sample_new[e, :, pair, 2 * pair + e] = new
    s = np.arange(P)
    causal = np.where(s[:, None] <= s[None], 0.0, NEG)
    r = np.arange(NS)
    sample_causal = np.where((r[:, None] <= r[None]) & (r[:, None] // DT == r[None] // DT), 0.0, NEG)
    restart = np.ones((H, N))
    restart[:, 0:SEQ:P] = 0
    restart[:, SEQ::DT] = 0
    head = np.arange(H)
    c = {
        "ident": np.eye(P),
        "prompt_bias": prompt_bias,
        "sample_bias": np.concatenate([cache, cache]),
        "sample_new_bias": sample_new.reshape(P, DB // 2 * NS),
        "causal": causal,
        "sample_causal": sample_causal,
        "restart": restart,
        "head_sel": np.repeat(np.eye(H), P, axis=1),
        "pair_sel": (head[:, None] == (2 * np.arange(NP)[:, None] + np.arange(P)[None] // HD).reshape(1, -1)),
        "batch_sel": r[:, None] // DT == np.arange(DB)[None],
    }
    return {k: np.ascontiguousarray(v, dtype=np.float32) for k, v in c.items()}


def build(nc, A, O):
    with ExitStack() as ctx:
        def sem(name):
            return ctx.enter_context(nc.semaphore(name))

        PS = ctx.enter_context(nc.psum_tensor("psum", [P, 8, 512], F32))

        BASE = 16512
        AT = {"ident": 0, "ones": 128, "params_T": 256, "eps": 352, "small": 360, "sample_q_wide": 512,
              "sample_k_new": 2560, "sample_v_new": 2816, "scratch": 3328, "weights": 7680, "x_hi": 13824, "x_lo": 22528,
              "wide": 31232, "end": 52992}

        def sb(name, *shape, at=None, dt=F32):
            at = AT[name] if at is None else at
            return nc.alloc_sbuf_tensor_at(name, list(shape), dt, offset=BASE + 4 * at)

        HB = sb("wide", P, AT["end"] - AT["wide"])
        XT0 = sb("residual_T_first", P, KB * N, at=AT["wide"])
        BIG = KB * N
        XTF = sb("residual_T", P, KB * N, at=AT["wide"] + BIG + 4352)
        XHI, XLO = (sb(n, P, KB * N, dt=F32R) for n in ("x_hi", "x_lo"))
        XN = sb("work_1", P, KB * N, at=AT["x_hi"])
        XW = sb("work_2", P, KB * N, at=AT["x_lo"])
        WRT = sb("weights_work", P, 6144, at=AT["weights"])
        RAW = sb("weights_raw", P, 2 * KB * P, at=AT["weights"])
        WHI = sb("weights_hi", P, 2 * KB * P, at=AT["weights"] + 2 * KB * P, dt=F32R)
        WLO = sb("weights_lo", P, 2 * KB * P, at=AT["weights"] + 4 * KB * P, dt=F32R)
        GHI = sb("hidden_hi", P, 6 * N, at=AT["wide"], dt=F32R)
        GLO = sb("hidden_lo", P, 6 * N, at=AT["wide"] + 6 * N, dt=F32R)
        SC = sb("scratch", P, 4352)
        IDENT = sb("ident", P, P)
        ONES = sb("ones", P, P)
        PAR = sb("params_T", P, N_PAR)
        EPSC = sb("eps", P, 1)
        QX = sb("sample_q_wide", P, NP, DB, NS)
        KNEW = sb("sample_k_new", P, NP, NS)
        VNEW = sb("sample_v_new", NS, AW)
        SMALL = sb("small", P, 96)
        XT_DRAM = nc.dram_tensor("residual_T_dram", [P, KB * N], F32, kind="Internal").ap()

        def cut(t, start, *shape):
            n = int(np.prod(shape))
            v = t[:, start:start + n]
            if len(shape) == 2:
                return v.rearrange("p (a b) -> p a b", b=shape[1])
            if len(shape) == 3:
                return v.rearrange("p (a b c) -> p a b c", b=shape[1], c=shape[2])
            return v

        XT = cut(XTF, 0, KB, N)
        x0 = cut(XT0, 0, KB, N)
        xn = cut(XN, 0, KB, N)
        xhi, xlo = cut(XHI, 0, KB, N), cut(XLO, 0, KB, N)
        cat = cut(HB, 0, KB, N)
        raw = cut(RAW, 0, 2, KB, P)
        whi, wlo = cut(WHI, 0, 2, KB, P), cut(WLO, 0, 2, KB, P)
        ghi, glo = cut(GHI, 0, 6, N), cut(GLO, 0, 6, N)
        nsq = cut(SC, 0, 2, N)
        nacc = cut(SC, 2 * N, N)
        nr = cut(SC, 3 * N, N)
        silu_g = cut(SC, 0, 2, N)

        phase_done = sem("phase_done")
        act_step, dve_step, pool_step = sem("act_step"), sem("dve_step"), sem("pool_step")
        w_landed = [sem(f"w_landed{i}") for i in range(2)]
        w_high, w_split = sem("w_high"), sem("w_split")
        n_high, n_half, n_low = sem("norm_high"), sem("norm_product"), sem("norm_low")
        z_ready, z_taken = sem("z_ready"), sem("z_taken")
        sq_ready, sq_summed, sum_ready, bcast_ready, rnorm_ready, norm_done = (
            sem("sq_ready"), sem("sq_summed"), sem("sum_ready"), sem("bcast_ready"), sem("rnorm_ready"),
            sem("norm_done"))
        x_landed, par_landed, x_turned, x_taken = sem("x_landed"), sem("par_landed"), sem("x_turned"), sem("x_taken")
        out_stored = sem("out_stored")
        stores = [0]

        def stored(ins):
            ins.then_inc(out_stored, 16)
            stores[0] += 1

        class Chain:

            def __init__(self, eng, s):
                self.eng, self.sem, self.n, self.phase = eng, s, 0, 0

            def __call__(self, ins):
                self.n += 1
                ins.then_inc(self.sem, 1)
                self.eng.wait_ge(self.sem, self.n)

            def meet(self):
                self.phase += 1
                self.eng.drain().then_inc(phase_done, 1)
                self.eng.wait_ge(phase_done, 4 * self.phase)

        def w_view(w, c0=0, r0=0, nk=KB):
            return w[r0:r0 + nk * P, :].rearrange("(k p) n -> p k n", p=P)[:, :, c0:]

        def proj_load(sp, views, blocks, n0, nk=KB):
            m = len(views)

            def block(i, s):
                c = i * 2 + s if m == 1 else i
                sp.dma_start(raw[:, s, 0:nk], views[s % m][:, :, bass.ds(c * P, P)]).then_inc(w_landed[s], 16)
            if n0 == 0:
                block(0, 0)
                block(0, 1)
            with sp.Fori(1 if n0 == 0 else 0, blocks // 2) as i:
                for s in range(2):
                    sp.wait_ge(w_split, i * 2 + (n0 + s - 1))
                    block(i, s)

        def split_block(dve, i, s, n0, nk, first=False):
            dve.wait_ge(w_landed[s], i * 16 + (16 * (n0 // 2) + 16))
            if not first:
                dve.wait_ge(z_ready, i * 2 + (n0 + s - 1))
            nc.vector.tensor_copy(whi[:, s, 0:nk, :], raw[:, s, 0:nk, :]).then_inc(w_high, 1)
            dve.wait_ge(w_high, i * 2 + (n0 + s + 1))
            nc.vector.tensor_tensor(wlo[:, s, 0:nk, :], raw[:, s, 0:nk, :], whi[:, s, 0:nk, :].bitcast(F32), ALU.subtract)\
                .then_inc(w_split, 1)

        def proj_split(dve, blocks, n0):
            if n0 == 0:
                split_block(dve, 0, 0, n0, KB, True)
                split_block(dve, 0, 1, n0, KB, True)
            with dve.Fori(1 if n0 == 0 else 0, blocks // 2) as i:
                split_block(dve, i, 0, n0, KB)
                split_block(dve, i, 1, n0, KB)

        def proj_split_add(dve, dst, blocks, n0, nk=KB):
            def add(i, s):
                dve.wait_ge(z_ready, i * 2 + (n0 + s + 1))
                for c, (t0, w) in enumerate(CHUNKS):
                    out = dst[:, bass.ds(i * 2 + s, 1), t0:t0 + w]
                    last = nc.vector.tensor_tensor(out, PS[:, 3 * s + c:3 * s + c + 1, 0:w], out, ALU.add)
                last.then_inc(z_taken, 1)
            split_block(dve, 0, 0, n0, nk)
            split_block(dve, 0, 1, n0, nk)
            with dve.Fori(0, blocks // 2 - 1) as i:
                for s in range(2):
                    split_block(dve, i, s, n0 + 2, nk)
                    add(i, s)
            add(blocks // 2 - 1, 0)
            add(blocks // 2 - 1, 1)

        def products(s, x, nk, chunks):
            for k in range(nk):
                for w, part in ((whi, 0), (whi, 1), (wlo, 0)):
                    for c, (t0, n) in enumerate(chunks):
                        mm = nc.tensor.matmul(PS[:, 3 * s + c, 0:n], w[:, s, k], x[part][:, k, t0:t0 + n],
                                              start=(k == 0 and w is whi and part == 0), stop=(k == nk - 1 and w is wlo))
            return mm

        def proj_tensor(pe, x, blocks, n0, chunks=CHUNKS, nk=KB, ffn_blocks=0):
            def block(i, s, first):
                pe.wait_ge(w_split, i * 2 + (n0 + s + 1))
                if not first:
                    pe.wait_ge(z_taken, i * 2 + (n0 - ffn_blocks + s - 1))
                products(s, x, nk, chunks).then_inc(z_ready, 1)
            if n0 == 0:
                block(0, 0, True)
                block(0, 1, True)
            with pe.Fori(1 if n0 == 0 else 0, blocks // 2) as i:
                block(i, 0, False)
                block(i, 1, False)

        def proj_evac(eng, dst, blocks, n0, put, chunks=CHUNKS):
            with eng.Fori(0, blocks // 2) as i:
                for s in range(2):
                    eng.wait_ge(z_ready, i * 2 + (n0 + s + 1))
                    for c, (t0, w) in enumerate(chunks):
                        last = put(dst[:, bass.ds(i * 2 + s, 1), t0:t0 + w], PS[:, 3 * s + c:3 * s + c + 1, 0:w])
                    last.then_inc(z_taken, 1)

        def act_copy(scale=1.0):
            return lambda out, ps: nc.scalar.activation(out, ps, ACT.Copy, scale=scale)

        def norm_scalar(act, src, hi, nb, cols, j0, r0, s0):
            if r0:
                act.wait_ge(norm_done, r0)
            for k in range(nb):
                if j0 + k >= 2:
                    act.wait_ge(sq_summed, j0 + k - 1)
                nc.scalar.activation(nsq[:, (j0 + k) % 2, 0:cols], src[:, k, 0:cols], ACT.Square).then_inc(sq_ready, 1)
            act.wait_ge(bcast_ready, r0 + 1)
            chain = chains["act"]
            for c, (t0, w) in enumerate(CHUNKS):
                w = min(w, cols - t0)
                if w > 0:
                    last = nc.scalar.activation(nr[:, t0:t0 + w], PS[:, c, 0:w], ACT.Ln, bias=EPSC[:, 0:1],
                                                scale=1.0 / (nb * P))
            chain(last)
            nc.scalar.activation(nr[:, 0:cols], nr[:, 0:cols], ACT.Exp, scale=-0.5).then_inc(rnorm_ready, 1)
            if hi is not None:
                for k in range(nb):
                    act.wait_ge(n_half, s0 + k + 1)
                    nc.scalar.activation(hi[:, k, 0:cols], nsq[:, k % 2, 0:cols], ACT.Copy).then_inc(n_high, 1)

        def norm_vector(dve, src, dst, nb, cols, gain, j0, r0, s0):
            for k in range(nb):
                dve.wait_ge(sq_ready, j0 + k + 1)
                if k:
                    dve.wait_ge(sq_summed, j0 + k)
                    nc.vector.tensor_tensor(nacc[:, 0:cols], nacc[:, 0:cols], nsq[:, (j0 + k) % 2, 0:cols],
                                            ALU.add).then_inc(sq_summed, 1)
                else:
                    nc.vector.tensor_copy(nacc[:, 0:cols], nsq[:, (j0 + k) % 2, 0:cols]).then_inc(sq_summed, 1)
            dve.wait_ge(rnorm_ready, r0 + 1)

            def scaled(k, out):
                return nc.vector.scalar_tensor_tensor(out=out, in0=src[:, k, 0:cols], scalar=PAR[:, gain + k:gain + k + 1],
                                                      in1=nr[:, 0:cols], op0=ALU.mult, op1=ALU.mult)
            if not isinstance(dst, tuple):
                for k in range(nb):
                    last = scaled(k, dst[:, k, 0:cols])
                last.then_inc(norm_done, 1)
                return
            hi, lo = dst
            dve.wait_ge(sq_summed, j0 + nb)
            for k in range(nb + 1):
                if k < nb:
                    if k >= 2:
                        dve.wait_ge(n_low, s0 + k - 1)
                    scaled(k, nsq[:, k % 2, 0:cols]).then_inc(n_half, 1)
                if k:
                    dve.wait_ge(n_high, s0 + k)
                    nc.vector.tensor_tensor(lo[:, k - 1, 0:cols], nsq[:, (k - 1) % 2, 0:cols], hi[:, k - 1, 0:cols].bitcast(F32),
                                            ALU.subtract).then_inc(n_low, 1)
            dve.wait_ge(n_low, s0 + nb)
            nc.vector.memset(SMALL[:, 41:42], 0.0).then_inc(norm_done, 1)

        def norm_tensor(pe, nb, cols, j0, r0, s0):
            pe.wait_ge(sq_summed, j0 + nb)
            if r0:
                pe.wait_ge(rnorm_ready, r0)
            for c, (t0, w) in enumerate(CHUNKS):
                w = min(w, cols - t0)
                if w > 0:
                    mm = nc.tensor.matmul(PS[:, c, 0:w], ONES[:, :], nacc[:, t0:t0 + w], start=True, stop=True)
            mm.then_inc(bcast_ready, 1)

        xs = cut(HB, BIG, TT, D)
        par_rows = cut(SC, 0, P)

        def load_inputs(sp):
            row = lambda a: a.rearrange("(k p) -> k p", p=P)
            for a, r, n in (("g_mix", G_MIX, 8), ("g_cross", G_CROSS, 8), ("g_mem", G_MEM, 8), ("g_ffn", G_FFN, 8),
                            ("g_final", G_FINAL, 8), ("g_attn_out", G_ATT, 4), ("g_mlstm_out", G_ML, 4),
                            ("conv_b", CONV_B, 8), ("b_og", B_OG, 4)):
                sp.dma_start(par_rows[r:r + n, :], row(A[a])).then_inc(par_landed, 16)
            sp.dma_start(par_rows[CONV_W:CONV_W + 32, :], A["conv_w"].rearrange("j (k p) -> (j k) p", p=P)).then_inc(par_landed, 16)
            sp.dma_start(IDENT[:, :], A["ident"]).then_inc(par_landed, 16)
            xp = A["x_prompt"][0].rearrange("(t p) d -> p t d", p=P)
            for t in range(TT - 1):
                sp.dma_start(xs[:, t, :], xp[:, t, :]).then_inc(x_landed, 16)
            sp.dma_start(xs[0:NS, TT - 1, :], A["x_sample"].rearrange("b t d -> (b t) d")).then_inc(x_landed, 16)

        def turn_tensor(pe):
            pe.wait_ge(par_landed, 16 * 11)
            nc.tensor.transpose(PS[:, 4, 0:N_PAR], par_rows[0:N_PAR, :], IDENT[0:N_PAR, 0:N_PAR]).then_inc(x_turned, 1)
            pe.wait_ge(x_landed, 16 * TT)
            for g in range(2 * TT):
                t, half = g // 2, g % 2
                n = P if t < TT - 1 else NS
                if g >= 4:
                    pe.wait_ge(x_taken, g - 2)
                for j in range(4):
                    mm = nc.tensor.transpose(PS[:, g % 4, j * P:j * P + n], xs[0:n, t, (4 * half + j) * P:(4 * half + j + 1) * P],
                                             IDENT[0:n, 0:n])
                mm.then_inc(x_turned, 1)

        def turn_vector(dve):
            chains["dve"](nc.vector.memset(EPSC[:, :], EPS))
            nc.vector.memset(ONES[:, :], 1.0)
            dve.wait_ge(x_turned, 1)
            nc.vector.tensor_copy(PAR[:, :], PS[:, 4, 0:N_PAR]).then_inc(x_taken, 1)
            for g in range(2 * TT):
                t, half = g // 2, g % 2
                n = P if t < TT - 1 else NS
                dve.wait_ge(x_turned, g + 2)
                nc.vector.tensor_copy(x0[:, 4 * half:4 * half + 4, t * P:t * P + n],
                                      PS[:, g % 4, :].rearrange("p (j n) -> p j n", j=4)[:, :, 0:n]).then_inc(x_taken, 1)

        aq, ak, av = (cut(HB, BIG + j * NP * N, NP, N) for j in range(3))
        akv = cut(HB, BIG + NP * N, 2 * NP, N)
        vtok = cut(HB, NP * N, TT - 1, AW)
        xt_stored, xt_back = sem("xt_stored"), sem("xt_back")
        AW0 = BIG + 2 * NP * N
        att_tok = cut(HB, AW0, NC, AW)
        bias_tab = cut(WRT, 4096, 2, SEQ)
        logit = cut(SC, 0, 3, SEQ)
        prob_T = cut(SC, 3 * SEQ, SEQ), cut(WRT, 2048, SEQ)
        k_stage = cut(WRT, 0, 4, AW)
        kv_turned, kv_taken, q_wide = sem("kv_turned"), sem("kv_taken"), sem("q_wide")
        k_stored = [sem(f"k_stored{i}") for i in range(4)]

        def kv_turn_tensor(pe):
            for g in range(2 * TT):
                t, which = g // 2, g % 2
                n = P if t < TT - 1 else NS
                if g >= 4:
                    pe.wait_ge(kv_taken, g - 3)
                for j in range(NP):
                    mm = nc.tensor.transpose(PS[0:n, g % 4, j * P:(j + 1) * P], akv[:, NP * which + j, t * P:t * P + n], IDENT[:, :])
                mm.then_inc(kv_turned, 1)

        def kv_turn_scalar(act):
            act.wait_ge(xt_stored, 16)
            for g in range(2 * TT):
                t, which = g // 2, g % 2
                n = P if t < TT - 1 else NS
                act.wait_ge(kv_turned, g + 1)
                if which == 0:
                    if t >= 4:
                        act.wait_ge(k_stored[t % 4], 16 * (t // 4))
                    out = k_stage[0:n, t % 4, :]
                else:
                    out = vtok[:, t, :] if t < TT - 1 else VNEW[:, :]
                nc.scalar.activation(out, PS[0:n, g % 4, :], ACT.Copy).then_inc(kv_taken, 1)

        def kv_store(sp):
            wk, wv = (O[n][0].rearrange("(t p) h d -> p t (h d)", p=P) for n in ("win_k_p", "win_v_p"))
            for t in range(TT):
                sp.wait_ge(kv_taken, 2 * t + 1)
                if t < TT - 1:
                    sp.dma_start(wk[:, t, :], k_stage[:, t % 4, :]).then_inc(k_stored[t % 4], 16)
                    sp.wait_ge(kv_taken, 2 * t + 2)
                    stored(sp.dma_start(wv[:, t, :], vtok[:, t, :]))
                else:
                    sp.wait_ge(kv_taken, 2 * t + 2)
                    for b in range(DB):
                        rows = slice(b * DT, (b + 1) * DT)
                        sp.dma_start(O["win_k_s"][b, PAST:PAST + DT].rearrange("t h d -> t (h d)"),
                                     k_stage[rows, t % 4, :]).then_inc(k_stored[t % 4], 16)
                        stored(sp.dma_start(O["win_v_s"][b, PAST:PAST + DT].rearrange("t h d -> t (h d)"), VNEW[rows, :]))
            for i in range(4):
                sp.wait_ge(k_stored[i], 16 * (len(range(i, TT - 1, 4)) + (DB if i == (TT - 1) % 4 else 0)))

        def q_wide_pool(pool):
            chains["pool"](nc.gpsimd.memset(QX[:, :, :, :], 0.0))
            for e in range(2):
                rows = slice(HD * e, HD * e + HD)
                for p in range(NP):
                    h = 2 * p + e
                    chains["pool"](nc.gpsimd.tensor_copy(QX[rows, p, :, h * DT:(h + 1) * DT],
                                                         aq[rows, p, SEQ:N].rearrange("p (b t) -> p b t", t=DT)))
            nc.gpsimd.tensor_copy(KNEW[:, :, :], ak[:, :, SEQ:N])

        tab_landed = [sem(f"tab_landed{i}") for i in range(2)]
        s_ready, logit_ready, prob_ready, pt_ready, pt_taken, o_ready, o_taken = (
            sem("s_ready"), sem("logit_ready"), sem("prob_ready"), sem("pt_ready"),
            sem("pt_taken"), sem("o_ready"), sem("o_taken"))
        UNITS = [(h, qb) for h in range(H) for qb in range(NC)]
        GROUPS = [(u, g) for u, (h, qb) in enumerate(UNITS) for g in range((qb + 4) // 4)]
        after = {u: sum(1 for v, _ in GROUPS if v <= u) for u in range(len(UNITS))}

        def att_load(sp):
            for h in range(H):
                if h >= 2:
                    sp.wait_ge(logit_ready, (h - 1) * NC)
                sp.dma_start(bias_tab[:, h % 2, :], A["prompt_bias"][h]).then_inc(tab_landed[h % 2], 16)

        def att_tensor(pe):
            def scores(u):
                h, qb = UNITS[u]
                rows = slice(HD * (h % 2), HD * (h % 2) + HD)
                if u >= 2:
                    pe.wait_ge(logit_ready, u - 1)
                for g in range((qb + 4) // 4):
                    w = min(4, qb + 1 - 4 * g) * P
                    mm = nc.tensor.matmul(PS[:, 2 * (u % 2) + g, 0:w], aq[rows, h // 2, qb * P:(qb + 1) * P],
                                          ak[rows, h // 2, 512 * g:512 * g + w], start=True, stop=True)
                mm.then_inc(s_ready, 1)

            def turn(u):
                h, qb = UNITS[u]
                pe.wait_ge(prob_ready, u + 1)
                for g in range((qb + 4) // 4):
                    n = after[u - 1] + g if u else g
                    if n >= 2:
                        pe.wait_ge(pt_taken, n - 1)
                    for j in range(min(4, qb + 1 - 4 * g)):
                        mm = nc.tensor.transpose(PS[:, 4 + n % 2, j * P:(j + 1) * P],
                                                 logit[:, u % 3, (4 * g + j) * P:(4 * g + j + 1) * P], IDENT[:, :])
                    mm.then_inc(pt_ready, 1)

            def values(u):
                h, qb = UNITS[u]
                pe.wait_ge(pt_taken, after[u])
                if u >= 2:
                    pe.wait_ge(o_taken, u - 1)
                for j in range(qb + 1):
                    mm = nc.tensor.matmul(PS[:, 6 + u % 2, 0:HD], prob_T[u % 2][:, j * P:(j + 1) * P],
                                          vtok[:, j, h * HD:(h + 1) * HD], start=(j == 0), stop=(j == qb))
                mm.then_inc(o_ready, 1)

            for u in range(len(UNITS) + 2):
                if u < len(UNITS):
                    scores(u)
                if 1 <= u <= len(UNITS):
                    turn(u - 1)
                if u >= 2:
                    values(u - 2)

        amax, asum, arec, negm = (SMALL[:, 4 * i:4 * i + 4] for i in range(4))

        def att_vector(dve):
            def finish(u):
                h, qb = UNITS[u]
                i = u % 4
                dve.wait_ge(prob_ready, u + 1)
                chains["dve"](nc.vector.reciprocal(arec[:, i:i + 1], asum[:, i:i + 1]))
                dve.wait_ge(o_ready, u + 1)
                nc.vector.tensor_scalar(att_tok[:, qb, h * HD:(h + 1) * HD], PS[:, 6 + u % 2, 0:HD],
                                        arec[:, i:i + 1], None, ALU.mult).then_inc(o_taken, 1)
            for u, (h, qb) in enumerate(UNITS):
                w, i = (qb + 1) * P, u % 4
                dve.wait_ge(s_ready, u + 1)
                dve.wait_ge(tab_landed[h % 2], 16 * (h // 2 + 1))
                if u >= 3:
                    dve.wait_ge(pt_ready, after[u - 3])
                chains["dve"](nc.vector.tensor_tensor_reduce(
                    logit[:, u % 3, 0:w], PS[:, 2 * (u % 2):2 * (u % 2) + 2, :].rearrange("p a b -> p (a b)")[:, 0:w],
                    bias_tab[:, h % 2, SEQ - w:SEQ], 1.0, 3 * NEG, ALU.add, ALU.max, amax[:, i:i + 1]))
                nc.vector.tensor_scalar(negm[:, i:i + 1], amax[:, i:i + 1], -1.0, None, ALU.mult).then_inc(logit_ready, 1)
                if u >= 2:
                    finish(u - 2)
            finish(len(UNITS) - 2)
            finish(len(UNITS) - 1)

        def att_scalar(act):
            def take(u):
                h, qb = UNITS[u]
                for g in range((qb + 4) // 4):
                    n = after[u - 1] + g if u else g
                    w = min(4, qb + 1 - 4 * g) * P
                    act.wait_ge(pt_ready, n + 1)
                    if g == 0 and u >= 2:
                        act.wait_ge(o_ready, u - 1)
                    nc.scalar.activation(prob_T[u % 2][:, 512 * g:512 * g + w], PS[:, 4 + n % 2, 0:w], ACT.Copy).then_inc(pt_taken, 1)
            for u, (h, qb) in enumerate(UNITS):
                w, i = (qb + 1) * P, u % 4
                act.wait_ge(logit_ready, u + 1)
                if u >= 4:
                    act.wait_ge(o_taken, u - 3)
                nc.scalar.activation(logit[:, u % 3, 0:w], logit[:, u % 3, 0:w], ACT.Exp, bias=negm[:, i:i + 1],
                                     accum_out=asum[:, i:i + 1]).then_inc(prob_ready, 1)
                if u >= 1:
                    take(u - 1)
            take(len(UNITS) - 1)

        at_turned, at_taken = sem("at_turned"), sem("at_taken")

        def att_turn_tensor(pe):
            for t in range(NC):
                if t >= 4:
                    pe.wait_ge(at_taken, t - 3)
                for j in range(NP):
                    mm = nc.tensor.transpose(PS[:, t % 4, j * P:(j + 1) * P], att_tok[:, t, j * P:(j + 1) * P], IDENT[:, :])
                mm.then_inc(at_turned, 1)

        def att_turn_scalar(act):
            for t in range(NC):
                act.wait_ge(at_turned, t + 1)
                nc.scalar.activation(cat[:, 0:NP, t * P:(t + 1) * P], PS[:, t % 4, :].rearrange("p (j n) -> p j n", j=NP),
                                     ACT.Copy).then_inc(at_taken, 1)

        qk = cut(HB, BIG, 2 * NP, N)
        mv = cut(HB, BIG + 2 * NP * N, NP, N)
        sig_o = cat[:, NP:2 * NP, :]
        V1W = HD + 1
        v1 = cut(XN, 0, TT, H * V1W)
        ML0 = TT * H * V1W
        head_sel = cut(XN, ML0, H, P)
        pair_sel = cut(XN, ML0 + 1024, NP, P)
        causal = cut(XN, ML0 + 1536, P)
        sample_causal = cut(XN, ML0 + 1664, NS)
        restart = cut(XN, ML0 + 1728, N)
        batch_sel = cut(XN, ML0 + 2816, DB)
        cols = cut(XN, ML0 + 2824, TT, 4, H)
        colx = cut(XN, ML0 + 3112, TT, 3, H)
        dec = cut(XN, ML0 + 3328, NP, NC + DB)
        bgate = cut(XN, ML0 + 3392, 2)
        wgate = cut(XN, ML0 + 3400, 1)
        mrow = cut(XN, ML0 + 3404, NC + DB)
        dkrow = cut(XN, ML0 + 3420, NC + DB)
        m_out = cut(XN, ML0 + 3436, DB + 1)
        ktok = cut(XW, 0, TT, AW)
        gate_w = cut(SC, 0, KB, P)
        g_raw = [cut(SC, 1024 + j * N, N) for j in range(2)]
        gb, gm, gw = (cut(SC, j * N, N) for j in range(3))
        gu = cut(XW, TT * AW, N)
        rows4 = cut(WRT, 0, N)
        gi, gf = cut(WRT, N, N), cut(WRT, 2 * N, N)
        conv_acc = cut(XW, 2048, 2, N)
        conv_x = cut(XW, 0, KB, DB, 11)
        state_rows = cut(XW, 704, D)
        mrows_stage = cut(WRT, 0, D)

        gw_landed, gate_ready, ml_landed, gate_rows = sem("gw_landed"), sem("gate_ready"), sem("ml_landed"), sem("gate_rows")

        def ml_loads(sp):
            sp.wait_ge(phase_done, 4 * PH["att"])
            sp.wait_ge(gw_zeroed, 1)
            wv = w_view(A["w_in"])
            with nc.allow_non_contiguous_dma(reason="sixteen gate columns"):
                sp.dma_start(gate_w[:, :, 0:8], wv[:, :, 3584:3592]).then_inc(gw_landed, 16)
                sp.dma_start(gate_w[:, :, 32:40], wv[:, :, 3592:3600]).then_inc(gw_landed, 16)

        def ml_tables(sp):
            sp.wait_ge(phase_done, 4 * PH["ml_proj"])
            with nc.allow_non_contiguous_dma(reason="small tables and columns"):
                for dst, src in ((head_sel[0:H].rearrange("p a b -> p (a b)"), A["head_sel"]),
                                 (pair_sel[0:H].rearrange("p a b -> p (a b)"), A["pair_sel"]),
                                 (causal, A["causal"]), (sample_causal[0:NS], A["sample_causal"]),
                                 (restart[0:H], A["restart"]), (batch_sel[0:NS], A["batch_sel"]),
                                 (bgate[0:H, 0:1], A["b_ig"].rearrange("(a b) -> a b", b=1)),
                                 (bgate[0:H, 1:2], A["b_fg"].rearrange("(a b) -> a b", b=1)),
                                 (mrow[0:H, NC:NC + DB], A["state_mlstm_m"].rearrange("b h -> h b")),
                                 (state_rows[0:DB * 3], A["state_conv"].rearrange("b j c -> (b j) c"))):
                    sp.dma_start(dst, src).then_inc(ml_landed, 16)

        gw_zeroed, gw_high, gw_split = sem("gw_zeroed"), sem("gw_high"), sem("gw_split")

        def gates_split(dve):
            dve.wait_ge(gw_landed, 32)
            nc.vector.tensor_copy(whi[:, 0], gate_w).then_inc(gw_high, 1)
            dve.wait_ge(gw_high, 1)
            nc.vector.tensor_tensor(wlo[:, 0], gate_w, whi[:, 0].bitcast(F32), ALU.subtract).then_inc(gw_split, 1)

        def gates_tensor(pe):
            pe.wait_ge(gw_split, 1)
            products(0, (xhi, xlo), KB, CHUNKS).then_inc(gate_ready, 1)

        def gates_vector(dve):
            dve.wait_ge(gate_ready, 1)
            for c, (t0, w) in enumerate(CHUNKS):
                nc.vector.tensor_copy(g_raw[0][0:H, t0:t0 + w], PS[0:H, c, 0:w])
                last = nc.vector.tensor_copy(g_raw[1][0:H, t0:t0 + w], PS[32:32 + H, c, 0:w])
            last.then_inc(gates_read, 1)

        gates_read = sem("gates_read")

        def gate_bias_vector(dve):
            dve.wait_ge(ml_landed, 160)
            for j, g in enumerate((gi, gf)):
                nc.vector.tensor_scalar(g[0:H], g_raw[j][0:H], bgate[0:H, j:j + 1], None, ALU.add)

        ct_turned, ct_taken = sem("ct_turned"), sem("ct_taken")

        def conv_state_tensor(pe):
            pe.wait_ge(ml_landed, 160)
            for g in range(TT + 3):
                if g >= 4:
                    pe.wait_ge(ct_taken, g - 3)
                n = P if g != TT - 1 else NS
                for j in range(NP):
                    if g < TT:
                        mm = nc.tensor.transpose(PS[0:n, g % 4, j * P:(j + 1) * P], mv[:, j, g * P:g * P + n], IDENT[:, :])
                    elif g < TT + 2:
                        mm = nc.tensor.transpose(PS[:, g % 4, j * P:(j + 1) * P], qk[:, 4 * (g - TT) + j, N - P:N], IDENT[:, :])
                    else:
                        for i in (j, j + 4):
                            mm = nc.tensor.transpose(PS[:, g % 4, i * 24:(i + 1) * 24], state_rows[0:24, i * P:(i + 1) * P],
                                                     IDENT[0:24, 0:24])
                mm.then_inc(ct_turned, 1)

        def conv_state_scalar(act):
            for k in range(NP):
                nc.scalar.activation(sig_o[:, k, :], sig_o[:, k, :], ACT.Sigmoid, bias=PAR[:, B_OG + k:B_OG + k + 1])
            for g in range(TT + 3):
                n = P if g != TT - 1 else NS
                act.wait_ge(ct_turned, g + 1)
                if g < TT:
                    last = nc.scalar.activation(v1[0:n, g, :].rearrange("p (h d) -> p h d", h=H)[:, :, 0:HD],
                                                PS[0:n, g % 4, :].rearrange("p (h d) -> p h d", h=H), ACT.Copy)
                elif g < TT + 2:
                    last = nc.scalar.activation(mrows_stage[:, 512 * (g - TT):512 * (g - TT) + 512], PS[:, g % 4, :], ACT.Copy)
                else:
                    last = nc.scalar.activation(conv_x[:, :, :, 0:3],
                                                PS[:, g % 4, 0:192].rearrange("p (k b j) -> p k b j", k=KB, b=DB), ACT.Copy)
                last.then_inc(ct_taken, 1)

        def conv_state_pool(pool):
            nc.gpsimd.memset(v1[:, :, :].rearrange("p t (h d) -> p (t h) d", h=H)[:, :, HD:V1W], 1.0)
            nc.gpsimd.tensor_copy(conv_x[:, :, :, 3:11], qk[:, :, SEQ:N].rearrange("p k (b t) -> p k b t", t=DT))

        def conv_store(sp):
            sp.wait_ge(ct_taken, TT + 2)
            first = P - NS - 3
            stored(sp.dma_start(O["conv_p"][0], mrows_stage[first:first + 3, :]))
            for b in range(DB):
                r = P - NS + b * DT + DT - 3
                stored(sp.dma_start(O["conv_s"][b], mrows_stage[r:r + 3, :]))
            mark["conv_rows"] = stores[0]

        mark = {}

        conv_ready, conv_used, scan_ready = sem("conv_ready"), sem("conv_used"), sem("scan_ready")

        def conv_vector(dve):
            chain = chains["dve"]
            for k in range(2 * NP):
                if k >= 2:
                    dve.wait_ge(conv_used, k - 1)
                acc = conv_acc[:, k % 2, :]
                w = [PAR[:, CONV_W + 8 * j + k:CONV_W + 8 * j + k + 1] for j in range(4)]
                sacc = acc[:, SEQ:N].rearrange("p (b t) -> p b t", t=DT)
                nc.vector.tensor_scalar(acc[:, 0:SEQ], qk[:, k, 0:SEQ], w[3], PAR[:, CONV_B + k:CONV_B + k + 1], ALU.mult, ALU.add)
                chain(nc.vector.tensor_scalar(sacc, conv_x[:, k, :, 3:11], w[3], PAR[:, CONV_B + k:CONV_B + k + 1], ALU.mult, ALU.add))
                for j in (2, 1, 0):
                    s = 3 - j
                    nc.vector.scalar_tensor_tensor(out=acc[:, s:SEQ], in0=qk[:, k, 0:SEQ - s], scalar=w[j], in1=acc[:, s:SEQ],
                                                   op0=ALU.mult, op1=ALU.add)
                    last = nc.vector.scalar_tensor_tensor(out=sacc, in0=conv_x[:, k, :, j:j + DT], scalar=w[j], in1=sacc,
                                                          op0=ALU.mult, op1=ALU.add)
                    if j:
                        chain(last)
                last.then_inc(conv_ready, 1)

        def conv_scalar(act):
            for k in range(2 * NP):
                act.wait_ge(conv_ready, k + 1)
                nc.scalar.activation(qk[:, k, :], conv_acc[:, k % 2, :], ACT.Silu).then_inc(conv_used, 1)

        kt_turned, kt_taken = sem("kt_turned"), sem("kt_taken")

        def k_turn_tensor(pe):
            for g in range(TT):
                if g >= 4:
                    pe.wait_ge(kt_taken, g - 3)
                n = P if g != TT - 1 else NS
                for j in range(NP):
                    mm = nc.tensor.transpose(PS[0:n, g % 4, j * P:(j + 1) * P], qk[:, NP + j, g * P:g * P + n], IDENT[:, :])
                mm.then_inc(kt_turned, 1)

        def k_turn_vector(dve):
            for g in range(TT):
                n = P if g != TT - 1 else NS
                dve.wait_ge(kt_turned, g + 1)
                nc.vector.tensor_copy(ktok[0:n, g, :], PS[0:n, g % 4, :]).then_inc(kt_taken, 1)

        gexp, rows_ready, cols_turned, dec_ready, cols_taken = (
            sem("gate_softplus"), sem("rows_ready"), sem("cols_turned"), sem("dec_ready"),
            sem("cols_taken"))

        def gate_scalar(act):
            chain = chains["act"]
            chain(nc.scalar.activation(gm[0:H], gf[0:H], ACT.Abs))
            chain(nc.scalar.activation(gm[0:H], gm[0:H], ACT.Exp, scale=-1.0))
            nc.scalar.activation(gm[0:H], gm[0:H], ACT.Ln, bias=1.0).then_inc(gexp, 1)
            act.wait_ge(cols_taken, TT)
            nc.scalar.activation(colx[:, :, 0, :], cols[:, :, 0, :], ACT.Exp)
            nc.scalar.activation(colx[:, :, 1, :], cols[:, :, 1, :], ACT.Exp, scale=-1.0)
            chain(nc.scalar.activation(colx[:, :, 2, :], cols[:, :, 3, :], ACT.Exp))
            nc.scalar.activation(colx[:, :, 2, :], colx[:, :, 2, :], ACT.Copy, scale=HD ** -0.5)
            act.wait_ge(dec_ready, 1)
            nc.scalar.activation(dec[:, :, :], PS[:, 5, 0:64].rearrange("p (a b) -> p a b", a=NP), ACT.Exp)

        def gate_vector(dve):
            chain = chains["dve"]
            dve.wait_ge(out_stored, 16 * mark["conv_rows"])
            nc.vector.memset(rows4[:, :], 0.0)
            nc.vector.memset(cols[:, :, :, :], 0.0)
            nc.vector.memset(cst[:, :, :], 0.0)
            chain(nc.vector.memset(mrow[0:H, 0:1], NEG))
            dve.wait_ge(gexp, 1)
            chain(nc.vector.scalar_tensor_tensor(out=gf[0:H], in0=gf[0:H], scalar=0.0, in1=gm[0:H],
                                                 op0=ALU.min, op1=ALU.subtract))
            nc.vector.tensor_tensor_scan(gb[0:H], restart[0:H], gf[0:H], 0.0, ALU.mult, ALU.add)
            nc.vector.tensor_tensor_scan(gm[0:H, 0:SEQ], gf[0:H, 0:SEQ], gi[0:H, 0:SEQ], NEG, ALU.add, ALU.max)
            for b in range(DB):
                t = slice(SEQ + b * DT, SEQ + (b + 1) * DT)
                last = nc.vector.tensor_tensor_scan(gm[0:H, t], gf[0:H, t], gi[0:H, t], mrow[0:H, NC + b:NC + b + 1],
                                                    ALU.add, ALU.max)
            chain(last)
            chunk3 = lambda r: r[:, 0:SEQ].rearrange("p (c t) -> p c t", t=P)
            batch3 = lambda r: r[:, SEQ:N].rearrange("p (c t) -> p c t", t=DT)
            nc.vector.tensor_copy(mrow[0:H, 1:NC], gm[0:H, P - 1:SEQ - P:P])
            nc.vector.tensor_copy(m_out[0:H, 1:1 + DB], gm[0:H, SEQ + DT - 1:N:DT])
            nc.vector.tensor_tensor(gu[0:H], gb[0:H], gm[0:H], ALU.subtract)
            nc.vector.tensor_copy(rows4[32:32 + H, :], gm[0:H])
            nc.vector.tensor_tensor(gw[0:H], gi[0:H], gb[0:H], ALU.subtract)
            chain(nc.vector.tensor_copy(m_out[0:H, 0:1], gm[0:H, SEQ - 1:SEQ]))
            g8, m8 = gu[0:H], mrow[0:H]
            nc.vector.tensor_tensor(chunk3(rows4[0:H]), chunk3(g8), m8[:, 0:NC].unsqueeze(2).to_broadcast([H, NC, P]), ALU.add)
            nc.vector.tensor_tensor(batch3(rows4[0:H]), batch3(g8), m8[:, NC:].unsqueeze(2).to_broadcast([H, DB, DT]), ALU.add)
            nc.vector.tensor_copy(rows4[64:64 + H, :], gw[0:H])
            nc.vector.tensor_tensor(chunk3(rows4[96:96 + H]), chunk3(gw[0:H]),
                                    chunk3(g8)[:, :, P - 1:P].to_broadcast([H, NC, P]), ALU.add)
            chain(nc.vector.tensor_tensor(batch3(rows4[96:96 + H]), batch3(gw[0:H]),
                                          batch3(g8)[:, :, DT - 1:DT].to_broadcast([H, DB, DT]), ALU.add))
            nc.vector.tensor_copy(dkrow[0:H, 0:NC], rows4[0:H, P - 1:SEQ:P])
            nc.vector.tensor_copy(dkrow[0:H, NC:], rows4[0:H, SEQ + DT - 1:N:DT]).then_inc(rows_ready, 1)
            for g in range(TT):
                n = P if g != TT - 1 else NS
                dve.wait_ge(cols_turned, g + 1)
                nc.vector.tensor_copy(cols[0:n, g, :, :], PS[0:n, g % 4, 0:P].rearrange("p (a b) -> p a b", a=4)[:, :, 0:H])\
                    .then_inc(cols_taken, 1)

        def gate_tensor(pe):
            pe.wait_ge(rows_ready, 1)
            for g in range(TT):
                n = P if g != TT - 1 else NS
                if g >= 4:
                    pe.wait_ge(cols_taken, g - 3)
                nc.tensor.transpose(PS[0:n, g % 4, 0:P], rows4[:, g * P:g * P + n], IDENT[:, :]).then_inc(cols_turned, 1)
            for p in range(NP):
                mm = nc.tensor.matmul(PS[:, 5, 16 * p:16 * p + 16], pair_sel[0:H, p, :], dkrow[0:H, :], start=True, stop=True)
            mm.then_inc(dec_ready, 1)

        def m_store(sp):
            sp.wait_ge(rows_ready, 1)
            with nc.allow_non_contiguous_dma(reason="one value per head"):
                stored(sp.dma_start(O["m_p"].rearrange("a h -> h a"), m_out[0:H, 0:1]))
                stored(sp.dma_start(O["m_s"].rearrange("b h -> h b"), m_out[0:H, 1:1 + DB]))

        lb = cut(SC, 0, H, P)
        la2 = cut(SC, 1024, H, P), cut(SC, 2048, H, P)
        mnum = cut(SC, 3072, H, V1W)
        hout = cut(SC, 3592, H, HD)
        kw = cut(XW, TT * AW + N, AW)
        cst = cut(XN, ML0 + 3448, NP, 2 * V1W)
        den = SMALL[:, 16:24]
        rden = SMALL[:, 24:32]
        sample_c = cut(WRT, 0, DB, NP * 2 * V1W)
        q_mask = cut(HB, BIG + 2 * NP * N, DB, NP * NS)
        kwm = cut(SC, 2048, 2, AW)
        n_rows = cut(HB, BIG + 2 * NP * N + DB * NP * NS, P)
        n_stage = cut(HB, BIG + 2 * NP * N + DB * NP * NS + P, 40)
        n_out = cut(HB, BIG + 2 * NP * N + DB * NP * NS + 2 * P, P)

        c_ready, c_l, c_e, c_a, c_num, c_h, c_ht, c_cat, c_kw, c_upd, c_state = (
            sem(n) for n in ("chunk_scores", "chunk_logits", "chunk_weights", "chunk_a", "chunk_num", "chunk_h",
                             "chunk_h_turned", "chunk_done", "chunk_kw", "chunk_update", "chunk_state"))

        def slot(h):
            return (h % 2) * (H // 2) + h // 2

        def scores_tensor(pe, t0, n):
            for h in range(H):
                rows = slice(HD * (h % 2), HD * (h % 2) + HD)
                nc.tensor.matmul(PS[0:n, h % 2, (h // 2) * P:(h // 2) * P + n], qk[rows, NP + h // 2, t0:t0 + n],
                                 qk[rows, h // 2, t0:t0 + n], start=True, stop=True)
                mm = nc.tensor.matmul(PS[0:n, 2 + h % 2, (h // 2) * P:(h // 2) * P + n], head_sel[0:H, h, 0:n],
                                      gu[0:H, t0:t0 + n], start=True, stop=True)
            mm.then_inc(c_ready, 1)

        def num_tensor(pe, c, n):
            pe.wait_ge(c_a, c + 1)
            for h in range(H):
                mm = nc.tensor.matmul(PS[0:n, 4 + h // 4, (h % 4) * V1W:(h % 4 + 1) * V1W], la2[c % 2][0:n, slot(h), 0:n],
                                      v1[0:n, c, h * V1W:(h + 1) * V1W], start=True, stop=True)
            mm.then_inc(c_num, 1)

        def turn_h_tensor(pe, c, n):
            pe.wait_ge(c_h, c + 1)
            for j in range(NP):
                mm = nc.tensor.transpose(PS[:, 4, j * P:j * P + n], hout[0:n, 2 * j:2 * j + 2, :].rearrange("p a b -> p (a b)"),
                                         IDENT[0:n, 0:n])
            mm.then_inc(c_ht, 1)

        def chunk_tensor(pe):
            scores_tensor(pe, 0, P)
            for c in range(NC):
                if c:
                    pe.wait_ge(c_state, c)
                for p in range(NP):
                    nc.tensor.matmul(PS[:, 6 + p // 2, (p % 2) * 2 * V1W:(p % 2 + 1) * 2 * V1W], qk[:, p, c * P:(c + 1) * P],
                                     cst[:, p, :], start=True, stop=True)
                if c:
                    pe.wait_ge(c_cat, c)
                num_tensor(pe, c, P)
                if c + 1 < NC:
                    scores_tensor(pe, (c + 1) * P, P)
                pe.wait_ge(c_kw, c + 1)
                pe.wait_ge(c_h, c + 1)
                for p in range(NP):
                    mm = nc.tensor.matmul(PS[:, 6 + p // 2, (p % 2) * 2 * V1W:(p % 2 + 1) * 2 * V1W], kw[:, p * P:(p + 1) * P],
                                          v1[:, c, p * 2 * V1W:(p + 1) * 2 * V1W], start=True, stop=True)
                mm.then_inc(c_upd, 1)
                turn_h_tensor(pe, c, P)

        def chunk_scalar(act, chunks):
            for c in chunks:
                n = P if c < NC else NS
                act.wait_ge(c_l, c + 1)
                for h in range(H):
                    last = nc.scalar.activation(lb[0:n, slot(h), 0:n], lb[0:n, slot(h), 0:n], ACT.Exp, bias=cols[0:n, c, 2, h:h + 1])
                last.then_inc(c_e, 1)

        def chunk_pool(pool, chunks):
            for c in chunks:
                n = P if c < NC else NS
                if 0 < c < NC:
                    pool.wait_ge(c_upd, c)
                nc.gpsimd.tensor_tensor(kw[0:n, :].rearrange("p (h d) -> p h d", h=H),
                                        ktok[0:n, c, :].rearrange("p (h d) -> p h d", h=H),
                                        colx[0:n, c, 2, :].unsqueeze(2).to_broadcast([n, H, HD]), ALU.mult).then_inc(c_kw, 1)

        def chunk_logits(dve, c, n, mask):
            dve.wait_ge(c_ready, c + 1)
            if c and c < NC:
                dve.wait_ge(c_a, c)
            nc.vector.tensor_tensor(lb[0:n, :, 0:n], bank2(n, 2), mask.unsqueeze(1).to_broadcast([n, H, n]), ALU.add).then_inc(c_l, 1)

        def bank2(n, b):
            return PS[0:n, b:b + 2, :].rearrange("p a (h t) -> p (a h) t", h=4)[:, :, 0:n]

        def chunk_weights(dve, c, n):
            dve.wait_ge(c_e, c + 1)
            nc.vector.scalar_tensor_tensor(out=la2[c % 2][0:n, :, 0:n], in0=bank2(n, 0), scalar=HD ** -0.5, in1=lb[0:n, :, 0:n],
                                           op0=ALU.mult, op1=ALU.mult).then_inc(c_a, 1)

        def chunk_output(dve, c, n):
            chain = chains["dve"]
            dve.wait_ge(c_num, c + 1)
            iw = colx[0:n, c, 0, :].rearrange("p (a h) -> p a h", a=2)
            m4 = mnum[0:n].rearrange("p (a h) d -> p a h d", a=2)
            part = lambda b: PS[0:n, b, 0:4 * V1W].rearrange("p (h d) -> p h d", h=4)
            for a in range(2):
                last = nc.vector.tensor_tensor(m4[:, a], part(6 + a), iw[:, a].unsqueeze(2).to_broadcast([n, 4, V1W]), ALU.mult)
            chain(last)
            for a in range(2):
                last = nc.vector.tensor_tensor(m4[:, a], part(4 + a), m4[:, a], ALU.add)
            chain(last)
            chain(nc.vector.tensor_scalar(den[0:n], mnum[0:n, :, HD], -1.0, None, ALU.mult))
            chain(nc.vector.tensor_tensor(den[0:n], den[0:n], mnum[0:n, :, HD], ALU.max))
            chain(nc.vector.tensor_tensor(den[0:n], den[0:n], colx[0:n, c, 1, :], ALU.max))
            chain(nc.vector.reciprocal(rden[0:n], den[0:n]))
            nc.vector.tensor_tensor(hout[0:n], mnum[0:n, :, 0:HD], rden[0:n].unsqueeze(2).to_broadcast([n, H, HD]), ALU.mult)\
                .then_inc(c_h, 1)

        def chunk_place(dve, c, n, t0):
            dve.wait_ge(c_ht, c + 1)
            nc.vector.tensor_tensor(sig_o[:, :, t0:t0 + n], PS[:, 4, :].rearrange("p (j t) -> p j t", j=NP)[:, :, 0:n],
                                    sig_o[:, :, t0:t0 + n], ALU.mult).then_inc(c_cat, 1)

        def state_update(state, c, banks, signal):
            chain = chains["dve"]
            for e in range(2):
                rows, cs = slice(HD * e, HD * e + HD), slice(V1W * e, V1W * e + V1W)
                last = nc.vector.tensor_tensor(state[rows, :, cs], state[rows, :, cs],
                                               dec[rows, :, c:c + 1].to_broadcast([HD, NP, V1W]), ALU.mult)
            chain(last)
            for e in range(2):
                rows, cs = slice(HD * e, HD * e + HD), slice(V1W * e, V1W * e + V1W)
                for a in range(2):
                    upd = PS[rows, banks + a, 0:4 * V1W].rearrange("p (j d) -> p j d", j=2)
                    last = nc.vector.tensor_tensor(state[rows, 2 * a:2 * a + 2, cs], upd[:, :, cs], state[rows, 2 * a:2 * a + 2, cs], ALU.add)
            last.then_inc(signal, 1)

        def chunk_vector(dve):
            chunk_logits(dve, 0, P, causal[:, :])
            chunk_weights(dve, 0, P)
            for c in range(NC):
                chunk_output(dve, c, P)
                if c + 1 < NC:
                    chunk_logits(dve, c + 1, P, causal[:, :])
                dve.wait_ge(c_upd, c + 1)
                if c:
                    dve.wait_ge(c_state, c)
                state_update(cst, c, 6, c_state)
                if c + 1 < NC:
                    chunk_weights(dve, c + 1, P)
                chunk_place(dve, c, P, c * P)
            dve.wait_ge(c_state, NC)

        sc_zeroed, sc_landed, n_turned, n_put, qm_ready, kwm_ready, su_ready, su_done, n_ready, n_rows_ready = (
            sem(n) for n in ("sc_zeroed", "sc_landed", "n_turned", "n_put", "q_mask_ready", "kwm_ready", "sample_update",
                             "sample_state", "n_ready", "n_rows_ready"))
        sc4 = sample_c[:, :, :].rearrange("p b (j d) -> p b j d", j=NP)

        def sample_state_load(sp):
            sp.wait_ge(sc_zeroed, 1)
            src = A["state_mlstm_C"].rearrange("b (j e) k v -> e k b j v", e=2)
            with nc.allow_non_contiguous_dma(reason="rows of 64 floats"):
                for e in range(2):
                    for b in range(DB):
                        sp.dma_start(sc4[HD * e:HD * e + HD, b, :, V1W * e:V1W * e + HD], src[e, :, b]).then_inc(sc_landed, 16)
            sp.wait_ge(phase_done, 4 * PH["chunks"])
            sp.dma_start(n_rows[0:DB * NP, :], A["state_mlstm_n"].rearrange("b (j e) k -> (b j) (e k)", e=2)).then_inc(n_landed, 16)

        n_landed = sem("n_landed")

        def sample_pool(pool):
            chains["pool"](nc.gpsimd.memset(sample_c[:, :, :], 0.0))
            nc.gpsimd.memset(SMALL[:, 40:41], 0.0).then_inc(sc_zeroed, 1)

        def q_mask_pool(pool):
            chains["pool"](nc.gpsimd.memset(q_mask[:, :, :], 0.0))
            for b in range(DB):
                qm = q_mask[:, b, :].rearrange("p (j t) -> p j t", j=NP)
                last = nc.gpsimd.tensor_copy(qm[:, :, b * DT:(b + 1) * DT], qk[:, 0:NP, SEQ + b * DT:SEQ + (b + 1) * DT])
            last.then_inc(qm_ready, 1)

        def sample_tensor(pe):
            pe.wait_ge(n_landed, 16)
            nc.tensor.transpose(PS[:, 7, 480:512], n_rows[0:DB * NP, :], IDENT[0:DB * NP, 0:DB * NP]).then_inc(n_turned, 1)
            scores_tensor(pe, SEQ, NS)
            pe.wait_ge(n_put, 1)
            pe.wait_ge(qm_ready, 1)
            for p in range(NP):
                for b in range(DB):
                    mm = nc.tensor.matmul(PS[0:NS, 6 + p // 2, (p % 2) * 2 * V1W:(p % 2 + 1) * 2 * V1W],
                                          q_mask[:, b, p * NS:(p + 1) * NS], sc4[:, b, p, :], start=(b == 0), stop=(b == DB - 1))
            num_tensor(pe, NC, NS)
            turn_h_tensor(pe, NC, NS)
            for b in range(DB):
                pe.wait_ge(kwm_ready, b + 1)
                bank = 4 + 2 * (b % 2)
                if b == 0:
                    pe.wait_ge(c_cat, NC + 1)
                if b >= 2:
                    pe.wait_ge(su_done, b - 1)
                for p in range(NP):
                    mm = nc.tensor.matmul(PS[:, bank + p // 2, (p % 2) * 2 * V1W:(p % 2 + 1) * 2 * V1W],
                                          kwm[0:NS, b % 2, p * P:(p + 1) * P], v1[0:NS, NC, p * 2 * V1W:(p + 1) * 2 * V1W],
                                          start=True, stop=True)
                mm.then_inc(su_ready, 1)
            pe.wait_ge(n_ready, 1)
            nc.tensor.transpose(PS[0:(DB + 1) * NP, 0, 0:P], n_stage[:, 0:(DB + 1) * NP], IDENT[:, :]).then_inc(n_rows_ready, 1)

        def sample_vector(dve):
            chain = chains["dve"]
            dve.wait_ge(n_turned, 1)
            dve.wait_ge(sc_landed, 16 * 16)
            for e in range(2):
                rows = slice(HD * e, HD * e + HD)
                last = nc.vector.tensor_copy(sc4[rows, :, :, V1W * e + HD], PS[rows, 7, 480:512].rearrange("p (b j) -> p b j", b=DB))
            last.then_inc(n_put, 1)
            chunk_logits(dve, NC, NS, sample_causal[0:NS])
            chunk_weights(dve, NC, NS)
            chunk_output(dve, NC, NS)
            chunk_place(dve, NC, NS, SEQ)
            dve.wait_ge(c_kw, NC + 1)

            def masked(b):
                if b >= 2:
                    dve.wait_ge(su_ready, b - 1)
                nc.vector.tensor_scalar(kwm[0:NS, b % 2, :], kw[0:NS, :], batch_sel[0:NS, b:b + 1], None, ALU.mult).then_inc(kwm_ready, 1)
            masked(0)
            for b in range(DB):
                if b + 1 < DB:
                    masked(b + 1)
                dve.wait_ge(su_ready, b + 1)
                state_update(sc4[:, b], NC + b, 4 + 2 * (b % 2), su_done)
            dve.wait_ge(su_done, DB)
            for e in range(2):
                rows = slice(HD * e, HD * e + HD)
                nc.vector.tensor_copy(n_stage[rows, 0:DB * NP].rearrange("p (b j) -> p b j", b=DB), sc4[rows, :, :, V1W * e + HD])
                last = nc.vector.tensor_copy(n_stage[rows, DB * NP:(DB + 1) * NP], cst[rows, :, V1W * e + HD])
            last.then_inc(n_ready, 1)
            dve.wait_ge(n_rows_ready, 1)
            nc.vector.tensor_copy(n_out[0:(DB + 1) * NP, :], PS[0:(DB + 1) * NP, 0, 0:P]).then_inc(n_out_ready, 1)

        n_out_ready = sem("n_out_ready")

        def state_store(sp):
            sp.wait_ge(n_out_ready, 1)
            cs, cp = (O[n].rearrange("b (j e) k v -> e k b j v", e=2) for n in ("C_s", "C_p"))
            with nc.allow_non_contiguous_dma(reason="rows of 64 floats"):
                for e in range(2):
                    rows, c64 = slice(HD * e, HD * e + HD), slice(V1W * e, V1W * e + HD)
                    stored(sp.dma_start(cp[e, :, 0], cst[rows, :, c64]))
                    for b in range(DB):
                        stored(sp.dma_start(cs[e, :, b], sc4[rows, b, :, c64]))
            stored(sp.dma_start(O["n_s"].rearrange("b (j e) k -> (b j) (e k)", e=2), n_out[0:DB * NP, :]))
            stored(sp.dma_start(O["n_p"].rearrange("b (j e) k -> (b j) (e k)", e=2), n_out[DB * NP:(DB + 1) * NP, :]))
            sp.wait_ge(out_stored, 16 * stores[0])

        KT = PAST // P
        kc = cut(XW, 0, 2, KT * AW)
        kT = cut(HB, BIG, NP, PAST), cut(HB, BIG + 4096, NP, PAST)
        wo = cut(HB, BIG + 8192, 2, AW)
        vc = cut(XN, 0, 2, KT * AW)
        wl = cut(SC, 0, PAST + NS)
        wbias = cut(SC, PAST + NS, PAST)
        wnew = cut(SC, 2 * PAST + NS, DB // 2 * NS)
        wpt = cut(SC, 2 * PAST + NS + DB // 2 * NS, 9, P)
        kc_landed = [sem(f"kc_landed{i}") for i in range(2)]
        vc_landed = [sem(f"vc_landed{i}") for i in range(2)]
        wb_landed = sem("wb_landed")
        wk_taken = [sem(f"wk_taken{i}") for i in range(2)]
        wk_turned, ws_ready, wl_ready, wp_ready, wp_turned, wp_taken, wo_ready, wo_taken, wl_free = (
            sem(n) for n in ("wk_turned", "ws_ready", "wl_ready", "wp_ready", "wp_turned", "wp_taken",
                             "wo_ready", "wo_taken", "wl_free"))

        def win_load(sp):
            sp.wait_ge(phase_done, 4 * PH["sample"])
            sp.dma_start(wbias, A["sample_bias"]).then_inc(wb_landed, 16)
            sp.dma_start(wnew, A["sample_new_bias"]).then_inc(wb_landed, 16)
            kd, vd = (A[n].rearrange("b (t p) h d -> b p t (h d)", p=P) for n in ("cache_win_k", "cache_win_v"))
            def load_k(b):
                if b >= 2:
                    sp.wait_ge(wk_turned, NP * 2 * (b - 1))
                sp.dma_start(kc[:, b % 2, :].rearrange("p (t n) -> p t n", n=AW), kd[b]).then_inc(kc_landed[b % 2], 16)

            def load_v(b):
                if b >= 2:
                    sp.wait_ge(wo_ready, b - 1)
                sp.dma_start(vc[:, b % 2, :].rearrange("p (t n) -> p t n", n=AW), vd[b]).then_inc(vc_landed[b % 2], 16)
            load_k(0)
            load_k(1)
            for pair in range(DB // 2):
                if pair + 1 < DB // 2:
                    load_k(2 * pair + 2)
                if pair == 0:
                    load_v(0)
                    load_v(1)
                if pair + 1 < DB // 2:
                    load_k(2 * pair + 3)
                if pair:
                    load_v(2 * pair)
                    load_v(2 * pair + 1)

        def win_tensor(pe):
            def turn_k(b):
                pe.wait_ge(kc_landed[b % 2], 16 * (b // 2 + 1))
                kb = kc[:, b % 2, :].rearrange("p (t n) -> p t n", n=AW)
                for p in range(NP):
                    for half in range(2):
                        if b or p:
                            pe.wait_ge(wk_taken[half], NP * b + p)
                        for j in range(4):
                            mm = nc.tensor.transpose(PS[:, half, j * P:(j + 1) * P], kb[:, 4 * half + j, p * P:(p + 1) * P],
                                                     IDENT[:, :])
                        mm.then_inc(wk_turned, 1)

            def scores(b):
                e, pair = b % 2, b // 2
                for half in range(2):
                    pe.wait_ge(wk_taken[half], NP * (b + 1))
                if e == 0 and pair:
                    pe.wait_ge(wl_ready, pair)
                x = kT[b % 2]
                for c, (w, x) in enumerate(((512, x[:, :, 0:512]), (512, x[:, :, 512:PAST]), (NS, KNEW[:, :, :]))):
                    for p in range(NP):
                        mm = nc.tensor.matmul(PS[HD * e:HD * e + HD, 2 + c, 0:w], QX[:, p, b, :], x[:, p, :],
                                              start=(p == 0), stop=(p == NP - 1))
                mm.then_inc(ws_ready, 1)

            def turn_p(pair):
                pe.wait_ge(wp_ready, pair + 1)
                for q in range(3):
                    n = 3 * pair + q
                    if n >= 2:
                        pe.wait_ge(wp_taken, n - 1)
                    if q < 2:
                        for j in range(4):
                            mm = nc.tensor.transpose(PS[:, 5 + n % 2, j * P:(j + 1) * P], wl[:, (4 * q + j) * P:(4 * q + j + 1) * P],
                                                     IDENT[:, :])
                    else:
                        mm = nc.tensor.transpose(PS[0:NS, 5 + n % 2, 0:P], wl[:, PAST:PAST + NS], IDENT[:, :])
                    mm.then_inc(wp_turned, 1)

            def values(pair):
                pe.wait_ge(wp_taken, 3 * pair + 3)
                if pair:
                    pe.wait_ge(wo_taken, pair)
                for e in range(2):
                    pe.wait_ge(vc_landed[e], 16 * (pair + 1))
                    vb = vc[:, e, :].rearrange("p (t n) -> p t n", n=AW)
                    cs = slice(HD * e, HD * e + HD)
                    for t in range(KT + 1):
                        p, v = (wpt[:, t, cs], vb[:, t, :]) if t < KT else (wpt[0:NS, t, cs], VNEW[:, :])
                        mm = nc.tensor.matmul(PS[cs, 7, :], p, v, start=(t == 0), stop=(t == KT))
                    mm.then_inc(wo_ready, 1)

            def turn_o(pair):
                pe.wait_ge(wv_taken, pair + 1)
                for j in range(NP):
                    mm = nc.tensor.transpose(PS[:, 7, j * P:(j + 1) * P], wo[:, pair % 2, j * P:(j + 1) * P], IDENT[:, :])
                mm.then_inc(wo_turned, 1)

            turn_k(0)
            for b in range(DB):
                if b + 1 < DB:
                    turn_k(b + 1)
                scores(b)
                if b >= 2:
                    (turn_p if b % 2 == 0 else values)(b // 2 - 1)
                if b >= 4 and b % 2 == 0:
                    turn_o(b // 2 - 2)
            turn_p(DB // 2 - 1)
            turn_o(DB // 2 - 2)
            values(DB // 2 - 1)
            turn_o(DB // 2 - 1)

        wv_taken, wo_turned = sem("wv_taken"), sem("wo_turned")

        def take_k(eng, half, b):
            for p in range(NP):
                eng.wait_ge(wk_turned, 2 * (NP * b + p) + half + 1)
                if p == 0 and b >= 2:
                    eng.wait_ge(ws_ready, b - 1)
                out, src = kT[b % 2][:, p, 512 * half:512 * half + 512], PS[:, half, :]
                ins = nc.vector.tensor_copy(out, src) if half else nc.scalar.activation(out, src, ACT.Copy)
                ins.then_inc(wk_taken[half], 1)

        def win_scalar(act):
            def take_p(pair):
                for q in range(3):
                    n = 3 * pair + q
                    act.wait_ge(wp_turned, n + 1)
                    if q == 0 and pair:
                        act.wait_ge(wo_ready, 2 * pair)
                    if q < 2:
                        last = nc.scalar.activation(wpt[:, 4 * q:4 * q + 4, :], PS[:, 5 + n % 2, :].rearrange("p (a b) -> p a b", a=4), ACT.Copy)
                    else:
                        last = nc.scalar.activation(wpt[0:NS, KT, :], PS[0:NS, 5 + n % 2, 0:P], ACT.Copy)
                    last.then_inc(wp_taken, 1)
            def take_values(pair):
                act.wait_ge(wo_ready, 2 * pair + 2)
                nc.scalar.activation(wo[:, pair % 2, :], PS[:, 7, :], ACT.Copy).then_inc(wv_taken, 1)
            take_k(act, 0, 0)
            for b in range(DB):
                if b + 1 < DB:
                    take_k(act, 0, b + 1)
                if b >= 4 and b % 2 == 0:
                    take_values(b // 2 - 2)
                if b % 2:
                    act.wait_ge(wl_ready, b // 2 + 1)
                    nc.scalar.activation(wl[:, :], wl[:, :], ACT.Exp, bias=negm[:, 0:1], accum_out=asum[:, 0:1]).then_inc(wl_free, 1)
                elif b:
                    take_p(b // 2 - 1)
            take_values(DB // 2 - 2)
            take_p(DB // 2 - 1)
            take_values(DB // 2 - 1)

        def win_vector(dve):
            chain = chains["dve"]

            def softmax(pair):
                dve.wait_ge(ws_ready, 2 * pair + 2)
                if pair:
                    dve.wait_ge(wp_turned, 3 * pair)
                nc.vector.tensor_tensor_reduce(wl[:, 0:PAST], PS[:, 2:4, :].rearrange("p a b -> p (a b)"), wbias, 1.0, 3 * NEG,
                                               ALU.add, ALU.max, amax[:, 0:1])
                chain(nc.vector.tensor_tensor_reduce(wl[:, PAST:PAST + NS], PS[:, 4, 0:NS], wnew[:, pair * NS:(pair + 1) * NS],
                                                     1.0, 3 * NEG, ALU.add, ALU.max, amax[:, 1:2]))
                chain(nc.vector.tensor_tensor(amax[:, 0:1], amax[:, 0:1], amax[:, 1:2], ALU.max))
                nc.vector.tensor_scalar(negm[:, 0:1], amax[:, 0:1], -1.0, None, ALU.mult).then_inc(wl_ready, 1)
                dve.wait_ge(wl_free, pair + 1)
                chain(nc.vector.reciprocal(arec[:, 0:1], asum[:, 0:1]))
                nc.vector.tensor_scalar(wl[:, :], wl[:, :], arec[:, 0:1], None, ALU.mult).then_inc(wp_ready, 1)

            def output(pair):
                dve.wait_ge(wo_turned, pair + 1)
                for e in range(2):
                    b = 2 * pair + e
                    for r in range(2):
                        rows = slice(HD * r, HD * r + HD)
                        for j in range(NP):
                            h = 2 * j + r
                            last = nc.vector.tensor_copy(cat[rows, j, SEQ + b * DT:SEQ + (b + 1) * DT],
                                                         PS[rows, 7, j * P + HD * e + DT * h:j * P + HD * e + DT * (h + 1)])
                last.then_inc(wo_taken, 1)

            dve.wait_ge(wb_landed, 32)
            take_k(dve, 1, 0)
            for b in range(DB):
                if b + 1 < DB:
                    take_k(dve, 1, b + 1)
                if b % 2:
                    softmax(b // 2)
                elif b >= 4:
                    output(b // 2 - 2)
            output(DB // 2 - 2)
            output(DB // 2 - 1)

        mem_tok = cut(HB, 0, 2, D)
        mem_T = cut(HB, 2048, KB, NMEM)
        mvT = cut(HB, 4096, KB, NMEM)
        mk_tok = cut(sb("mem_k_tok", P, 2 * D, at=AT["sample_q_wide"]), 0, 2, D)
        mkT = cut(HB, BIG, KB, NMEM)
        mv_tok = cut(HB, BIG + 2048, 2, D)
        mhi, mlo = cut(XHI, 0, KB, NMEM), cut(XLO, 0, KB, NMEM)
        mem_landed, mem_turned, mem_taken, mkv_turned, mkv_taken = (
            sem(n) for n in ("mem_landed", "mem_turned", "mem_taken", "mkv_turned", "mkv_taken"))

        def mem_load(sp):
            sp.wait_ge(phase_done, 4 * PH["mix_norm"])
            sp.dma_start(XTF[:, :], XT_DRAM).then_inc(xt_back, 16)
            sp.dma_start(mem_tok[:, :, :], A["mem_prompt"][0].rearrange("(t p) d -> p t d", p=P)).then_inc(mem_landed, 16)

        def mem_turn_tensor(pe):
            pe.wait_ge(mem_landed, 16)
            for g in range(4):
                t, half = g // 2, g % 2
                for j in range(4):
                    mm = nc.tensor.transpose(PS[:, g, j * P:(j + 1) * P], mem_tok[:, t, (4 * half + j) * P:(4 * half + j + 1) * P], IDENT[:, :])
                mm.then_inc(mem_turned, 1)

        def mem_turn_vector(dve):
            for g in range(4):
                t, half = g // 2, g % 2
                dve.wait_ge(mem_turned, g + 1)
                nc.vector.tensor_copy(mem_T[:, 4 * half:4 * half + 4, t * P:(t + 1) * P], PS[:, g, :].rearrange("p (j n) -> p j n", j=4))

        def mkv_turn_tensor(pe):
            for g in range(8):
                src, t, half = (mkT, mvT)[g // 4], g % 4 // 2, g % 2
                for j in range(4):
                    mm = nc.tensor.transpose(PS[:, g, j * P:(j + 1) * P], src[:, 4 * half + j, t * P:(t + 1) * P], IDENT[:, :])
                mm.then_inc(mkv_turned, 1)

        def mkv_turn_scalar(act):
            for g in range(8):
                dst, t, half = (mk_tok, mv_tok)[g // 4], g % 4 // 2, g % 2
                act.wait_ge(mkv_turned, g + 1)
                nc.scalar.activation(dst[:, t, 512 * half:512 * half + 512], PS[:, g, :], ACT.Copy).then_inc(mkv_taken, 1)

        def mkv_store(sp):
            sp.wait_ge(mkv_taken, 8)
            for name, src in (("mem_k", mk_tok), ("mem_v", mv_tok)):
                stored(sp.dma_start(O[name][0].rearrange("(t p) h d -> p t (h d)", p=P), src[:, :, :]))
            mark["mkv"] = stores[0]

        cq = cat
        xl = cut(SC, 0, 2, XH * NMEM)
        xpt = cut(SC, 2048, 2, 8 * P)
        xmax, xsum, xrec = SMALL[:, 48:56], SMALL[:, 56:64], SMALL[:, 64:72]
        xs_ready, xm_ready, xp_ready, xn_ready, xt_ready, xt_taken, xo_ready, xo_taken = (
            sem(n) for n in ("xs_ready", "xm_ready", "xp_ready", "xn_ready", "xt_ready", "xt_taken", "xo_ready", "xo_taken"))

        def cross_tensor(pe):
            def scores(t):
                if t >= 2:
                    pe.wait_ge(xp_ready, t - 1)
                b0 = 2 * (t % 2)
                for h in range(XH):
                    for k in range(2):
                        mm = nc.tensor.matmul(PS[:, b0 + h // 2, (h % 2) * NMEM:(h % 2 + 1) * NMEM], cq[:, 2 * h + k, t * P:(t + 1) * P],
                                              mkT[:, 2 * h + k, :], start=(k == 0), stop=(k == 1))
                mm.then_inc(xs_ready, 1)
            scores(0)
            for t in range(NC):
                if t + 1 < NC:
                    scores(t + 1)
                pe.wait_ge(xn_ready, t + 1)
                if t:
                    pe.wait_ge(xt_taken, t)
                for i in range(8):
                    mm = nc.tensor.transpose(PS[:, 4 + i // 4, (i % 4) * P:(i % 4 + 1) * P], xl[:, t % 2, i * P:(i + 1) * P], IDENT[:, :])
                mm.then_inc(xt_ready, 1)
                pe.wait_ge(xt_taken, t + 1)
                if t:
                    pe.wait_ge(xo_taken, t)
                for h in range(XH):
                    for db in range(2):
                        i = 2 * h + db
                        for m in range(2):
                            mm = nc.tensor.matmul(PS[:, 6 + i // 4, (i % 4) * P:(i % 4 + 1) * P], mv_tok[:, m, i * P:(i + 1) * P],
                                                  xpt[:, t % 2, (2 * h + m) * P:(2 * h + m + 1) * P], start=(m == 0), stop=(m == 1))
                mm.then_inc(xo_ready, 1)

        def cross_scalar(act):
            for t in range(NC):
                act.wait_ge(xm_ready, t + 1)
                b0, s4 = 2 * (t % 2), 4 * (t % 2)
                for h in range(XH):
                    last = nc.scalar.activation(xl[:, t % 2, h * NMEM:(h + 1) * NMEM],
                                                PS[:, b0 + h // 2, (h % 2) * NMEM:(h % 2 + 1) * NMEM], ACT.Exp,
                                                bias=xmax[:, s4 + h:s4 + h + 1], accum_out=xsum[:, s4 + h:s4 + h + 1])
                last.then_inc(xp_ready, 1)
                act.wait_ge(xt_ready, t + 1)
                if t >= 2:
                    act.wait_ge(xo_ready, t - 1)
                nc.scalar.activation(xpt[:, t % 2, :], PS[:, 4:6, :].rearrange("p a b -> p (a b)"), ACT.Copy).then_inc(xt_taken, 1)
                act.wait_ge(xo_ready, t + 1)
                nc.scalar.activation(xhi[:, :, t * P:(t + 1) * P], PS[:, 6:8, :].rearrange("p a (j n) -> p (a j) n", j=4), ACT.Copy)\
                    .then_inc(xo_high, 1)

        out8 = PS[:, 6:8, :].rearrange("p a (j n) -> p (a j) n", j=4)
        xo_high = sem("xo_high")

        def cross_vector(dve):
            chain = chains["dve"]

            def maxima(t):
                b0, s4 = 2 * (t % 2), 4 * (t % 2)
                dve.wait_ge(xs_ready, t + 1)
                if t >= 2:
                    dve.wait_ge(xp_ready, t - 1)
                    dve.wait_ge(xt_ready, t - 1)
                nc.vector.tensor_reduce(xmax[:, s4:s4 + 4], PS[:, b0:b0 + 2, :].rearrange("p a (h m) -> p (a h) m", h=2), AX_X, ALU.max,
                                        negate=True).then_inc(xm_ready, 1)
            maxima(0)
            for t in range(NC):
                if t + 1 < NC:
                    maxima(t + 1)
                s4 = 4 * (t % 2)
                dve.wait_ge(xp_ready, t + 1)
                chain(nc.vector.reciprocal(xrec[:, s4:s4 + 4], xsum[:, s4:s4 + 4]))
                x3 = xl[:, t % 2, :].rearrange("p (h m) -> p h m", h=XH)
                nc.vector.tensor_tensor(x3, x3, xrec[:, s4:s4 + 4].unsqueeze(2).to_broadcast([P, XH, NMEM]), ALU.mult).then_inc(xn_ready, 1)
                dve.wait_ge(xo_high, t + 1)
                nc.vector.tensor_tensor(xlo[:, :, t * P:(t + 1) * P], out8, xhi[:, :, t * P:(t + 1) * P].bitcast(F32), ALU.subtract)\
                    .then_inc(xo_taken, 1)

        ck = cut(HB, BIG, 2, 2 * D)
        cv = cut(HB, 0, 4, 2 * D)
        ckT = cut(WRT, 0, KB, NMEM), cut(WRT, 2048, KB, NMEM)
        yo = cut(WRT, 4096, D)
        cqx = cut(SC, 0, KB, DB, XH * DT)
        yl = cut(SC, 2048, NMEM)
        ypt = cut(SC, 2304, 2, P)
        ck_landed = [sem(f"ck_landed{i}") for i in range(2)]
        cv_landed = [sem(f"cv_landed{i}") for i in range(2)]
        cqx_ready, yk_turned, yk_taken, ys_ready, ym_ready, yp_ready, yn_ready, yt_ready, yt_taken, yo_ready, yo_taken = (
            sem(n) for n in ("cqx_ready", "yk_turned", "yk_taken", "ys_ready", "ym_ready", "yp_ready", "yn_ready", "yt_ready",
                             "yt_taken", "yo_ready", "yo_taken"))

        def xsample_load(sp):
            sp.wait_ge(out_stored, 16 * mark["mkv"])
            sp.wait_ge(phase_done, 4 * PH["cross"])
            kd, vd = (A[n].rearrange("b (t p) h d -> b p t (h d)", p=P) for n in ("cache_mem_k", "cache_mem_v"))
            for b in range(DB):
                if b >= 2:
                    sp.wait_ge(yk_turned, 4 * (b - 1))
                sp.dma_start(ck[:, b % 2, :].rearrange("p (t n) -> p t n", n=D), kd[b]).then_inc(ck_landed[b % 2], 16)
                if b == 1:
                    sp.wait_ge(cqx_ready, 1)
                    for v in range(4):
                        sp.dma_start(cv[:, v, :].rearrange("p (t n) -> p t n", n=D), vd[v]).then_inc(cv_landed[0], 16)
            for b in range(4, DB):
                sp.wait_ge(yo_ready, b - 3)
                sp.dma_start(cv[:, b % 4, :].rearrange("p (t n) -> p t n", n=D), vd[b]).then_inc(cv_landed[1], 16)
            sp.wait_ge(yo_turned, 2)

        def xsample_pool(pool):
            chains["pool"](nc.gpsimd.memset(cqx[:, :, :, :], 0.0))
            for h in range(XH):
                for k in (2 * h, 2 * h + 1):
                    last = nc.gpsimd.tensor_copy(cqx[:, k, :, h * DT:(h + 1) * DT], cq[:, k, SEQ:N].rearrange("p (b t) -> p b t", t=DT))
            last.then_inc(cqx_ready, 1)

        def xsample_tensor(pe):
            pe.wait_ge(cqx_ready, 1)
            def turn_k(b):
                pe.wait_ge(ck_landed[b % 2], 16 * (b // 2 + 1))
                kb = ck[:, b % 2, :].rearrange("p (t n) -> p t n", n=D)
                for q in range(4):
                    g = 4 * b + q
                    if g >= 2:
                        pe.wait_ge(yk_taken, g - 1)
                    for j in range(4):
                        mm = nc.tensor.transpose(PS[:, g % 2, j * P:(j + 1) * P], kb[:, j % 2, (2 * q + j // 2) * P:(2 * q + j // 2 + 1) * P],
                                                 IDENT[:, :])
                    mm.then_inc(yk_turned, 1)
            turn_k(0)
            for quad in range(2):
                for i in range(4):
                    b = 4 * quad + i
                    if b + 1 < DB:
                        turn_k(b + 1)
                    pe.wait_ge(yk_taken, 4 * (b + 1))
                    if i == 0 and quad:
                        pe.wait_ge(yp_ready, quad)
                    for k in range(KB):
                        mm = nc.tensor.matmul(PS[32 * i:32 * i + 32, 2, 0:NMEM], cqx[:, k, b, :], ckT[b % 2][:, k, :],
                                              start=(k == 0), stop=(k == KB - 1), tile_position=(0, 32 * i))
                    mm.then_inc(ys_ready, 1)
                pe.wait_ge(yn_ready, quad + 1)
                if quad:
                    pe.wait_ge(yt_taken, quad)
                for m in range(2):
                    mm = nc.tensor.transpose(PS[:, 3, m * P:(m + 1) * P], yl[:, m * P:(m + 1) * P], IDENT[:, :])
                mm.then_inc(yt_ready, 1)
                pe.wait_ge(yt_taken, quad + 1)
                pe.wait_ge(cv_landed[quad], 64)
                if quad:
                    pe.wait_ge(yo_taken, quad)
                for i in range(4):
                    vb = cv[:, i, :].rearrange("p (t n) -> p t n", n=D)
                    rows = slice(32 * i, 32 * i + 32)
                    for half in range(2):
                        for m in range(2):
                            mm = nc.tensor.matmul(PS[rows, 4 + half, :], ypt[:, m, rows], vb[:, m, 512 * half:512 * half + 512],
                                                  start=(m == 0), stop=(m == 1), tile_position=(0, 32 * i))
                    mm.then_inc(yo_ready, 1)
                pe.wait_ge(yv_taken, quad + 1)
                for k in range(KB):
                    mm = nc.tensor.transpose(PS[:, 6 + k // 4, (k % 4) * P:(k % 4 + 1) * P], yo[:, k * P:(k + 1) * P], IDENT[:, :])
                mm.then_inc(yo_turned, 1)

        yv_taken, yo_turned, yo_high = sem("yv_taken"), sem("yo_turned"), sem("yo_high")

        def sample_out(quad, k, x):
            src = PS[:, 6 + k // 4, (k % 4) * P:(k % 4 + 1) * P].rearrange("p (b c) -> p b c", b=4)
            return (x[:, k, SEQ + quad * 32:SEQ + quad * 32 + 32].rearrange("p (b t) -> p b t", b=4),
                    src[:, :, DT * (k // 2):DT * (k // 2) + DT])

        def xsample_scalar(act):
            def take_k(b):
                for q in range(4):
                    g = 4 * b + q
                    act.wait_ge(yk_turned, g + 1)
                    if q == 0 and b >= 2:
                        act.wait_ge(ys_ready, b - 1)
                    nc.scalar.activation(ckT[b % 2][:, 2 * q:2 * q + 2, :], PS[:, g % 2, :].rearrange("p (a b) -> p a b", a=2), ACT.Copy)\
                        .then_inc(yk_taken, 1)
            take_k(0)
            for quad in range(2):
                for i in range(4):
                    if 4 * quad + i + 1 < DB:
                        take_k(4 * quad + i + 1)
                act.wait_ge(ym_ready, quad + 1)
                nc.scalar.activation(yl[:, :], PS[:, 2, 0:NMEM], ACT.Exp, bias=xmax[:, 0:1], accum_out=xsum[:, 0:1]).then_inc(yp_ready, 1)
                act.wait_ge(yt_ready, quad + 1)
                if quad:
                    act.wait_ge(yo_ready, 4 * quad)
                nc.scalar.activation(ypt[:, :, :], PS[:, 3, 0:2 * P].rearrange("p (a b) -> p a b", a=2), ACT.Copy).then_inc(yt_taken, 1)
                act.wait_ge(yo_ready, 4 * quad + 4)
                nc.scalar.activation(yo, PS[:, 4:6, :].rearrange("p a b -> p (a b)"), ACT.Copy).then_inc(yv_taken, 1)
                act.wait_ge(yo_turned, quad + 1)
                for k in range(KB):
                    out, src = sample_out(quad, k, xhi)
                    last = nc.scalar.activation(out, src, ACT.Copy)
                last.then_inc(yo_high, 1)

        def xsample_vector(dve):
            for quad in range(2):
                dve.wait_ge(ys_ready, 4 * quad + 4)
                if quad:
                    dve.wait_ge(yt_ready, quad)
                nc.vector.tensor_reduce(xmax[:, 0:1], PS[:, 2, 0:NMEM], AX_X, ALU.max, negate=True).then_inc(ym_ready, 1)
                dve.wait_ge(yp_ready, quad + 1)
                chains["dve"](nc.vector.reciprocal(xrec[:, 0:1], xsum[:, 0:1]))
                nc.vector.tensor_scalar(yl[:, :], yl[:, :], xrec[:, 0:1], None, ALU.mult).then_inc(yn_ready, 1)
                dve.wait_ge(yo_high, quad + 1)
                for k in range(KB):
                    (hi, src), (lo, _) = sample_out(quad, k, xhi), sample_out(quad, k, xlo)
                    last = nc.vector.tensor_tensor(lo, src, hi.bitcast(F32), ALU.subtract)
                last.then_inc(yo_taken, 1)

        gate_taken, up_taken, h_high, h_low = sem("gate_taken"), sem("up_taken"), sem("hidden_high"), sem("hidden_low")

        def ffn_tensor(pe, nb, n0, q0):
            def pair(i, first):
                for s in range(2):
                    pe.wait_ge(w_split, i * 2 + (n0 + s + 1))
                    if not first:
                        pe.wait_ge((gate_taken, up_taken)[s], i + q0)
                    products(s, (xhi, xlo), KB, CHUNKS).then_inc(z_ready, 1)
            if q0 == 0:
                pair(0, True)
            with pe.Fori(1 if q0 == 0 else 0, nb) as i:
                pair(i, False)

        def ffn_scalar(act, nb, n0, q0):
            def pair(i, s, first):
                act.wait_ge(z_ready, i * 4 + (n0 + 2 * s + 1))
                if not first:
                    act.wait_ge(h_low, i * 2 + (q0 + s - 1))
                for c, (t0, w) in enumerate(CHUNKS):
                    last = nc.scalar.activation(silu_g[:, s, t0:t0 + w], PS[:, c, 0:w], ACT.Silu)
                last.then_inc(gate_taken, 1)
                act.wait_ge(up_taken, i * 2 + (q0 + s + 1))
                nc.scalar.activation(ghi[:, bass.ds(i * 2 + s, 1), :], silu_g[:, s:s + 1, :], ACT.Copy).then_inc(h_high, 1)
            if q0 == 0:
                pair(0, 0, True)
                pair(0, 1, True)
            with act.Fori(1 if q0 == 0 else 0, nb // 2) as i:
                pair(i, 0, False)
                pair(i, 1, False)

        def ffn_vector(dve, nb, n0, q0):
            def split(i, s):
                for which in range(2):
                    split_block(dve, i * 2, which, n0 + 2 * s, KB)

            def combine(i, s):
                dve.wait_ge(z_ready, i * 4 + (n0 + 2 * s + 2))
                dve.wait_ge(gate_taken, i * 2 + (q0 + s + 1))
                for c, (t0, w) in enumerate(CHUNKS):
                    last = nc.vector.tensor_tensor(silu_g[:, s, t0:t0 + w], PS[:, 3 + c, 0:w], silu_g[:, s, t0:t0 + w], ALU.mult)
                last.then_inc(up_taken, 1)
                dve.wait_ge(h_high, i * 2 + (q0 + s + 1))
                nc.vector.tensor_tensor(glo[:, bass.ds(i * 2 + s, 1), :], silu_g[:, s:s + 1, :],
                                        ghi[:, bass.ds(i * 2 + s, 1), :].bitcast(F32), ALU.subtract).then_inc(h_low, 1)
            split(0, 0)
            with dve.Fori(0, nb // 2 - 1) as i:
                split(i, 1)
                combine(i, 0)
                split(i + 1, 0)
                combine(i, 1)
            split(nb // 2 - 1, 1)
            combine(nb // 2 - 1, 0)
            combine(nb // 2 - 1, 1)

        yst = cut(HB, 0, 4, D)
        y_turned, y_taken = sem("y_turned"), sem("y_taken")
        y_stored = [sem(f"y_stored{i}") for i in range(4)]

        def out_tensor(pe):
            for g in range(2 * TT):
                t, half = g // 2, g % 2
                n = P if t < TT - 1 else NS
                if g >= 4:
                    pe.wait_ge(y_taken, g - 3)
                for j in range(4):
                    mm = nc.tensor.transpose(PS[0:n, g % 4, j * P:(j + 1) * P], xn[:, 4 * half + j, t * P:t * P + n], IDENT[:, :])
                mm.then_inc(y_turned, 1)

        def out_scalar(act):
            for g in range(2 * TT):
                t, half = g // 2, g % 2
                n = P if t < TT - 1 else NS
                act.wait_ge(y_turned, g + 1)
                if t >= 4:
                    act.wait_ge(y_stored[t % 4], 16 * (t // 4))
                nc.scalar.activation(yst[0:n, t % 4, 512 * half:512 * half + 512], PS[0:n, g % 4, :], ACT.Copy).then_inc(y_taken, 1)

        def out_store(sp):
            yp = O["y_p"][0].rearrange("(t p) d -> p t d", p=P)
            for t in range(TT):
                sp.wait_ge(y_taken, 2 * t + 2)
                if t < TT - 1:
                    sp.dma_start(yp[:, t, :], yst[:, t % 4, :]).then_inc(y_stored[t % 4], 16)
                else:
                    sp.dma_start(O["y_s"].rearrange("b t d -> (b t) d"), yst[0:NS, t % 4, :]).then_inc(y_stored[t % 4], 16)
            for s in range(4):
                sp.wait_ge(y_stored[s], 16 * len(range(s, TT, 4)))

        cache_stored = sem("cache_stored")

        def cache_copy(act):
            for b in range(DB):
                for o, a in (("win_k_s", "cache_win_k"), ("win_v_s", "cache_win_v")):
                    act.dma_start(O[o][b, 0:PAST].rearrange("(p r) h d -> p (r h d)", p=P),
                                  A[a][b].rearrange("(p r) h d -> p (r h d)", p=P)).then_inc(cache_stored, 16)

        order = ["turn", "norm_x", "att_proj", "kv", "att", "ml_proj", "conv_state", "conv", "gates", "chunks", "sample",
                 "win", "mix_norm", "out", "mem_turn", "mem_norm", "mem_proj", "mkv", "cq_norm", "cq", "cross", "xsample", "co", "ffn_norm",
                 *(f"{x}{g}" for g in range(len(FGROUPS)) for x in ("ffn", "down")), "final_norm", "end"]
        PH = {name: i + 1 for i, name in enumerate(order)}
        groups = [(n, sum(FGROUPS[:g])) for g, n in enumerate(FGROUPS)]
        NB = {}
        count = 0
        for name, blocks in (("aq", 4), ("akv", 8), ("qk", 8), ("mv", 4), ("mo", 4), ("out", 8), ("mk", 8), ("mv2", 8), ("cq", 8),
                             ("co", 8), *((f"{x}{g}", 2 * n if x == "ffn" else KB) for g, n in enumerate(FGROUPS) for x in ("ffn", "down"))):
            NB[name] = count
            count += blocks
        MCH = ((0, NMEM),)
        J = {}
        j = 0
        for r, (name, nb) in enumerate((("x", 8), ("att", 4), ("ml", 4), ("mem", 8), ("cross", 8), ("ffn", 8), ("final", 8))):
            J[name] = (j, r, j)
            j += nb
        chains = {}

        block = ctx.enter_context(nc.Block())

        @block.sync
        def _(sp):
            load_inputs(sp)
            win = A["w_in"]
            proj_load(sp, [w_view(win, 0)], 4, NB["aq"])
            sp.wait_ge(phase_done, 4 * PH["turn"])
            sp.dma_start(XT_DRAM, XT0[:, :]).then_inc(xt_stored, 16)
            proj_load(sp, [w_view(win, AW)], 8, NB["akv"])
            sp.wait_ge(phase_done, 4 * PH["att_proj"])
            kv_store(sp)
            sp.wait_ge(phase_done, 4 * PH["kv"])
            att_load(sp)
            ml_loads(sp)
            sp.wait_ge(phase_done, 4 * PH["att"])
            proj_load(sp, [w_view(win, 3 * AW)], 8, NB["qk"])
            proj_load(sp, [w_view(win, 5 * AW)], 4, NB["mv"])
            proj_load(sp, [w_view(win, 6 * AW)], 4, NB["mo"])
            ml_tables(sp)
            conv_store(sp)
            m_store(sp)
            sp.wait_ge(phase_done, 4 * PH["gates"])
            sample_state_load(sp)
            state_store(sp)
            win_load(sp)
            mem_load(sp)
            proj_load(sp, [w_view(A["w_out"])], 8, NB["out"])
            proj_load(sp, [w_view(A["w_ck"])], 8, NB["mk"])
            proj_load(sp, [w_view(A["w_cv"])], 8, NB["mv2"])
            mkv_store(sp)
            proj_load(sp, [w_view(A["w_cq"])], 8, NB["cq"])
            xsample_load(sp)
            proj_load(sp, [w_view(A["w_co"])], 8, NB["co"])
            for g, (nb, q0) in enumerate(groups):
                proj_load(sp, [w_view(A[w], q0 * P) for w in ("w_gate", "w_up")], 2 * nb, NB[f"ffn{g}"])
                proj_load(sp, [w_view(A["w_down"], 0, q0 * P, nb)], KB, NB[f"down{g}"], nb)
            out_store(sp)
            sp.wait_ge(out_stored, 16 * stores[0])
            sp.wait_ge(cache_stored, 16 * 2 * DB)

        @block.tensor
        def _(pe):
            c = chains["pe"] = Chain(pe, None)
            turn_tensor(pe)
            c.meet()
            norm_tensor(pe, KB, N, *J["x"])
            c.meet()
            proj_tensor(pe, (xhi, xlo), 4, NB["aq"])
            proj_tensor(pe, (xhi, xlo), 8, NB["akv"])
            c.meet()
            kv_turn_tensor(pe)
            c.meet()
            att_tensor(pe)
            pe.wait_ge(o_taken, len(UNITS))
            att_turn_tensor(pe)
            c.meet()
            gates_tensor(pe)
            pe.wait_ge(gates_read, 1)
            proj_tensor(pe, (xhi, xlo), 8, NB["qk"])
            proj_tensor(pe, (xhi, xlo), 4, NB["mv"])
            proj_tensor(pe, (xhi, xlo), 4, NB["mo"])
            c.meet()
            conv_state_tensor(pe)
            c.meet()
            c.meet()
            k_turn_tensor(pe)
            pe.wait_ge(kt_taken, TT)
            gate_tensor(pe)
            c.meet()
            chunk_tensor(pe)
            c.meet()
            sample_tensor(pe)
            c.meet()
            win_tensor(pe)
            c.meet()
            norm_tensor(pe, 4, N, *J["att"])
            norm_tensor(pe, 4, N, *J["ml"])
            c.meet()
            proj_tensor(pe, (xhi, xlo), 8, NB["out"])
            c.meet()
            mem_turn_tensor(pe)
            c.meet()
            norm_tensor(pe, KB, NMEM, *J["mem"])
            c.meet()
            proj_tensor(pe, (mhi, mlo), 8, NB["mk"], MCH)
            proj_tensor(pe, (mhi, mlo), 8, NB["mv2"], MCH)
            c.meet()
            mkv_turn_tensor(pe)
            c.meet()
            norm_tensor(pe, KB, N, *J["cross"])
            c.meet()
            proj_tensor(pe, (xhi, xlo), 8, NB["cq"])
            c.meet()
            cross_tensor(pe)
            c.meet()
            xsample_tensor(pe)
            c.meet()
            proj_tensor(pe, (xhi, xlo), 8, NB["co"])
            c.meet()
            norm_tensor(pe, KB, N, *J["ffn"])
            c.meet()
            for g, (nb, q0) in enumerate(groups):
                ffn_tensor(pe, nb, NB[f"ffn{g}"], q0)
                c.meet()
                proj_tensor(pe, (ghi, glo), KB, NB[f"down{g}"], nk=nb, ffn_blocks=2 * (q0 + nb))
                c.meet()
            norm_tensor(pe, KB, N, *J["final"])
            c.meet()
            out_tensor(pe)
            c.meet()

        @block.scalar
        def _(act):
            c = chains["act"] = Chain(act, act_step)
            c.meet()
            norm_scalar(act, x0, xhi, KB, N, *J["x"])
            c.meet()
            proj_evac(act, aq, 4, NB["aq"], act_copy(HD ** -0.5))
            proj_evac(act, akv, 8, NB["akv"], act_copy())
            c.meet()
            kv_turn_scalar(act)
            c.meet()
            att_scalar(act)
            att_turn_scalar(act)
            c.meet()
            proj_evac(act, qk, 8, NB["qk"], act_copy())
            proj_evac(act, mv, 4, NB["mv"], act_copy())
            proj_evac(act, sig_o, 4, NB["mo"], act_copy())
            c.meet()
            conv_state_scalar(act)
            c.meet()
            conv_scalar(act)
            c.meet()
            gate_scalar(act)
            c.meet()
            chunk_scalar(act, range(NC))
            c.meet()
            chunk_scalar(act, [NC])
            c.meet()
            win_scalar(act)
            c.meet()
            norm_scalar(act, cat, xhi, 4, N, *J["att"])
            norm_scalar(act, cat[:, NP:, :], xhi[:, NP:, :], 4, N, *J["ml"])
            c.meet()
            c.meet()
            c.meet()
            norm_scalar(act, mem_T, mhi, KB, NMEM, *J["mem"])
            c.meet()
            proj_evac(act, mkT, 8, NB["mk"], act_copy(), MCH)
            proj_evac(act, mvT, 8, NB["mv2"], act_copy(), MCH)
            c.meet()
            mkv_turn_scalar(act)
            c.meet()
            norm_scalar(act, XT, xhi, KB, N, *J["cross"])
            c.meet()
            proj_evac(act, cq, 8, NB["cq"], act_copy(XD ** -0.5))
            c.meet()
            cross_scalar(act)
            c.meet()
            xsample_scalar(act)
            c.meet()
            c.meet()
            norm_scalar(act, XT, xhi, KB, N, *J["ffn"])
            c.meet()
            cache_copy(act)
            for g, (nb, q0) in enumerate(groups):
                ffn_scalar(act, nb, NB[f"ffn{g}"], q0)
                c.meet()
                c.meet()
            norm_scalar(act, XT, None, KB, N, *J["final"])
            c.meet()
            out_scalar(act)
            c.meet()

        @block.vector
        def _(dve):
            c = chains["dve"] = Chain(dve, dve_step)
            turn_vector(dve)
            c.meet()
            norm_vector(dve, x0, (xhi, xlo), KB, N, G_MIX, *J["x"])
            c.meet()
            proj_split(dve, 4, NB["aq"])
            proj_split(dve, 8, NB["akv"])
            c.meet()
            c.meet()
            att_vector(dve)
            c.meet()
            nc.vector.memset(gate_w[:, :, :], 0.0).then_inc(gw_zeroed, 1)
            gates_split(dve)
            gates_vector(dve)
            for part, blocks in (("qk", 8), ("mv", 4), ("mo", 4)):
                proj_split(dve, blocks, NB[part])
            c.meet()
            gate_bias_vector(dve)
            c.meet()
            conv_vector(dve)
            c.meet()
            k_turn_vector(dve)
            gate_vector(dve)
            c.meet()
            chunk_vector(dve)
            c.meet()
            sample_vector(dve)
            c.meet()
            win_vector(dve)
            c.meet()
            norm_vector(dve, cat, (xhi, xlo), 4, N, G_ATT, *J["att"])
            norm_vector(dve, cat[:, NP:, :], (xhi[:, NP:, :], xlo[:, NP:, :]), 4, N, G_ML, *J["ml"])
            c.meet()
            dve.wait_ge(xt_back, 16)
            proj_split_add(dve, XT, 8, NB["out"])
            c.meet()
            mem_turn_vector(dve)
            c.meet()
            norm_vector(dve, mem_T, (mhi, mlo), KB, NMEM, G_MEM, *J["mem"])
            c.meet()
            proj_split(dve, 8, NB["mk"])
            proj_split(dve, 8, NB["mv2"])
            c.meet()
            c.meet()
            norm_vector(dve, XT, (xhi, xlo), KB, N, G_CROSS, *J["cross"])
            c.meet()
            proj_split(dve, 8, NB["cq"])
            c.meet()
            cross_vector(dve)
            c.meet()
            xsample_vector(dve)
            c.meet()
            proj_split_add(dve, XT, 8, NB["co"])
            c.meet()
            norm_vector(dve, XT, (xhi, xlo), KB, N, G_FFN, *J["ffn"])
            c.meet()
            for g, (nb, q0) in enumerate(groups):
                ffn_vector(dve, nb, NB[f"ffn{g}"], q0)
                c.meet()
                proj_split_add(dve, XT, KB, NB[f"down{g}"], nb)
                c.meet()
            norm_vector(dve, XT, xn, KB, N, G_FINAL, *J["final"])
            c.meet()
            c.meet()

        @block.gpsimd
        def _(pool):
            c = chains["pool"] = Chain(pool, pool_step)
            for name in order:
                if name == "kv":
                    q_wide_pool(pool)
                elif name == "conv_state":
                    conv_state_pool(pool)
                elif name == "chunks":
                    sample_pool(pool)
                    chunk_pool(pool, range(NC))
                elif name == "sample":
                    q_mask_pool(pool)
                    chunk_pool(pool, [NC])
                elif name == "xsample":
                    xsample_pool(pool)
                c.meet()


_INS = ['x_prompt', 'x_sample', 'mem_prompt', 'cache_win_k', 'cache_win_v', 'cache_mem_k', 'cache_mem_v', 'state_conv',
        'state_mlstm_C', 'state_mlstm_n', 'state_mlstm_m', 'g_mix', 'w_in', 'conv_w', 'conv_b', 'b_ig', 'b_fg', 'b_og',
        'g_attn_out', 'g_mlstm_out', 'w_out', 'g_cross', 'g_mem', 'w_cq', 'w_ck', 'w_cv', 'w_co', 'g_ffn', 'w_gate', 'w_up',
        'w_down', 'g_final']
_OUTS = [('y_p', (1, SEQ, D)), ('y_s', (DB, DT, D)), ('win_k_p', (1, SEQ, H, HD)), ('win_v_p', (1, SEQ, H, HD)),
         ('conv_p', (1, 3, D)), ('C_p', (1, H, HD, HD)), ('n_p', (1, H, HD)), ('m_p', (1, H)),
         ('mem_k', (1, NMEM, XH, XD)), ('mem_v', (1, NMEM, XH, XD)), ('win_k_s', (DB, PAST + DT, H, HD)),
         ('win_v_s', (DB, PAST + DT, H, HD)), ('conv_s', (DB, 3, D)), ('C_s', (DB, H, HD, HD)), ('n_s', (DB, H, HD)),
         ('m_s', (DB, H))]


def kernel(**inputs):
    import concourse.bacc as _bacc
    from concourse.bass_utils import run_bass_kernel_spmd as _run

    nc = _bacc.Bacc("TRN2", target_bir_lowering=False, num_devices=1)
    arrays, ins, outs = {}, {}, {}
    given = {name: np.ascontiguousarray(inputs[name]) for name in _INS}
    given.update(constants())
    for name, a in given.items():
        arrays[f"in_{name}_dram"] = a
        ins[name] = nc.dram_tensor(f"in_{name}_dram", a.shape, F32, kind="ExternalInput").ap()
    for name, shape in _OUTS:
        outs[name] = nc.dram_tensor(f"out_{name}_dram", shape, F32, kind="ExternalOutput").ap()
    build(nc, ins, outs)
    r = _run(nc, [arrays], core_ids=[0])
    return tuple(r.results[0][f"out_{name}_dram"] for name, _ in _OUTS)
```

```python
from contextlib import ExitStack

import numpy as np

import concourse.bass as bass
from concourse import mybir

F32 = mybir.dt.float32
F32R = mybir.dt.float32r
ALU = mybir.AluOpType
ACT = mybir.ActivationFunctionType
AX_X = mybir.AxisListType.X

P = 128
D = 1024
KB = D // P
SEQ = 1024
DB, DT = 8, 8
NS = DB * DT
N = SEQ + NS
TT = 9
PAST = 1024
H, HD = 8, 64
NP = H // 2
AW = H * HD
NMEM, XH, XD = 256, 4, 256
FB = 22
FGROUPS = (6, 6, 6, 4)
D_FF = FB * P
EPS = 1e-6
NEG = -1e30
CHUNKS = ((0, 384), (384, 384), (768, 320))
NC = SEQ // P
G_MIX, G_CROSS, G_MEM, G_FFN, G_FINAL = 0, 8, 16, 24, 32
G_ATT, G_ML, CONV_W, CONV_B, B_OG, N_PAR = 40, 44, 48, 80, 88, 92


def constants():
    slopes = np.exp2(-8.0 * (np.arange(H) + 1.0) / H)

    def bias(delta):
        count = ((delta <= 128).astype(int) + ((delta <= 512) & (delta % 4 == 0))
                 + ((delta <= 2048) & (delta % 16 == 0))) * (delta >= 0)
        log_count = np.where(count > 0, np.log(np.maximum(count, 1)), 0.0)
        return [np.where(count > 0, -s * delta + log_count, NEG) for s in slopes]

    delta = np.arange(P)[:, None] + (SEQ - P) - np.arange(SEQ)[None]
    prompt_bias = np.stack(bias(delta))
    t = np.arange(DT)
    cache = np.stack(bias(PAST + t[:, None] - np.arange(PAST)[None])).reshape(AW // DT, PAST)
    new = np.stack(bias(t[:, None] - t[None])).reshape(H * DT, DT)
    sample_new = np.full((2, H * DT, DB // 2, DB, DT), NEG)
    for pair in range(DB // 2):
        for e in range(2):
            sample_new[e, :, pair, 2 * pair + e] = new
    s = np.arange(P)
    causal = np.where(s[:, None] <= s[None], 0.0, NEG)
    r = np.arange(NS)
    sample_causal = np.where((r[:, None] <= r[None]) & (r[:, None] // DT == r[None] // DT), 0.0, NEG)
    restart = np.ones((H, N))
    restart[:, 0:SEQ:P] = 0
    restart[:, SEQ::DT] = 0
    head = np.arange(H)
    c = {
        "ident": np.eye(P),
        "prompt_bias": prompt_bias,
        "sample_bias": np.concatenate([cache, cache]),
        "sample_new_bias": sample_new.reshape(P, DB // 2 * NS),
        "causal": causal,
        "sample_causal": sample_causal,
        "restart": restart,
        "head_sel": np.concatenate([np.repeat(np.eye(H), P, axis=1), np.zeros((P - H, H * P))]),
        "pair_sel": (head[:, None] == (2 * np.arange(NP)[:, None] + np.arange(P)[None] // HD).reshape(1, -1)),
        "batch_sel": r[:, None] // DT == np.arange(DB)[None],
    }
    return {k: np.ascontiguousarray(v, dtype=np.float32) for k, v in c.items()}


def build(nc, A, O):
    with ExitStack() as ctx:
        def sem(name):
            return ctx.enter_context(nc.semaphore(name))

        PS = ctx.enter_context(nc.psum_tensor("psum", [P, 8, 512], F32))

        BASE = 16512
        AT = {"ident": 0, "ones": 128, "params_T": 256, "eps": 352, "small": 360, "sample_q_wide": 512,
              "sample_k_new": 2560, "sample_v_new": 2816, "scratch": 3328, "weights": 7680, "x_hi": 13824, "x_lo": 22528,
              "wide": 31232, "end": 52992}

        def sb(name, *shape, at=None, dt=F32):
            at = AT[name] if at is None else at
            return nc.alloc_sbuf_tensor_at(name, list(shape), dt, offset=BASE + 4 * at)

        HB = sb("wide", P, AT["end"] - AT["wide"])
        XT0 = sb("residual_T_first", P, KB * N, at=AT["wide"])
        BIG = KB * N
        XTF = sb("residual_T", P, KB * N, at=AT["wide"] + BIG + 4352)
        XHI, XLO = (sb(n, P, KB * N, dt=F32R) for n in ("x_hi", "x_lo"))
        XN = sb("work_1", P, KB * N, at=AT["x_hi"])
        XW = sb("work_2", P, KB * N, at=AT["x_lo"])
        WRT = sb("weights_work", P, 6144, at=AT["weights"])
        RAW = sb("weights_raw", P, 2 * KB * P, at=AT["weights"])
        WHI = sb("weights_hi", P, 2 * KB * P, at=AT["weights"] + 2 * KB * P, dt=F32R)
        WLO = sb("weights_lo", P, 2 * KB * P, at=AT["weights"] + 4 * KB * P, dt=F32R)
        GHI = sb("hidden_hi", P, 6 * N, at=AT["wide"], dt=F32R)
        GLO = sb("hidden_lo", P, 6 * N, at=AT["wide"] + 6 * N, dt=F32R)
        SC = sb("scratch", P, 4352)
        IDENT = sb("ident", P, P)
        ONES = sb("ones", P, P)
        PAR = sb("params_T", P, N_PAR)
        EPSC = sb("eps", P, 1)
        QX = sb("sample_q_wide", P, NP, DB, NS)
        KNEW = sb("sample_k_new", P, NP, NS)
        VNEW = sb("sample_v_new", NS, AW)
        SMALL = sb("small", P, 96)
        XT_DRAM = nc.dram_tensor("residual_T_dram", [P, KB * N], F32, kind="Internal").ap()

        def cut(t, start, *shape):
            n = int(np.prod(shape))
            v = t[:, start:start + n]
            if len(shape) == 2:
                return v.rearrange("p (a b) -> p a b", b=shape[1])
            if len(shape) == 3:
                return v.rearrange("p (a b c) -> p a b c", b=shape[1], c=shape[2])
            return v

        XT = cut(XTF, 0, KB, N)
        x0 = cut(XT0, 0, KB, N)
        xn = cut(XN, 0, KB, N)
        xhi, xlo = cut(XHI, 0, KB, N), cut(XLO, 0, KB, N)
        cat = cut(HB, 0, KB, N)
        raw = cut(RAW, 0, 2, KB, P)
        whi, wlo = cut(WHI, 0, 2, KB, P), cut(WLO, 0, 2, KB, P)
        ghi, glo = cut(GHI, 0, 6, N), cut(GLO, 0, 6, N)
        nsq = cut(SC, 0, 2, N)
        nacc = cut(SC, 2 * N, N)
        nr = cut(SC, 3 * N, N)
        silu_g = cut(SC, 0, 2, N)

        phase_done = sem("phase_done")
        act_step, dve_step, pool_step = sem("act_step"), sem("dve_step"), sem("pool_step")
        w_landed = [sem(f"w_landed{i}") for i in range(2)]
        w_high, w_split = sem("w_high"), sem("w_split")
        n_high, n_half, n_low = sem("norm_high"), sem("norm_product"), sem("norm_low")
        z_ready, z_taken = sem("z_ready"), sem("z_taken")
        sq_ready, sq_summed, bcast_ready, rnorm_ready, norm_done = (
            sem("sq_ready"), sem("sq_summed"), sem("bcast_ready"), sem("rnorm_ready"),
            sem("norm_done"))
        par_landed, x_turned, x_taken = sem("par_landed"), sem("x_turned"), sem("x_taken")
        x_landed = [sem(f"x_landed{i}") for i in range(3)]
        out_stored = sem("out_stored")
        stores = [0]

        def stored(ins):
            ins.then_inc(out_stored, 16)
            stores[0] += 1

        class Chain:

            def __init__(self, eng, s):
                self.eng, self.sem, self.n, self.phase = eng, s, 0, 0

            def __call__(self, ins):
                self.n += 1
                ins.then_inc(self.sem, 1)
                self.eng.wait_ge(self.sem, self.n)

            def meet(self):
                self.phase += 1
                self.eng.drain().then_inc(phase_done, 1)
                self.eng.wait_ge(phase_done, 4 * self.phase)

        def w_view(w, c0=0, r0=0, nk=KB):
            return w[r0:r0 + nk * P, :].rearrange("(k p) n -> p k n", p=P)[:, :, c0:]

        def proj_load(sp, views, blocks, n0, nk=KB):
            m = len(views)

            def block(i, s):
                c = i * 2 + s if m == 1 else i
                sp.dma_start(raw[:, s, 0:nk], views[s % m][:, :, bass.ds(c * P, P)]).then_inc(w_landed[s], 16)
            if n0 == 0:
                block(0, 0)
                block(0, 1)
            with sp.Fori(1 if n0 == 0 else 0, blocks // 2) as i:
                for s in range(2):
                    sp.wait_ge(w_split, i * 2 + (n0 + s - 1))
                    block(i, s)

        def split_block(dve, i, s, n0, nk, first=False):
            dve.wait_ge(w_landed[s], i * 16 + (16 * (n0 // 2) + 16))
            if not first:
                dve.wait_ge(z_ready, i * 2 + (n0 + s - 1))
            nc.vector.tensor_copy(whi[:, s, 0:nk, :], raw[:, s, 0:nk, :]).then_inc(w_high, 1)
            dve.wait_ge(w_high, i * 2 + (n0 + s + 1))
            nc.vector.tensor_tensor(wlo[:, s, 0:nk, :], raw[:, s, 0:nk, :], whi[:, s, 0:nk, :].bitcast(F32), ALU.subtract)\
                .then_inc(w_split, 1)

        def split_first(dve, n0, nk=KB):
            split_block(dve, 0, 0, n0, nk, n0 == 0)
            split_block(dve, 0, 1, n0, nk, n0 == 0)

        def proj_split(dve, blocks, n0, start=0):
            with dve.Fori(start, blocks // 2) as i:
                split_block(dve, i, 0, n0, KB)
                split_block(dve, i, 1, n0, KB)

        def proj_split_add(dve, dst, blocks, n0, nk=KB, split_next=lambda: None):
            def add(i, s):
                dve.wait_ge(z_ready, i * 2 + (n0 + s + 1))
                for c, (t0, w) in enumerate(CHUNKS):
                    out = dst[:, bass.ds(i * 2 + s, 1), t0:t0 + w]
                    last = nc.vector.tensor_tensor(out, PS[:, 3 * s + c:3 * s + c + 1, 0:w], out, ALU.add)
                last.then_inc(z_taken, 1)
            with dve.Fori(0, blocks // 2 - 1) as i:
                for s in range(2):
                    split_block(dve, i, s, n0 + 2, nk)
                    add(i, s)
            split_next()
            add(blocks // 2 - 1, 0)
            add(blocks // 2 - 1, 1)

        def products(s, x, nk, chunks, before=lambda k: None):
            for k in range(nk):
                before(k)
                for w, part in ((whi, 0), (whi, 1), (wlo, 0)):
                    for c, (t0, n) in enumerate(chunks):
                        mm = nc.tensor.matmul(PS[:, 3 * s + c, 0:n], w[:, s, k], x[part][:, k, t0:t0 + n],
                                              start=(k == 0 and w is whi and part == 0), stop=(k == nk - 1 and w is wlo))
            return mm

        def proj_tensor(pe, x, blocks, n0, chunks=CHUNKS, nk=KB, ffn_blocks=0, before_first=None):
            def block(i, s, first, before=lambda k: None):
                pe.wait_ge(w_split, i * 2 + (n0 + s + 1))
                if not first:
                    pe.wait_ge(z_taken, i * 2 + (n0 - ffn_blocks + s - 1))
                products(s, x, nk, chunks, before).then_inc(z_ready, 1)
            peel = n0 == 0 or before_first is not None
            if peel:
                block(0, 0, n0 == 0, before_first or (lambda k: None))
                block(0, 1, n0 == 0)
            with pe.Fori(1 if peel else 0, blocks // 2) as i:
                block(i, 0, False)
                block(i, 1, False)

        def evac_block(act, dst, i, s, n0, scale=1.0, chunks=CHUNKS):
            act.wait_ge(z_ready, i * 2 + (n0 + s + 1))
            for c, (t0, w) in enumerate(chunks):
                last = nc.scalar.activation(dst[:, bass.ds(i * 2 + s, 1), t0:t0 + w], PS[:, 3 * s + c:3 * s + c + 1, 0:w],
                                            ACT.Copy, scale=scale)
            last.then_inc(z_taken, 1)

        def proj_evac(act, dst, blocks, n0, scale=1.0, chunks=CHUNKS):
            with act.Fori(0, blocks // 2) as i:
                evac_block(act, dst, i, 0, n0, scale, chunks)
                evac_block(act, dst, i, 1, n0, scale, chunks)

        def norm_scalar(act, src, hi, nb, cols, j0, r0, s0):
            if r0:
                act.wait_ge(norm_done, r0)
            for k in range(nb):
                if j0 + k >= 2:
                    act.wait_ge(sq_summed, j0 + k - 1)
                nc.scalar.activation(nsq[:, (j0 + k) % 2, 0:cols], src[:, k, 0:cols], ACT.Square).then_inc(sq_ready, 1)
            act.wait_ge(bcast_ready, r0 + 1)
            chain = chains["act"]
            for c, (t0, w) in enumerate(CHUNKS):
                w = min(w, cols - t0)
                if w > 0:
                    last = nc.scalar.activation(nr[:, t0:t0 + w], PS[:, c, 0:w], ACT.Ln, bias=EPSC[:, 0:1],
                                                scale=1.0 / (nb * P))
            chain(last)
            nc.scalar.activation(nr[:, 0:cols], nr[:, 0:cols], ACT.Exp, scale=-0.5).then_inc(rnorm_ready, 1)
            if hi is not None:
                for k in range(nb):
                    act.wait_ge(n_half, s0 + k + 1)
                    nc.scalar.activation(hi[:, k, 0:cols], nsq[:, k % 2, 0:cols], ACT.Copy).then_inc(n_high, 1)

        def norm_vector(dve, src, dst, nb, cols, gain, j0, r0, s0, meanwhile=lambda: None):
            for k in range(nb):
                dve.wait_ge(sq_ready, j0 + k + 1)
                if k:
                    dve.wait_ge(sq_summed, j0 + k)
                    nc.vector.tensor_tensor(nacc[:, 0:cols], nacc[:, 0:cols], nsq[:, (j0 + k) % 2, 0:cols],
                                            ALU.add).then_inc(sq_summed, 1)
                else:
                    nc.vector.tensor_copy(nacc[:, 0:cols], nsq[:, (j0 + k) % 2, 0:cols]).then_inc(sq_summed, 1)
            meanwhile()
            dve.wait_ge(rnorm_ready, r0 + 1)

            def scaled(k, out):
                return nc.vector.scalar_tensor_tensor(out=out, in0=src[:, k, 0:cols], scalar=PAR[:, gain + k:gain + k + 1],
                                                      in1=nr[:, 0:cols], op0=ALU.mult, op1=ALU.mult)
            if not isinstance(dst, tuple):
                for k in range(nb):
                    last = scaled(k, dst[:, k, 0:cols])
                last.then_inc(norm_done, 1)
                return
            hi, lo = dst
            dve.wait_ge(sq_summed, j0 + nb)
            for k in range(nb + 1):
                if k < nb:
                    if k >= 2:
                        dve.wait_ge(n_low, s0 + k - 1)
                    scaled(k, nsq[:, k % 2, 0:cols]).then_inc(n_half, 1)
                if k:
                    dve.wait_ge(n_high, s0 + k)
                    nc.vector.tensor_tensor(lo[:, k - 1, 0:cols], nsq[:, (k - 1) % 2, 0:cols], hi[:, k - 1, 0:cols].bitcast(F32),
                                            ALU.subtract).then_inc(n_low, 1)
            dve.wait_ge(n_low, s0 + nb)
            nc.vector.memset(SMALL[:, 41:42], 0.0).then_inc(norm_done, 1)

        def norm_tensor(pe, nb, cols, j0, r0, s0):
            pe.wait_ge(sq_summed, j0 + nb)
            if r0:
                pe.wait_ge(rnorm_ready, r0)
            for c, (t0, w) in enumerate(CHUNKS):
                w = min(w, cols - t0)
                if w > 0:
                    mm = nc.tensor.matmul(PS[:, c, 0:w], ONES[:, :], nacc[:, t0:t0 + w], start=True, stop=True)
            mm.then_inc(bcast_ready, 1)

        def normed(pe, r0, s0):
            def before(k):
                if k == 0:
                    pe.wait_ge(rnorm_ready, r0 + 1)
                pe.wait_ge(n_low, s0 + k + 1)
            return before

        xs = cut(HB, BIG, TT, D)
        par_rows = cut(SC, 0, P)

        def load_inputs(sp):
            sp.dma_start(IDENT[:, :], A["ident"]).then_inc(x_landed[0], 16)
            xp = A["x_prompt"][0].rearrange("(t p) d -> p t d", p=P)
            for t in range(TT - 1):
                sp.dma_start(xs[:, t, :], xp[:, t, :]).then_inc(x_landed[t // 3], 16)
            sp.dma_start(xs[0:NS, TT - 1, :], A["x_sample"].rearrange("b t d -> (b t) d")).then_inc(x_landed[2], 16)
            row = lambda a: a.rearrange("(k p) -> k p", p=P)
            for a, r, n in (("g_mix", G_MIX, 8), ("g_cross", G_CROSS, 8), ("g_mem", G_MEM, 8), ("g_ffn", G_FFN, 8),
                            ("g_final", G_FINAL, 8), ("g_attn_out", G_ATT, 4), ("g_mlstm_out", G_ML, 4),
                            ("conv_b", CONV_B, 8), ("b_og", B_OG, 4)):
                sp.dma_start(par_rows[r:r + n, :], row(A[a])).then_inc(par_landed, 16)
            sp.dma_start(par_rows[CONV_W:CONV_W + 32, :], A["conv_w"].rearrange("j (k p) -> (j k) p", p=P)).then_inc(par_landed, 16)

        def turn_tensor(pe):
            for g in range(2 * TT):
                t, half = g // 2, g % 2
                n = P if t < TT - 1 else NS
                pe.wait_ge(x_landed[t // 3], 16 * (4 if t < 3 else 3))
                if g >= 4:
                    pe.wait_ge(x_taken, g - 3)
                for j in range(4):
                    mm = nc.tensor.transpose(PS[:, g % 4, j * P:j * P + n], xs[0:n, t, (4 * half + j) * P:(4 * half + j + 1) * P],
                                             IDENT[0:n, 0:n])
                mm.then_inc(x_turned, 1)
            pe.wait_ge(par_landed, 16 * 10)
            nc.tensor.transpose(PS[:, 4, 0:N_PAR], par_rows[0:N_PAR, :], IDENT[0:N_PAR, 0:N_PAR]).then_inc(x_turned, 1)

        def turn_vector(dve):
            chains["dve"](nc.vector.memset(EPSC[:, :], EPS))
            nc.vector.memset(ONES[:, :], 1.0)
            for g in range(2 * TT):
                t, half = g // 2, g % 2
                n = P if t < TT - 1 else NS
                dve.wait_ge(x_turned, g + 1)
                nc.vector.tensor_copy(x0[:, 4 * half:4 * half + 4, t * P:t * P + n],
                                      PS[:, g % 4, :].rearrange("p (j n) -> p j n", j=4)[:, :, 0:n]).then_inc(x_taken, 1)
            dve.wait_ge(x_turned, 2 * TT + 1)
            nc.vector.tensor_copy(PAR[:, :], PS[:, 4, 0:N_PAR])

        cache_stored = sem("cache_stored")

        def cache_copy(eng, b, which):
            o, a = (("win_k_s", "cache_win_k"), ("win_v_s", "cache_win_v"))[which]
            eng.dma_start(O[o][b, 0:PAST].rearrange("(p r) h d -> p (r h d)", p=P),
                          A[a][b].rearrange("(p r) h d -> p (r h d)", p=P)).then_inc(cache_stored, 16)

        aq, ak, av = (cut(HB, BIG + j * NP * N, NP, N) for j in range(3))
        akv = cut(HB, BIG + NP * N, 2 * NP, N)
        vtok = cut(HB, NP * N, TT - 1, AW)
        xt_stored, xt_back = sem("xt_stored"), sem("xt_back")
        AW0 = BIG + 2 * NP * N
        att_tok = cut(HB, AW0, NC, AW)
        bias_tab = cut(WRT, 4096, 2, SEQ)
        logit = cut(SC, 0, 3, SEQ)
        prob_T = cut(SC, 3 * SEQ, SEQ), cut(WRT, 2048, SEQ)
        k_stage = cut(WRT, 0, 4, AW)
        q_pad = cut(HB, 0, 2, SEQ)
        kv_turned, kv_taken, q_padded = sem("kv_turned"), sem("kv_taken"), sem("q_padded")
        k_stored = [sem(f"k_stored{i}") for i in range(4)]

        def kv_turn_tensor(pe):
            for g in range(2 * TT):
                t, which = g // 2, g % 2
                n = P if t < TT - 1 else NS
                if g >= 4:
                    pe.wait_ge(kv_taken, g - 3)
                for j in range(NP):
                    mm = nc.tensor.transpose(PS[0:n, g % 4, j * P:(j + 1) * P], akv[:, NP * which + j, t * P:t * P + n], IDENT[:, :])
                mm.then_inc(kv_turned, 1)

        def kv_turn_scalar(act):
            act.wait_ge(xt_stored, 16)
            for g in range(2 * TT):
                t, which = g // 2, g % 2
                n = P if t < TT - 1 else NS
                act.wait_ge(kv_turned, g + 1)
                if which == 0:
                    if t >= 4:
                        act.wait_ge(k_stored[t % 4], 16 * (t // 4))
                    out = k_stage[0:n, t % 4, :]
                else:
                    out = vtok[:, t, :] if t < TT - 1 else VNEW[:, :]
                nc.scalar.activation(out, PS[0:n, g % 4, :], ACT.Copy).then_inc(kv_taken, 1)

        def kv_store(sp):
            wk, wv = (O[n][0].rearrange("(t p) h d -> p t (h d)", p=P) for n in ("win_k_p", "win_v_p"))
            for t in range(TT):
                sp.wait_ge(kv_taken, 2 * t + 1)
                if t < TT - 1:
                    sp.dma_start(wk[:, t, :], k_stage[:, t % 4, :]).then_inc(k_stored[t % 4], 16)
                    sp.wait_ge(kv_taken, 2 * t + 2)
                    stored(sp.dma_start(wv[:, t, :], vtok[:, t, :]))
                else:
                    sp.wait_ge(kv_taken, 2 * t + 2)
                    for b in range(DB):
                        rows = slice(b * DT, (b + 1) * DT)
                        sp.dma_start(O["win_k_s"][b, PAST:PAST + DT].rearrange("t h d -> t (h d)"),
                                     k_stage[rows, t % 4, :]).then_inc(k_stored[t % 4], 16)
                        stored(sp.dma_start(O["win_v_s"][b, PAST:PAST + DT].rearrange("t h d -> t (h d)"), VNEW[rows, :]))
            for i in range(4):
                sp.wait_ge(k_stored[i], 16 * (len(range(i, TT - 1, 4)) + (DB if i == (TT - 1) % 4 else 0)))

        def q_wide_pool(pool):
            chains["pool"](nc.gpsimd.memset(QX[:, :, :, :], 0.0))
            for e in range(2):
                rows = slice(HD * e, HD * e + HD)
                for p in range(NP):
                    h = 2 * p + e
                    chains["pool"](nc.gpsimd.tensor_copy(QX[rows, p, :, h * DT:(h + 1) * DT],
                                                         aq[rows, p, SEQ:N].rearrange("p (b t) -> p b t", t=DT)))
            chains["pool"](nc.gpsimd.tensor_copy(KNEW[:, :, :], ak[:, :, SEQ:N]))
            pool.wait_ge(xt_stored, 16)
            for h in range(2):
                other = HD * (1 - h)
                chains["pool"](nc.gpsimd.memset(q_pad[other:other + HD, h], 0.0))
            pad_q(0)
            pad_q(1)

        def pad_q(h):
            rows = slice(HD * (h % 2), HD * (h % 2) + HD)
            ins = nc.gpsimd.tensor_copy(q_pad[rows, h % 2], aq[rows, h // 2, 0:SEQ]).then_inc(q_padded, 1)
            chains["pool"].eng.wait_ge(q_padded, h + 1)
            return ins

        def att_pool(pool):
            for h in range(2, H):
                pool.wait_ge(s_ready, (h - 1) * NC)
                pad_q(h)

        tab_landed = [sem(f"tab_landed{i}") for i in range(2)]
        s_ready, logit_ready, prob_ready, pt_ready, pt_taken, o_ready, o_taken = (
            sem("s_ready"), sem("logit_ready"), sem("prob_ready"), sem("pt_ready"),
            sem("pt_taken"), sem("o_ready"), sem("o_taken"))
        UNITS = [(h, qb) for h in range(H) for qb in range(NC)]
        GROUPS = [(u, g) for u, (h, qb) in enumerate(UNITS) for g in range((qb + 4) // 4)]
        after = {u: sum(1 for v, _ in GROUPS if v <= u) for u in range(len(UNITS))}

        def att_load(sp):
            for h in range(H):
                if h >= 2:
                    sp.wait_ge(logit_ready, (h - 1) * NC)
                sp.dma_start(bias_tab[:, h % 2, :], A["prompt_bias"][h]).then_inc(tab_landed[h % 2], 16)
                if h:
                    cache_copy(sp, h - 1, 0)
            cache_copy(sp, H - 1, 0)

        def att_tensor(pe):
            def scores(u):
                h, qb = UNITS[u]
                if qb == 0:
                    pe.wait_ge(q_padded, h + 1)
                if u >= 2:
                    pe.wait_ge(logit_ready, u - 1)
                for g in range((qb + 4) // 4):
                    w = min(4, qb + 1 - 4 * g) * P
                    mm = nc.tensor.matmul(PS[:, 2 * (u % 2) + g, 0:w], q_pad[:, h % 2, qb * P:(qb + 1) * P],
                                          ak[:, h // 2, 512 * g:512 * g + w], start=True, stop=True)
                mm.then_inc(s_ready, 1)

            def turn(u):
                h, qb = UNITS[u]
                pe.wait_ge(prob_ready, u + 1)
                for g in range((qb + 4) // 4):
                    n = after[u - 1] + g if u else g
                    if n >= 2:
                        pe.wait_ge(pt_taken, n - 1)
                    for j in range(min(4, qb + 1 - 4 * g)):
                        mm = nc.tensor.transpose(PS[:, 4 + n % 2, j * P:(j + 1) * P],
                                                 logit[:, u % 3, (4 * g + j) * P:(4 * g + j + 1) * P], IDENT[:, :])
                    mm.then_inc(pt_ready, 1)

            def values(u):
                h, qb = UNITS[u]
                pe.wait_ge(pt_taken, after[u])
                if u >= 2:
                    pe.wait_ge(o_taken, u - 1)
                for j in range(qb + 1):
                    mm = nc.tensor.matmul(PS[:, 6 + u % 2, 0:HD], prob_T[u % 2][:, j * P:(j + 1) * P],
                                          vtok[:, j, h * HD:(h + 1) * HD], start=(j == 0), stop=(j == qb))
                mm.then_inc(o_ready, 1)

            for u in range(len(UNITS) + 2):
                if u < len(UNITS):
                    scores(u)
                if 1 <= u <= len(UNITS):
                    turn(u - 1)
                if u >= 2:
                    values(u - 2)

        amax, asum, arec, negm = (SMALL[:, 4 * i:4 * i + 4] for i in range(4))

        def att_vector(dve):
            def finish(u):
                h, qb = UNITS[u]
                i = u % 4
                dve.wait_ge(prob_ready, u + 1)
                chains["dve"](nc.vector.reciprocal(arec[:, i:i + 1], asum[:, i:i + 1]))
                dve.wait_ge(o_ready, u + 1)
                nc.vector.tensor_scalar(att_tok[:, qb, h * HD:(h + 1) * HD], PS[:, 6 + u % 2, 0:HD],
                                        arec[:, i:i + 1], None, ALU.mult).then_inc(o_taken, 1)
            for u, (h, qb) in enumerate(UNITS):
                w, i = (qb + 1) * P, u % 4
                dve.wait_ge(s_ready, u + 1)
                dve.wait_ge(tab_landed[h % 2], 16 * (h // 2 + 1))
                if u >= 3:
                    dve.wait_ge(pt_ready, after[u - 3])
                chains["dve"](nc.vector.tensor_tensor_reduce(
                    logit[:, u % 3, 0:w], PS[:, 2 * (u % 2):2 * (u % 2) + 2, :].rearrange("p a b -> p (a b)")[:, 0:w],
                    bias_tab[:, h % 2, SEQ - w:SEQ], 1.0, 3 * NEG, ALU.add, ALU.max, amax[:, i:i + 1]))
                nc.vector.tensor_scalar(negm[:, i:i + 1], amax[:, i:i + 1], -1.0, None, ALU.mult).then_inc(logit_ready, 1)
                if u >= 2:
                    finish(u - 2)
            finish(len(UNITS) - 2)
            finish(len(UNITS) - 1)

        def att_scalar(act):
            def take(u):
                h, qb = UNITS[u]
                for g in range((qb + 4) // 4):
                    n = after[u - 1] + g if u else g
                    w = min(4, qb + 1 - 4 * g) * P
                    act.wait_ge(pt_ready, n + 1)
                    if g == 0 and u >= 2:
                        act.wait_ge(o_ready, u - 1)
                    nc.scalar.activation(prob_T[u % 2][:, 512 * g:512 * g + w], PS[:, 4 + n % 2, 0:w], ACT.Copy).then_inc(pt_taken, 1)
            for u, (h, qb) in enumerate(UNITS):
                w, i = (qb + 1) * P, u % 4
                act.wait_ge(logit_ready, u + 1)
                if u >= 4:
                    act.wait_ge(o_taken, u - 3)
                nc.scalar.activation(logit[:, u % 3, 0:w], logit[:, u % 3, 0:w], ACT.Exp, bias=negm[:, i:i + 1],
                                     accum_out=asum[:, i:i + 1]).then_inc(prob_ready, 1)
                if u >= 1:
                    take(u - 1)
            take(len(UNITS) - 1)

        at_turned, at_taken = sem("at_turned"), sem("at_taken")

        def att_turn_tensor(pe):
            for t in range(NC):
                if t >= 4:
                    pe.wait_ge(at_taken, t - 3)
                for j in range(NP):
                    mm = nc.tensor.transpose(PS[:, t % 4, j * P:(j + 1) * P], att_tok[:, t, j * P:(j + 1) * P], IDENT[:, :])
                mm.then_inc(at_turned, 1)

        def att_turn_scalar(act):
            for t in range(NC):
                act.wait_ge(at_turned, t + 1)
                nc.scalar.activation(cat[:, 0:NP, t * P:(t + 1) * P], PS[:, t % 4, :].rearrange("p (j n) -> p j n", j=NP),
                                     ACT.Copy).then_inc(at_taken, 1)

        qk = cut(HB, BIG, 2 * NP, N)
        mv = cut(HB, BIG + 2 * NP * N, NP, N)
        sig_o = cat[:, NP:2 * NP, :]
        V1W = HD + 1
        WIDE = 96
        VPAD = 32
        v1 = cut(XN, VPAD, TT, H * V1W)
        v1_flat = cut(XN, 0, VPAD + TT * H * V1W)
        ML0 = VPAD + TT * H * V1W
        head_sel = cut(XN, ML0, H, P)
        pair_sel = cut(XN, ML0 + 1024, NP, P)
        causal = cut(XN, ML0 + 1536, P)
        sample_causal = cut(XN, ML0 + 1664, NS)
        restart = cut(XN, ML0 + 1728, N)
        batch_sel = cut(XN, ML0 + 2816, DB)
        cols = cut(XN, ML0 + 2824, TT, 4, H)
        colx = cut(XN, ML0 + 3112, TT, 3, H)
        dec = cut(XN, ML0 + 3328, NP, NC + DB)
        bgate = cut(XN, ML0 + 3392, 2)
        mrow = cut(XN, ML0 + 3404, NC + DB)
        dkrow = cut(XN, ML0 + 3420, NC + DB)
        m_out = cut(XN, ML0 + 3436, DB + 1)
        ktok = cut(XW, 0, TT, AW)
        gate_w = cut(SC, 0, KB, P)
        g_raw = [cut(SC, (1 + j) * N, N) for j in range(2)]
        gb, gm, gw = (cut(SC, j * N, N) for j in range(3))
        gu = cut(XW, TT * AW, N)
        rows4 = cut(WRT, 0, N)
        gi, gf = cut(WRT, N, N), cut(WRT, 2 * N, N)
        conv_acc = cut(SC, 0, N), cut(SC, 3 * N, N)
        conv_tail = SMALL[:, 72:96].rearrange("p (k j) -> p k j", k=KB)
        conv_s = cut(XW, 1728, KB, DB, DT)
        tail_stage = cut(WRT, 3 * N, D)
        conv_x = cut(XW, 0, KB, DB, 11)
        state_rows = cut(XW, 704, D)
        mrows_stage = cut(WRT, 0, D)

        gw_landed, gate_ready, ml_landed = sem("gw_landed"), sem("gate_ready"), sem("ml_landed")

        def ml_loads(sp):
            sp.wait_ge(phase_done, 4 * PH["att"])
            sp.wait_ge(gw_zeroed, 1)
            wv = w_view(A["w_in"])
            with nc.allow_non_contiguous_dma(reason="sixteen gate columns"):
                sp.dma_start(gate_w[:, :, 0:8], wv[:, :, 3584:3592]).then_inc(gw_landed, 16)
                sp.dma_start(gate_w[:, :, 32:40], wv[:, :, 3592:3600]).then_inc(gw_landed, 16)

        def ml_tables(sp):
            sp.wait_ge(phase_done, 4 * PH["ml_proj"])
            with nc.allow_non_contiguous_dma(reason="small tables and columns"):
                for dst, src in ((head_sel.rearrange("p a b -> p (a b)"), A["head_sel"]),
                                 (pair_sel[0:H].rearrange("p a b -> p (a b)"), A["pair_sel"]),
                                 (causal, A["causal"]), (sample_causal[0:NS], A["sample_causal"]),
                                 (restart[0:H], A["restart"]), (batch_sel[0:NS], A["batch_sel"]),
                                 (bgate[0:H, 0:1], A["b_ig"].rearrange("(a b) -> a b", b=1)),
                                 (bgate[0:H, 1:2], A["b_fg"].rearrange("(a b) -> a b", b=1)),
                                 (mrow[0:H, NC:NC + DB], A["state_mlstm_m"].rearrange("b h -> h b")),
                                 (state_rows[0:DB * 3], A["state_conv"].rearrange("b j c -> (b j) c"))):
                    sp.dma_start(dst, src).then_inc(ml_landed, 16)

        gw_zeroed, gw_high, gw_split = sem("gw_zeroed"), sem("gw_high"), sem("gw_split")

        def gates_split(dve):
            dve.wait_ge(gw_landed, 32)
            nc.vector.tensor_copy(whi[:, 0], gate_w).then_inc(gw_high, 1)
            dve.wait_ge(gw_high, 1)
            nc.vector.tensor_tensor(wlo[:, 0], gate_w, whi[:, 0].bitcast(F32), ALU.subtract).then_inc(gw_split, 1)

        def gates_tensor(pe):
            pe.wait_ge(gw_split, 1)
            products(0, (xhi, xlo), KB, CHUNKS).then_inc(gate_ready, 1)

        def gates_vector(dve):
            dve.wait_ge(gate_ready, 1)
            for c, (t0, w) in enumerate(CHUNKS):
                nc.vector.tensor_copy(g_raw[0][0:H, t0:t0 + w], PS[0:H, c, 0:w])
                last = nc.vector.tensor_copy(g_raw[1][0:H, t0:t0 + w], PS[32:32 + H, c, 0:w])
            last.then_inc(gates_read, 1)

        gates_read = sem("gates_read")

        def gate_bias_vector(dve):
            dve.wait_ge(ml_landed, 160)
            for j, g in enumerate((gi, gf)):
                nc.vector.tensor_scalar(g[0:H], g_raw[j][0:H], bgate[0:H, j:j + 1], None, ALU.add)

        ct_turned, ct_taken = sem("ct_turned"), sem("ct_taken")

        def conv_state_tensor(pe):
            pe.wait_ge(ml_landed, 160)
            for g in range(TT + 5):
                if g >= 4:
                    pe.wait_ge(ct_taken, g - 3)
                n = P if g != TT - 1 else NS
                for j in range(NP):
                    if g < TT:
                        mm = nc.tensor.transpose(PS[0:n, g % 4, j * P:(j + 1) * P], mv[:, j, g * P:g * P + n], IDENT[:, :])
                    elif g < TT + 2:
                        mm = nc.tensor.transpose(PS[0:NS, g % 4, j * P:(j + 1) * P], qk[:, 4 * (g - TT) + j, SEQ:N], IDENT[:, :])
                    elif g < TT + 4:
                        mm = nc.tensor.transpose(PS[0:3, g % 4, j * P:(j + 1) * P], conv_tail[:, 4 * (g - TT - 2) + j, :], IDENT[:, :])
                    else:
                        for i in (j, j + 4):
                            mm = nc.tensor.transpose(PS[:, g % 4, i * 24:(i + 1) * 24], state_rows[0:24, i * P:(i + 1) * P],
                                                     IDENT[0:24, 0:24])
                mm.then_inc(ct_turned, 1)

        def conv_state_scalar(act):
            for k in range(NP):
                nc.scalar.activation(sig_o[:, k, :], sig_o[:, k, :], ACT.Sigmoid, bias=PAR[:, B_OG + k:B_OG + k + 1])
            for g in range(TT + 5):
                n = P if g != TT - 1 else NS
                act.wait_ge(ct_turned, g + 1)
                if g < TT:
                    last = nc.scalar.activation(v1[0:n, g, :].rearrange("p (h d) -> p h d", h=H)[:, :, 0:HD],
                                                PS[0:n, g % 4, :].rearrange("p (h d) -> p h d", h=H), ACT.Copy)
                elif g < TT + 2:
                    last = nc.scalar.activation(mrows_stage[0:NS, 512 * (g - TT):512 * (g - TT) + 512], PS[0:NS, g % 4, :], ACT.Copy)
                elif g < TT + 4:
                    last = nc.scalar.activation(tail_stage[0:3, 512 * (g - TT - 2):512 * (g - TT - 2) + 512], PS[0:3, g % 4, :], ACT.Copy)
                else:
                    last = nc.scalar.activation(conv_x[:, :, :, 0:3],
                                                PS[:, g % 4, 0:192].rearrange("p (k b j) -> p k b j", k=KB, b=DB), ACT.Copy)
                last.then_inc(ct_taken, 1)

        def conv_state_pool(pool):
            chains["pool"](nc.gpsimd.memset(v1_flat[:, 0:VPAD], 0.0))
            nc.gpsimd.memset(v1[:, :, :].rearrange("p t (h d) -> p (t h) d", h=H)[:, :, HD:V1W], 1.0)
            nc.gpsimd.tensor_copy(conv_x[:, :, :, 3:11], qk[:, :, SEQ:N].rearrange("p k (b t) -> p k b t", t=DT))

        def conv_store(sp):
            sp.wait_ge(ct_taken, TT + 4)
            stored(sp.dma_start(O["conv_p"][0], tail_stage[0:3, :]))
            for b in range(DB):
                r = b * DT + DT - 3
                stored(sp.dma_start(O["conv_s"][b], mrows_stage[r:r + 3, :]))
            mark["conv_rows"] = stores[0]

        mark = {}

        conv_ready, conv_used = sem("conv_ready"), sem("conv_used")

        def conv_weight(j, k):
            return PAR[:, CONV_W + 8 * j + k:CONV_W + 8 * j + k + 1]

        def conv_bias(k):
            return PAR[:, CONV_B + k:CONV_B + k + 1]

        def conv_block(dve, k):
            chain = chains["dve"]
            dve.wait_ge(z_taken, NB["qk"] + k + 1)
            if k >= 2:
                dve.wait_ge(conv_used, k - 1)
            acc = conv_acc[k % 2]
            chain(nc.vector.tensor_scalar(acc[:, 0:SEQ], qk[:, k, 0:SEQ], conv_weight(3, k), conv_bias(k), ALU.mult, ALU.add))
            for j in (2, 1, 0):
                s = 3 - j
                last = nc.vector.scalar_tensor_tensor(out=acc[:, s:SEQ], in0=qk[:, k, 0:SEQ - s], scalar=conv_weight(j, k),
                                                      in1=acc[:, s:SEQ], op0=ALU.mult, op1=ALU.add)
                if j:
                    chain(last)
            last.then_inc(conv_ready, 1)

        def conv_silu(act, k):
            act.wait_ge(conv_ready, k + 1)
            chains["act"](nc.scalar.activation(conv_tail[:, k, :], qk[:, k, SEQ - 3:SEQ], ACT.Copy))
            nc.scalar.activation(qk[:, k, 0:SEQ], conv_acc[k % 2][:, 0:SEQ], ACT.Silu).then_inc(conv_used, 1)

        def conv_vector(dve):
            for j in (3, 2, 1, 0):
                for k in range(2 * NP):
                    x = conv_x[:, k, :, j:j + DT]
                    if j == 3:
                        last = nc.vector.tensor_scalar(conv_s[:, k], x, conv_weight(j, k), conv_bias(k), ALU.mult, ALU.add)
                    else:
                        last = nc.vector.scalar_tensor_tensor(out=conv_s[:, k], in0=x, scalar=conv_weight(j, k), in1=conv_s[:, k],
                                                              op0=ALU.mult, op1=ALU.add)
                if j:
                    chains["dve"](last)
            last.then_inc(conv_ready, 1)

        def conv_scalar(act):
            act.wait_ge(conv_ready, 2 * NP + 1)
            nc.scalar.activation(qk[:, :, SEQ:N], conv_s.rearrange("p k b t -> p k (b t)"), ACT.Silu)

        kt_turned, kt_taken = sem("kt_turned"), sem("kt_taken")

        def k_turn_tensor(pe):
            for g in range(TT):
                if g >= 4:
                    pe.wait_ge(kt_taken, g - 3)
                n = P if g != TT - 1 else NS
                for j in range(NP):
                    mm = nc.tensor.transpose(PS[0:n, g % 4, j * P:(j + 1) * P], qk[:, NP + j, g * P:g * P + n], IDENT[:, :])
                mm.then_inc(kt_turned, 1)

        def k_turn_vector(dve):
            for g in range(TT):
                n = P if g != TT - 1 else NS
                dve.wait_ge(kt_turned, g + 1)
                nc.vector.tensor_copy(ktok[0:n, g, :], PS[0:n, g % 4, :]).then_inc(kt_taken, 1)

        gexp, rows_ready, cols_turned, dec_ready, cols_taken = (
            sem("gate_softplus"), sem("rows_ready"), sem("cols_turned"), sem("dec_ready"),
            sem("cols_taken"))

        def gate_scalar(act):
            chain = chains["act"]
            chain(nc.scalar.activation(gm[0:H], gf[0:H], ACT.Abs))
            chain(nc.scalar.activation(gm[0:H], gm[0:H], ACT.Exp, scale=-1.0))
            nc.scalar.activation(gm[0:H], gm[0:H], ACT.Ln, bias=1.0).then_inc(gexp, 1)
            act.wait_ge(cols_taken, TT)
            nc.scalar.activation(colx[:, :, 0, :], cols[:, :, 0, :], ACT.Exp)
            nc.scalar.activation(colx[:, :, 1, :], cols[:, :, 1, :], ACT.Exp, scale=-1.0)
            chain(nc.scalar.activation(colx[:, :, 2, :], cols[:, :, 3, :], ACT.Exp))
            nc.scalar.activation(colx[:, :, 2, :], colx[:, :, 2, :], ACT.Copy, scale=HD ** -0.5)
            act.wait_ge(dec_ready, 1)
            nc.scalar.activation(dec[:, :, :], PS[:, 5, 0:64].rearrange("p (a b) -> p a b", a=NP), ACT.Exp)

        def gate_vector(dve):
            chain = chains["dve"]
            dve.wait_ge(out_stored, 16 * mark["conv_rows"])
            nc.vector.memset(rows4[:, :], 0.0)
            nc.vector.memset(gu[:, :], 0.0)
            nc.vector.memset(cols[:, :, :, :], 0.0)
            nc.vector.memset(cst[:, :, :], 0.0)
            chain(nc.vector.memset(mrow[0:H, 0:1], NEG))
            dve.wait_ge(gexp, 1)
            chain(nc.vector.scalar_tensor_tensor(out=gf[0:H], in0=gf[0:H], scalar=0.0, in1=gm[0:H],
                                                 op0=ALU.min, op1=ALU.subtract))
            nc.vector.tensor_tensor_scan(gb[0:H], restart[0:H], gf[0:H], 0.0, ALU.mult, ALU.add)
            nc.vector.tensor_tensor_scan(gm[0:H, 0:SEQ], gf[0:H, 0:SEQ], gi[0:H, 0:SEQ], NEG, ALU.add, ALU.max)
            for b in range(DB):
                t = slice(SEQ + b * DT, SEQ + (b + 1) * DT)
                last = nc.vector.tensor_tensor_scan(gm[0:H, t], gf[0:H, t], gi[0:H, t], mrow[0:H, NC + b:NC + b + 1],
                                                    ALU.add, ALU.max)
            chain(last)
            chunk3 = lambda r: r[:, 0:SEQ].rearrange("p (c t) -> p c t", t=P)
            batch3 = lambda r: r[:, SEQ:N].rearrange("p (c t) -> p c t", t=DT)
            nc.vector.tensor_copy(mrow[0:H, 1:NC], gm[0:H, P - 1:SEQ - P:P])
            nc.vector.tensor_copy(m_out[0:H, 1:1 + DB], gm[0:H, SEQ + DT - 1:N:DT])
            nc.vector.tensor_tensor(gu[0:H], gb[0:H], gm[0:H], ALU.subtract)
            nc.vector.tensor_copy(rows4[32:32 + H, :], gm[0:H])
            nc.vector.tensor_tensor(gw[0:H], gi[0:H], gb[0:H], ALU.subtract)
            chain(nc.vector.tensor_copy(m_out[0:H, 0:1], gm[0:H, SEQ - 1:SEQ]))
            g8, m8 = gu[0:H], mrow[0:H]
            nc.vector.tensor_tensor(chunk3(rows4[0:H]), chunk3(g8), m8[:, 0:NC].unsqueeze(2).to_broadcast([H, NC, P]), ALU.add)
            nc.vector.tensor_tensor(batch3(rows4[0:H]), batch3(g8), m8[:, NC:].unsqueeze(2).to_broadcast([H, DB, DT]), ALU.add)
            nc.vector.tensor_copy(rows4[64:64 + H, :], gw[0:H])
            nc.vector.tensor_tensor(chunk3(rows4[96:96 + H]), chunk3(gw[0:H]),
                                    chunk3(g8)[:, :, P - 1:P].to_broadcast([H, NC, P]), ALU.add)
            chain(nc.vector.tensor_tensor(batch3(rows4[96:96 + H]), batch3(gw[0:H]),
                                          batch3(g8)[:, :, DT - 1:DT].to_broadcast([H, DB, DT]), ALU.add))
            nc.vector.tensor_copy(dkrow[0:H, 0:NC], rows4[0:H, P - 1:SEQ:P])
            nc.vector.tensor_copy(dkrow[0:H, NC:], rows4[0:H, SEQ + DT - 1:N:DT]).then_inc(rows_ready, 1)
            for g in range(TT):
                n = P if g != TT - 1 else NS
                dve.wait_ge(cols_turned, g + 1)
                nc.vector.tensor_copy(cols[0:n, g, :, :], PS[0:n, g % 4, 0:P].rearrange("p (a b) -> p a b", a=4)[:, :, 0:H])\
                    .then_inc(cols_taken, 1)

        def gate_tensor(pe):
            pe.wait_ge(rows_ready, 1)
            for g in range(TT):
                n = P if g != TT - 1 else NS
                if g >= 4:
                    pe.wait_ge(cols_taken, g - 3)
                nc.tensor.transpose(PS[0:n, g % 4, 0:P], rows4[:, g * P:g * P + n], IDENT[:, :]).then_inc(cols_turned, 1)
            for p in range(NP):
                mm = nc.tensor.matmul(PS[:, 5, 16 * p:16 * p + 16], pair_sel[0:H, p, :], dkrow[0:H, :], start=True, stop=True)
            mm.then_inc(dec_ready, 1)

        def m_store(sp):
            sp.wait_ge(rows_ready, 1)
            with nc.allow_non_contiguous_dma(reason="one value per head"):
                stored(sp.dma_start(O["m_p"].rearrange("a h -> h a"), m_out[0:H, 0:1]))
                stored(sp.dma_start(O["m_s"].rearrange("b h -> h b"), m_out[0:H, 1:1 + DB]))

        lb = cut(SC, 0, H, P)
        la2 = cut(SC, 1024, H, P), cut(SC, 2048, H, P)
        mnum = cut(SC, 3072, H, V1W)
        hout = cut(SC, 3592, H, HD)
        kw = cut(XW, TT * AW + N, AW)
        qz = cut(XW, TT * AW + N + AW, 2, H * P)
        qz_ready = sem("qz_ready")
        cst = cut(XN, ML0 + 3448, NP, 2 * V1W)
        den = SMALL[:, 16:24]
        rden = SMALL[:, 24:32]
        sample_c = cut(WRT, 0, DB, NP * 2 * V1W)
        q_mask = cut(HB, BIG + 2 * NP * N, DB, NP * NS)
        kwm = cut(SC, 2048, 2, AW)
        n_rows = cut(HB, BIG + 2 * NP * N + DB * NP * NS, P)
        n_stage = cut(HB, BIG + 2 * NP * N + DB * NP * NS + P, 40)
        n_out = cut(HB, BIG + 2 * NP * N + DB * NP * NS + 2 * P, P)

        c_inter, c_inter_read = sem("chunk_inter"), sem("chunk_inter_read")
        c_ready, c_l, c_e, c_a, c_num, c_h, c_ht, c_cat, c_kw, c_upd, c_state = (
            sem(n) for n in ("chunk_scores", "chunk_logits", "chunk_weights", "chunk_a", "chunk_num", "chunk_h",
                             "chunk_h_turned", "chunk_done", "chunk_kw", "chunk_update", "chunk_state"))

        def q_part(c, n):
            return qz[:, c % 2, :].rearrange("p (h t) -> p h t", h=H)[:, :, 0:n]

        def q_pad_pool(pool, c):
            n, t0 = P if c < NC else NS, c * P
            if c >= 2:
                pool.wait_ge(c_ready, c - 1)
            for e in range(2):
                rows = slice(HD * e, HD * e + HD)
                ins = nc.gpsimd.tensor_copy(q_part(c, n)[rows, e::2], qk[rows, 0:NP, t0:t0 + n]).then_inc(qz_ready, 1)
                pool.wait_ge(qz_ready, 2 * c + e + 1)

        def q_zero_pool(pool):
            chains["pool"](nc.gpsimd.memset(qz[:, :, :], 0.0))

        def scores_tensor(pe, c, n):
            t0 = c * P
            pe.wait_ge(qz_ready, 2 * c + 2)
            for p in range(NP):
                nc.tensor.matmul(bank2(n, p // 2, 1)[:, 2 * (p % 2):2 * (p % 2) + 2], qk[:, NP + p, t0:t0 + n],
                                 q_part(c, n)[:, 2 * p:2 * p + 2], start=True, stop=True)
            for h in range(H):
                mm = nc.tensor.matmul(PS[0:n, 2 + h // 4, (h % 4) * P:(h % 4) * P + n], head_sel[:, h, 0:n],
                                      gu[:, t0:t0 + n], start=True, stop=True)
            mm.then_inc(c_ready, 1)

        def num_tensor(pe, c, n):
            pe.wait_ge(c_a, c + 1)
            for h in reversed(range(H)):
                b0, v0 = (h % 4) * V1W, c * H * V1W + h * V1W
                mm = nc.tensor.matmul(PS[0:n, 4 + h // 4, b0:b0 + WIDE], la2[c % 2][0:n, h, 0:n],
                                      v1_flat[0:n, VPAD + V1W - WIDE + v0:][:, 0:WIDE], start=True, stop=True)
            mm.then_inc(c_num, 1)

        def turn_h_tensor(pe, c, n):
            pe.wait_ge(c_h, c + 1)
            for j in range(NP):
                mm = nc.tensor.transpose(PS[:, 4, j * P:j * P + n], hout[0:n, 2 * j:2 * j + 2, :].rearrange("p a b -> p (a b)"),
                                         IDENT[0:n, 0:n])
            mm.then_inc(c_ht, 1)

        def chunk_tensor(pe):
            scores_tensor(pe, 0, P)
            for c in range(NC):
                if c:
                    pe.wait_ge(c_state, c)
                for p in range(NP):
                    mm = nc.tensor.matmul(PS[:, 6 + p // 2, (p % 2) * 2 * V1W:(p % 2 + 1) * 2 * V1W], qk[:, p, c * P:(c + 1) * P],
                                          cst[:, p, :], start=True, stop=True)
                mm.then_inc(c_inter, 1)
                pe.wait_ge(c_a, c + 1)
                if c + 1 < NC:
                    scores_tensor(pe, c + 1, P)
                if c:
                    pe.wait_ge(c_cat, c)
                num_tensor(pe, c, P)
                pe.wait_ge(c_kw, c + 1)
                pe.wait_ge(c_inter_read, c + 1)
                for p in range(NP):
                    mm = nc.tensor.matmul(PS[:, 6 + p // 2, (p % 2) * 2 * V1W:(p % 2 + 1) * 2 * V1W], kw[:, p * P:(p + 1) * P],
                                          v1[:, c, p * 2 * V1W:(p + 1) * 2 * V1W], start=True, stop=True)
                mm.then_inc(c_upd, 1)
                turn_h_tensor(pe, c, P)

        def chunk_scalar(act, chunks):
            for c in chunks:
                n = P if c < NC else NS
                act.wait_ge(c_l, c + 1)
                if c < NC:
                    cache_copy(act, c, 1)
                for h in range(H):
                    last = nc.scalar.activation(lb[0:n, h, 0:n], lb[0:n, h, 0:n], ACT.Exp, bias=cols[0:n, c, 2, h:h + 1])
                last.then_inc(c_e, 1)

        def chunk_pool(pool, chunks):
            for c in chunks:
                n = P if c < NC else NS
                if 1 <= c < NC:
                    q_pad_pool(pool, c + 1)
                if 0 < c < NC:
                    pool.wait_ge(c_upd, c)
                nc.gpsimd.tensor_tensor(kw[0:n, :].rearrange("p (h d) -> p h d", h=H),
                                        ktok[0:n, c, :].rearrange("p (h d) -> p h d", h=H),
                                        colx[0:n, c, 2, :].unsqueeze(2).to_broadcast([n, H, HD]), ALU.mult).then_inc(c_kw, 1)

        def chunk_logits(dve, c, n, mask):
            dve.wait_ge(c_ready, c + 1)
            if c and c < NC:
                dve.wait_ge(c_a, c)
            nc.vector.tensor_tensor(lb[0:n, :, 0:n], bank2(n, 2), mask.unsqueeze(1).to_broadcast([n, H, n]), ALU.add).then_inc(c_l, 1)

        def bank2(n, b, banks=2):
            return PS[0:n, b:b + banks, :].rearrange("p a (h t) -> p (a h) t", h=4)[:, :, 0:n]

        def chunk_weights(dve, c, n):
            dve.wait_ge(c_e, c + 1)
            nc.vector.scalar_tensor_tensor(out=la2[c % 2][0:n, :, 0:n], in0=bank2(n, 0), scalar=HD ** -0.5, in1=lb[0:n, :, 0:n],
                                           op0=ALU.mult, op1=ALU.mult).then_inc(c_a, 1)

        def chunk_inter(dve, c, n):
            iw = colx[0:n, c, 0, :].rearrange("p (a h) -> p a h", a=2)
            m4 = mnum[0:n].rearrange("p (a h) d -> p a h d", a=2)
            for a in range(2):
                ins = nc.vector.tensor_tensor(m4[:, a], PS[0:n, 6 + a, 0:4 * V1W].rearrange("p (h d) -> p h d", h=4),
                                              iw[:, a].unsqueeze(2).to_broadcast([n, 4, V1W]), ALU.mult)
            chains["dve"](ins)

        def chunk_output(dve, c, n):
            chain = chains["dve"]
            m4 = mnum[0:n].rearrange("p (a h) d -> p a h d", a=2)
            dve.wait_ge(c_num, c + 1)
            for a in range(2):
                last = nc.vector.tensor_tensor(m4[:, a], PS[0:n, 4 + a, WIDE - V1W:WIDE + 3 * V1W].rearrange("p (h d) -> p h d", h=4),
                                               m4[:, a], ALU.add)
            chain(last)
            chain(nc.vector.tensor_scalar(den[0:n], mnum[0:n, :, HD], -1.0, None, ALU.mult))
            chain(nc.vector.tensor_tensor(den[0:n], den[0:n], mnum[0:n, :, HD], ALU.max))
            chain(nc.vector.tensor_tensor(den[0:n], den[0:n], colx[0:n, c, 1, :], ALU.max))
            chain(nc.vector.reciprocal(rden[0:n], den[0:n]))
            nc.vector.tensor_tensor(hout[0:n], mnum[0:n, :, 0:HD], rden[0:n].unsqueeze(2).to_broadcast([n, H, HD]), ALU.mult)\
                .then_inc(c_h, 1)

        def chunk_place(dve, c, n, t0):
            dve.wait_ge(c_ht, c + 1)
            nc.vector.tensor_tensor(sig_o[:, :, t0:t0 + n], PS[:, 4, :].rearrange("p (j t) -> p j t", j=NP)[:, :, 0:n],
                                    sig_o[:, :, t0:t0 + n], ALU.mult).then_inc(c_cat, 1)

        def state_decay(state, c):
            for e in range(2):
                rows, cs = slice(HD * e, HD * e + HD), slice(V1W * e, V1W * e + V1W)
                last = nc.vector.tensor_tensor(state[rows, :, cs], state[rows, :, cs],
                                               dec[rows, :, c:c + 1].to_broadcast([HD, NP, V1W]), ALU.mult)
            chains["dve"](last)

        def state_add(state, banks, signal):
            for e in range(2):
                rows, cs = slice(HD * e, HD * e + HD), slice(V1W * e, V1W * e + V1W)
                for a in range(2):
                    upd = PS[rows, banks + a, 0:4 * V1W].rearrange("p (j d) -> p j d", j=2)
                    last = nc.vector.tensor_tensor(state[rows, 2 * a:2 * a + 2, cs], upd[:, :, cs], state[rows, 2 * a:2 * a + 2, cs], ALU.add)
            last.then_inc(signal, 1)

        def chunk_vector(dve):
            chunk_logits(dve, 0, P, causal[:, :])
            chunk_weights(dve, 0, P)
            for c in range(NC):
                dve.wait_ge(c_inter, c + 1)
                chunk_inter(dve, c, P)
                nc.vector.memset(SMALL[:, 42:43], 0.0).then_inc(c_inter_read, 1)
                state_decay(cst, c)
                if c + 1 < NC:
                    chunk_logits(dve, c + 1, P, causal[:, :])
                chunk_output(dve, c, P)
                dve.wait_ge(c_upd, c + 1)
                state_add(cst, 6, c_state)
                if c + 1 < NC:
                    chunk_weights(dve, c + 1, P)
                chunk_place(dve, c, P, c * P)
            dve.wait_ge(c_state, NC)

        sc_zeroed, sc_landed, n_turned, n_put, qm_ready, kwm_ready, su_ready, su_done, n_ready, n_rows_ready = (
            sem(n) for n in ("sc_zeroed", "sc_landed", "n_turned", "n_put", "q_mask_ready", "kwm_ready", "sample_update",
                             "sample_state", "n_ready", "n_rows_ready"))
        sc4 = sample_c[:, :, :].rearrange("p b (j d) -> p b j d", j=NP)

        def sample_state_load(sp):
            sp.wait_ge(sc_zeroed, 1)
            src = A["state_mlstm_C"].rearrange("b (j e) k v -> e k b j v", e=2)
            with nc.allow_non_contiguous_dma(reason="rows of 64 floats"):
                for e in range(2):
                    for b in range(DB):
                        sp.dma_start(sc4[HD * e:HD * e + HD, b, :, V1W * e:V1W * e + HD], src[e, :, b]).then_inc(sc_landed, 16)
            sp.wait_ge(phase_done, 4 * PH["chunks"])
            sp.dma_start(n_rows[0:DB * NP, :], A["state_mlstm_n"].rearrange("b (j e) k -> (b j) (e k)", e=2)).then_inc(n_landed, 16)

        n_landed = sem("n_landed")

        def sample_pool(pool):
            chains["pool"](nc.gpsimd.memset(sample_c[:, :, :], 0.0))
            nc.gpsimd.memset(SMALL[:, 40:41], 0.0).then_inc(sc_zeroed, 1)

        def q_mask_pool(pool):
            chains["pool"](nc.gpsimd.memset(q_mask[:, :, :], 0.0))
            for b in range(DB):
                qm = q_mask[:, b, :].rearrange("p (j t) -> p j t", j=NP)
                last = nc.gpsimd.tensor_copy(qm[:, :, b * DT:(b + 1) * DT], qk[:, 0:NP, SEQ + b * DT:SEQ + (b + 1) * DT])
            last.then_inc(qm_ready, 1)

        def sample_tensor(pe):
            pe.wait_ge(n_landed, 16)
            nc.tensor.transpose(PS[:, 7, 480:512], n_rows[0:DB * NP, :], IDENT[0:DB * NP, 0:DB * NP]).then_inc(n_turned, 1)
            scores_tensor(pe, NC, NS)
            pe.wait_ge(n_put, 1)
            pe.wait_ge(qm_ready, 1)
            for p in range(NP):
                for b in range(DB):
                    mm = nc.tensor.matmul(PS[0:NS, 6 + p // 2, (p % 2) * 2 * V1W:(p % 2 + 1) * 2 * V1W],
                                          q_mask[:, b, p * NS:(p + 1) * NS], sc4[:, b, p, :], start=(b == 0), stop=(b == DB - 1))
            num_tensor(pe, NC, NS)
            turn_h_tensor(pe, NC, NS)
            for b in range(DB):
                pe.wait_ge(kwm_ready, b + 1)
                bank = 4 + 2 * (b % 2)
                if b == 0:
                    pe.wait_ge(c_cat, NC + 1)
                if b >= 2:
                    pe.wait_ge(su_done, b - 1)
                for p in range(NP):
                    mm = nc.tensor.matmul(PS[:, bank + p // 2, (p % 2) * 2 * V1W:(p % 2 + 1) * 2 * V1W],
                                          kwm[0:NS, b % 2, p * P:(p + 1) * P], v1[0:NS, NC, p * 2 * V1W:(p + 1) * 2 * V1W],
                                          start=True, stop=True)
                mm.then_inc(su_ready, 1)
            pe.wait_ge(n_ready, 1)
            nc.tensor.transpose(PS[0:(DB + 1) * NP, 0, 0:P], n_stage[:, 0:(DB + 1) * NP], IDENT[:, :]).then_inc(n_rows_ready, 1)

        def sample_vector(dve):
            chain = chains["dve"]
            dve.wait_ge(n_turned, 1)
            dve.wait_ge(sc_landed, 16 * 16)
            for e in range(2):
                rows = slice(HD * e, HD * e + HD)
                last = nc.vector.tensor_copy(sc4[rows, :, :, V1W * e + HD], PS[rows, 7, 480:512].rearrange("p (b j) -> p b j", b=DB))
            last.then_inc(n_put, 1)
            chunk_logits(dve, NC, NS, sample_causal[0:NS])
            chunk_weights(dve, NC, NS)
            dve.wait_ge(c_num, NC + 1)
            chunk_inter(dve, NC, NS)
            chunk_output(dve, NC, NS)
            chunk_place(dve, NC, NS, SEQ)
            dve.wait_ge(c_kw, NC + 1)

            def masked(b):
                if b >= 2:
                    dve.wait_ge(su_ready, b - 1)
                nc.vector.tensor_scalar(kwm[0:NS, b % 2, :], kw[0:NS, :], batch_sel[0:NS, b:b + 1], None, ALU.mult).then_inc(kwm_ready, 1)
            masked(0)
            for b in range(DB):
                if b + 1 < DB:
                    masked(b + 1)
                state_decay(sc4[:, b], NC + b)
                dve.wait_ge(su_ready, b + 1)
                state_add(sc4[:, b], 4 + 2 * (b % 2), su_done)
            dve.wait_ge(su_done, DB)
            for e in range(2):
                rows = slice(HD * e, HD * e + HD)
                nc.vector.tensor_copy(n_stage[rows, 0:DB * NP].rearrange("p (b j) -> p b j", b=DB), sc4[rows, :, :, V1W * e + HD])
                last = nc.vector.tensor_copy(n_stage[rows, DB * NP:(DB + 1) * NP], cst[rows, :, V1W * e + HD])
            last.then_inc(n_ready, 1)
            dve.wait_ge(n_rows_ready, 1)
            nc.vector.tensor_copy(n_out[0:(DB + 1) * NP, :], PS[0:(DB + 1) * NP, 0, 0:P]).then_inc(n_out_ready, 1)

        n_out_ready = sem("n_out_ready")

        def state_store(sp):
            sp.wait_ge(n_out_ready, 1)
            cs, cp = (O[n].rearrange("b (j e) k v -> e k b j v", e=2) for n in ("C_s", "C_p"))
            with nc.allow_non_contiguous_dma(reason="rows of 64 floats"):
                for e in range(2):
                    rows, c64 = slice(HD * e, HD * e + HD), slice(V1W * e, V1W * e + HD)
                    stored(sp.dma_start(cp[e, :, 0], cst[rows, :, c64]))
                    for b in range(DB):
                        stored(sp.dma_start(cs[e, :, b], sc4[rows, b, :, c64]))
            stored(sp.dma_start(O["n_s"].rearrange("b (j e) k -> (b j) (e k)", e=2), n_out[0:DB * NP, :]))
            stored(sp.dma_start(O["n_p"].rearrange("b (j e) k -> (b j) (e k)", e=2), n_out[DB * NP:(DB + 1) * NP, :]))
            mark["state"] = stores[0]

        KT = PAST // P
        kc = cut(XW, 0, 2, KT * AW)
        kT = cut(HB, BIG, NP, PAST), cut(HB, BIG + 4096, NP, PAST)
        wo = cut(HB, BIG + 8192, 2, AW)
        vc = cut(XN, 0, 2, KT * AW)
        wl = cut(SC, 0, PAST + NS)
        wbias = cut(SC, PAST + NS, PAST)
        wnew = cut(SC, 2 * PAST + NS, DB // 2 * NS)
        wpt = cut(SC, 2 * PAST + NS + DB // 2 * NS, 9, P)
        kc_landed = [sem(f"kc_landed{i}") for i in range(2)]
        vc_landed = [sem(f"vc_landed{i}") for i in range(2)]
        wb_landed = sem("wb_landed")
        wk_taken = [sem(f"wk_taken{i}") for i in range(2)]
        wk_turned, ws_ready, wl_ready, wp_ready, wp_turned, wp_taken, wo_ready, wo_taken, wl_free = (
            sem(n) for n in ("wk_turned", "ws_ready", "wl_ready", "wp_ready", "wp_turned", "wp_taken",
                             "wo_ready", "wo_taken", "wl_free"))

        def load_k(sp, b):
            if b >= 2:
                sp.wait_ge(wk_turned, NP * 2 * (b - 1))
            sp.dma_start(kc[:, b % 2, :].rearrange("p (t n) -> p t n", n=AW),
                         A["cache_win_k"][b].rearrange("(t p) h d -> p t (h d)", p=P)).then_inc(kc_landed[b % 2], 16)

        def win_load_first(sp):
            load_k(sp, 0)
            sp.wait_ge(phase_done, 4 * PH["sample"])
            load_k(sp, 1)
            sp.dma_start(wbias, A["sample_bias"]).then_inc(wb_landed, 16)
            sp.dma_start(wnew, A["sample_new_bias"]).then_inc(wb_landed, 16)

        def win_load(sp):
            vd = A["cache_win_v"].rearrange("b (t p) h d -> b p t (h d)", p=P)

            def load_v(b):
                if b >= 2:
                    sp.wait_ge(wo_ready, b - 1)
                sp.dma_start(vc[:, b % 2, :].rearrange("p (t n) -> p t n", n=AW), vd[b]).then_inc(vc_landed[b % 2], 16)
            for pair in range(DB // 2):
                if pair + 1 < DB // 2:
                    load_k(sp, 2 * pair + 2)
                if pair == 0:
                    sp.wait_ge(out_stored, 16 * mark["state"])
                    load_v(0)
                    load_v(1)
                if pair + 1 < DB // 2:
                    load_k(sp, 2 * pair + 3)
                if pair:
                    load_v(2 * pair)
                    load_v(2 * pair + 1)

        def win_tensor(pe):
            def turn_k(b, p):
                if p == 0:
                    pe.wait_ge(kc_landed[b % 2], 16 * (b // 2 + 1))
                kb = kc[:, b % 2, :].rearrange("p (t n) -> p t n", n=AW)
                for half in range(2):
                    if b or p:
                        pe.wait_ge(wk_taken[half], NP * b + p)
                    for j in range(4):
                        mm = nc.tensor.transpose(PS[:, half, j * P:(j + 1) * P], kb[:, 4 * half + j, p * P:(p + 1) * P],
                                                 IDENT[:, :])
                    mm.then_inc(wk_turned, 1)

            def scores(b):
                e, pair = b % 2, b // 2
                for half in range(2):
                    pe.wait_ge(wk_taken[half], NP * (b + 1))
                if e == 0 and pair:
                    pe.wait_ge(wl_ready, pair)
                k = kT[b % 2]
                for p in range(NP):
                    for c, (w, x) in enumerate(((512, k[:, p, 0:512]), (512, k[:, p, 512:PAST]), (NS, KNEW[:, p, :]))):
                        mm = nc.tensor.matmul(PS[HD * e:HD * e + HD, 2 + c, 0:w], QX[:, p, b, :], x,
                                              start=(p == 0), stop=(p == NP - 1))
                    if p == NP - 1:
                        mm.then_inc(ws_ready, 1)
                    if b + 1 < DB:
                        turn_k(b + 1, p)

            def turn_p(pair):
                pe.wait_ge(wp_ready, pair + 1)
                for q in range(3):
                    n = 3 * pair + q
                    if n >= 2:
                        pe.wait_ge(wp_taken, n - 1)
                    if q < 2:
                        for j in range(4):
                            mm = nc.tensor.transpose(PS[:, 5 + n % 2, j * P:(j + 1) * P], wl[:, (4 * q + j) * P:(4 * q + j + 1) * P],
                                                     IDENT[:, :])
                    else:
                        mm = nc.tensor.transpose(PS[0:NS, 5 + n % 2, 0:P], wl[:, PAST:PAST + NS], IDENT[:, :])
                    mm.then_inc(wp_turned, 1)

            def values(pair):
                pe.wait_ge(wp_taken, 3 * pair + 3)
                if pair:
                    pe.wait_ge(wo_taken, pair)
                for e in range(2):
                    pe.wait_ge(vc_landed[e], 16 * (pair + 1))
                    vb = vc[:, e, :].rearrange("p (t n) -> p t n", n=AW)
                    cs = slice(HD * e, HD * e + HD)
                    for t in range(KT + 1):
                        p, v = (wpt[:, t, cs], vb[:, t, :]) if t < KT else (wpt[0:NS, t, cs], VNEW[:, :])
                        mm = nc.tensor.matmul(PS[cs, 7, :], p, v, start=(t == 0), stop=(t == KT))
                    mm.then_inc(wo_ready, 1)

            def turn_o(pair):
                pe.wait_ge(wv_taken, pair + 1)
                for j in range(NP):
                    mm = nc.tensor.transpose(PS[:, 7, j * P:(j + 1) * P], wo[:, pair % 2, j * P:(j + 1) * P], IDENT[:, :])
                mm.then_inc(wo_turned, 1)

            for p in range(NP):
                turn_k(0, p)
            for b in range(DB):
                scores(b)
                if b >= 2:
                    (turn_p if b % 2 == 0 else values)(b // 2 - 1)
                if b >= 4 and b % 2 == 0:
                    turn_o(b // 2 - 2)
            turn_p(DB // 2 - 1)
            turn_o(DB // 2 - 2)
            values(DB // 2 - 1)
            turn_o(DB // 2 - 1)

        wv_taken, wo_turned = sem("wv_taken"), sem("wo_turned")

        def take_k(eng, half, b):
            for p in range(NP):
                eng.wait_ge(wk_turned, 2 * (NP * b + p) + half + 1)
                if p == 0 and b >= 2:
                    eng.wait_ge(ws_ready, b - 1)
                out, src = kT[b % 2][:, p, 512 * half:512 * half + 512], PS[:, half, :]
                ins = nc.vector.tensor_copy(out, src) if half else nc.scalar.activation(out, src, ACT.Copy)
                ins.then_inc(wk_taken[half], 1)

        def win_scalar(act):
            def take_p(pair):
                for q in range(3):
                    n = 3 * pair + q
                    act.wait_ge(wp_turned, n + 1)
                    if q == 0 and pair:
                        act.wait_ge(wo_ready, 2 * pair)
                    if q < 2:
                        last = nc.scalar.activation(wpt[:, 4 * q:4 * q + 4, :], PS[:, 5 + n % 2, :].rearrange("p (a b) -> p a b", a=4), ACT.Copy)
                    else:
                        last = nc.scalar.activation(wpt[0:NS, KT, :], PS[0:NS, 5 + n % 2, 0:P], ACT.Copy)
                    last.then_inc(wp_taken, 1)
            def take_values(pair):
                act.wait_ge(wo_ready, 2 * pair + 2)
                nc.scalar.activation(wo[:, pair % 2, :], PS[:, 7, :], ACT.Copy).then_inc(wv_taken, 1)
            take_k(act, 0, 0)
            for b in range(DB):
                if b + 1 < DB:
                    take_k(act, 0, b + 1)
                if b >= 4 and b % 2 == 0:
                    take_values(b // 2 - 2)
                if b % 2:
                    act.wait_ge(wl_ready, b // 2 + 1)
                    nc.scalar.activation(wl[:, :], wl[:, :], ACT.Exp, bias=negm[:, 0:1], accum_out=asum[:, 0:1]).then_inc(wl_free, 1)
                elif b:
                    take_p(b // 2 - 1)
            take_values(DB // 2 - 2)
            take_p(DB // 2 - 1)
            take_values(DB // 2 - 1)

        def win_vector(dve):
            chain = chains["dve"]

            def softmax(pair):
                dve.wait_ge(ws_ready, 2 * pair + 2)
                if pair:
                    dve.wait_ge(wp_turned, 3 * pair)
                else:
                    dve.wait_ge(wb_landed, 32)
                nc.vector.tensor_tensor_reduce(wl[:, 0:PAST], PS[:, 2:4, :].rearrange("p a b -> p (a b)"), wbias, 1.0, 3 * NEG,
                                               ALU.add, ALU.max, amax[:, 0:1])
                chain(nc.vector.tensor_tensor_reduce(wl[:, PAST:PAST + NS], PS[:, 4, 0:NS], wnew[:, pair * NS:(pair + 1) * NS],
                                                     1.0, 3 * NEG, ALU.add, ALU.max, amax[:, 1:2]))
                chain(nc.vector.tensor_tensor(amax[:, 0:1], amax[:, 0:1], amax[:, 1:2], ALU.max))
                nc.vector.tensor_scalar(negm[:, 0:1], amax[:, 0:1], -1.0, None, ALU.mult).then_inc(wl_ready, 1)
                dve.wait_ge(wl_free, pair + 1)
                chain(nc.vector.reciprocal(arec[:, 0:1], asum[:, 0:1]))
                nc.vector.tensor_scalar(wl[:, :], wl[:, :], arec[:, 0:1], None, ALU.mult).then_inc(wp_ready, 1)

            def output(pair):
                dve.wait_ge(wo_turned, pair + 1)
                for e in range(2):
                    b = 2 * pair + e
                    for r in range(2):
                        rows = slice(HD * r, HD * r + HD)
                        for j in range(NP):
                            h = 2 * j + r
                            last = nc.vector.tensor_copy(cat[rows, j, SEQ + b * DT:SEQ + (b + 1) * DT],
                                                         PS[rows, 7, j * P + HD * e + DT * h:j * P + HD * e + DT * (h + 1)])
                last.then_inc(wo_taken, 1)

            take_k(dve, 1, 0)
            for b in range(DB):
                if b + 1 < DB:
                    take_k(dve, 1, b + 1)
                if b % 2:
                    softmax(b // 2)
                elif b >= 4:
                    output(b // 2 - 2)
            output(DB // 2 - 2)
            output(DB // 2 - 1)

        mem_tok = cut(HB, 0, 2, D)
        mem_T = cut(HB, 2048, KB, NMEM)
        mvT = cut(HB, 4096, KB, NMEM)
        mk_tok = cut(sb("mem_k_tok", P, 2 * D, at=AT["sample_q_wide"]), 0, 2, D)
        mkT = cut(HB, BIG, KB, NMEM)
        mv_tok = cut(HB, BIG + 2048, 2, D)
        mhi, mlo = cut(XHI, 0, KB, NMEM), cut(XLO, 0, KB, NMEM)
        mem_landed, mem_turned, mkv_turned, mkv_taken = (
            sem(n) for n in ("mem_landed", "mem_turned", "mkv_turned", "mkv_taken"))

        def mem_load(sp):
            sp.wait_ge(norm_done, J["ml"][1] + 1)
            sp.dma_start(mem_tok[:, :, :], A["mem_prompt"][0].rearrange("(t p) d -> p t d", p=P)).then_inc(mem_landed, 16)

        def mem_turn_tensor(pe):
            pe.wait_ge(mem_landed, 16)
            for g in range(4):
                t, half = g // 2, g % 2
                for j in range(4):
                    mm = nc.tensor.transpose(PS[:, g, j * P:(j + 1) * P], mem_tok[:, t, (4 * half + j) * P:(4 * half + j + 1) * P], IDENT[:, :])
                mm.then_inc(mem_turned, 1)

        def mem_turn_vector(dve):
            for g in range(4):
                t, half = g // 2, g % 2
                dve.wait_ge(mem_turned, g + 1)
                nc.vector.tensor_copy(mem_T[:, 4 * half:4 * half + 4, t * P:(t + 1) * P], PS[:, g, :].rearrange("p (j n) -> p j n", j=4))

        def mkv_turn_tensor(pe):
            for g in range(8):
                src, t, half = (mkT, mvT)[g // 4], g % 4 // 2, g % 2
                for j in range(4):
                    mm = nc.tensor.transpose(PS[:, g, j * P:(j + 1) * P], src[:, 4 * half + j, t * P:(t + 1) * P], IDENT[:, :])
                mm.then_inc(mkv_turned, 1)

        def mkv_turn_scalar(act):
            for g in range(8):
                dst, t, half = (mk_tok, mv_tok)[g // 4], g % 4 // 2, g % 2
                act.wait_ge(mkv_turned, g + 1)
                nc.scalar.activation(dst[:, t, 512 * half:512 * half + 512], PS[:, g, :], ACT.Copy).then_inc(mkv_taken, 1)

        def mkv_store(sp):
            sp.wait_ge(mkv_taken, 8)
            for name, src in (("mem_k", mk_tok), ("mem_v", mv_tok)):
                stored(sp.dma_start(O[name][0].rearrange("(t p) h d -> p t (h d)", p=P), src[:, :, :]))
            mark["mkv"] = stores[0]

        cq = cat
        xl = cut(SC, 0, 2, XH * NMEM)
        xpt = cut(SC, 2048, 2, 8 * P)
        xmax, xsum, xrec = SMALL[:, 48:56], SMALL[:, 56:64], SMALL[:, 64:72]
        xs_ready, xm_ready, xp_ready, xn_ready, xt_ready, xt_taken, xo_ready, xo_taken = (
            sem(n) for n in ("xs_ready", "xm_ready", "xp_ready", "xn_ready", "xt_ready", "xt_taken", "xo_ready", "xo_taken"))

        def cross_tensor(pe):
            def scores(t):
                if t >= 2:
                    pe.wait_ge(xp_ready, t - 1)
                b0 = 2 * (t % 2)
                for h in range(XH):
                    for k in range(2):
                        mm = nc.tensor.matmul(PS[:, b0 + h // 2, (h % 2) * NMEM:(h % 2 + 1) * NMEM], cq[:, 2 * h + k, t * P:(t + 1) * P],
                                              mkT[:, 2 * h + k, :], start=(k == 0), stop=(k == 1))
                mm.then_inc(xs_ready, 1)

            def turn(t):
                pe.wait_ge(xn_ready, t + 1)
                if t:
                    pe.wait_ge(xt_taken, t)
                for i in range(8):
                    mm = nc.tensor.transpose(PS[:, 4 + i // 4, (i % 4) * P:(i % 4 + 1) * P], xl[:, t % 2, i * P:(i + 1) * P], IDENT[:, :])
                mm.then_inc(xt_ready, 1)

            def values(t):
                pe.wait_ge(xt_taken, t + 1)
                if t:
                    pe.wait_ge(xo_taken, t)
                for h in range(XH):
                    for db in range(2):
                        i = 2 * h + db
                        for m in range(2):
                            mm = nc.tensor.matmul(PS[:, 6 + i // 4, (i % 4) * P:(i % 4 + 1) * P], mv_tok[:, m, i * P:(i + 1) * P],
                                                  xpt[:, t % 2, (2 * h + m) * P:(2 * h + m + 1) * P], start=(m == 0), stop=(m == 1))
                mm.then_inc(xo_ready, 1)
            scores(0)
            for t in range(NC + 1):
                if t + 1 < NC:
                    scores(t + 1)
                if t < NC:
                    turn(t)
                if t:
                    values(t - 1)

        def cross_scalar(act):
            def high(t):
                act.wait_ge(xo_ready, t + 1)
                nc.scalar.activation(xhi[:, :, t * P:(t + 1) * P], PS[:, 6:8, :].rearrange("p a (j n) -> p (a j) n", j=4), ACT.Copy)\
                    .then_inc(xo_high, 1)
            for t in range(NC):
                act.wait_ge(xm_ready, t + 1)
                b0, s4 = 2 * (t % 2), 4 * (t % 2)
                for h in range(XH):
                    last = nc.scalar.activation(xl[:, t % 2, h * NMEM:(h + 1) * NMEM],
                                                PS[:, b0 + h // 2, (h % 2) * NMEM:(h % 2 + 1) * NMEM], ACT.Exp,
                                                bias=xmax[:, s4 + h:s4 + h + 1], accum_out=xsum[:, s4 + h:s4 + h + 1])
                last.then_inc(xp_ready, 1)
                act.wait_ge(xt_ready, t + 1)
                if t >= 2:
                    act.wait_ge(xo_ready, t - 1)
                nc.scalar.activation(xpt[:, t % 2, :], PS[:, 4:6, :].rearrange("p a b -> p (a b)"), ACT.Copy).then_inc(xt_taken, 1)
                if t:
                    high(t - 1)
            high(NC - 1)

        out8 = PS[:, 6:8, :].rearrange("p a (j n) -> p (a j) n", j=4)
        xo_high = sem("xo_high")

        def cross_vector(dve):
            chain = chains["dve"]

            def maxima(t):
                b0, s4 = 2 * (t % 2), 4 * (t % 2)
                dve.wait_ge(xs_ready, t + 1)
                if t >= 2:
                    dve.wait_ge(xp_ready, t - 1)
                    dve.wait_ge(xt_ready, t - 1)
                nc.vector.tensor_reduce(xmax[:, s4:s4 + 4], PS[:, b0:b0 + 2, :].rearrange("p a (h m) -> p (a h) m", h=2), AX_X, ALU.max,
                                        negate=True).then_inc(xm_ready, 1)

            def low(t):
                dve.wait_ge(xo_high, t + 1)
                nc.vector.tensor_tensor(xlo[:, :, t * P:(t + 1) * P], out8, xhi[:, :, t * P:(t + 1) * P].bitcast(F32), ALU.subtract)\
                    .then_inc(xo_taken, 1)
            maxima(0)
            for t in range(NC):
                s4 = 4 * (t % 2)
                dve.wait_ge(xp_ready, t + 1)
                chain(nc.vector.reciprocal(xrec[:, s4:s4 + 4], xsum[:, s4:s4 + 4]))
                x3 = xl[:, t % 2, :].rearrange("p (h m) -> p h m", h=XH)
                nc.vector.tensor_tensor(x3, x3, xrec[:, s4:s4 + 4].unsqueeze(2).to_broadcast([P, XH, NMEM]), ALU.mult).then_inc(xn_ready, 1)
                if t + 1 < NC:
                    maxima(t + 1)
                if t:
                    low(t - 1)
            low(NC - 1)

        ck = cut(WRT, 0, 2, 2 * D)
        cv = cut(HB, 0, 4, 2 * D)
        ckT = cut(HB, BIG, KB, NMEM), cut(HB, BIG + 2048, KB, NMEM)
        yo = cut(WRT, 4096, D)
        cqx = cut(sb("cross_sample_q", P, 2 * D, at=AT["sample_q_wide"]), 0, KB, DB, XH * DT)
        yl = cut(SC, 2048, NMEM)
        ypt = cut(SC, 2304, 2, P)
        ck_landed = [sem(f"ck_landed{i}") for i in range(2)]
        cv_landed = [sem(f"cv_landed{i}") for i in range(2)]
        cqx_ready, yk_turned, yk_taken, ys_ready, ym_ready, yp_ready, yn_ready, yt_ready, yt_taken, yo_ready, yo_taken = (
            sem(n) for n in ("cqx_ready", "yk_turned", "yk_taken", "ys_ready", "ym_ready", "yp_ready", "yn_ready", "yt_ready",
                             "yt_taken", "yo_ready", "yo_taken"))

        def xsample_load(sp):
            sp.wait_ge(phase_done, 4 * PH["cq"])
            kd, vd = (A[n].rearrange("b (t p) h d -> b p t (h d)", p=P) for n in ("cache_mem_k", "cache_mem_v"))
            for b in range(DB):
                if b >= 2:
                    sp.wait_ge(yk_turned, 4 * (b - 1))
                sp.dma_start(ck[:, b % 2, :].rearrange("p (t n) -> p t n", n=D), kd[b]).then_inc(ck_landed[b % 2], 16)
                if b == 1:
                    sp.wait_ge(phase_done, 4 * PH["cross"])
                    for v in range(4):
                        sp.dma_start(cv[:, v, :].rearrange("p (t n) -> p t n", n=D), vd[v]).then_inc(cv_landed[0], 16)
            for b in range(4, DB):
                sp.wait_ge(yo_ready, b - 3)
                sp.dma_start(cv[:, b % 4, :].rearrange("p (t n) -> p t n", n=D), vd[b]).then_inc(cv_landed[1], 16)
            sp.wait_ge(yo_turned, 2)

        def xsample_pool(pool):
            pool.wait_ge(out_stored, 16 * mark["mkv"])
            chains["pool"](nc.gpsimd.memset(cqx[:, :, :, :], 0.0))
            for h in range(XH):
                for k in (2 * h, 2 * h + 1):
                    last = nc.gpsimd.tensor_copy(cqx[:, k, :, h * DT:(h + 1) * DT], cq[:, k, SEQ:N].rearrange("p (b t) -> p b t", t=DT))
            last.then_inc(cqx_ready, 1)

        def xsample_tensor(pe):
            pe.wait_ge(cqx_ready, 1)
            def turn_k(b, q):
                if q == 0:
                    pe.wait_ge(ck_landed[b % 2], 16 * (b // 2 + 1))
                kb = ck[:, b % 2, :].rearrange("p (t n) -> p t n", n=D)
                g = 4 * b + q
                if g >= 2:
                    pe.wait_ge(yk_taken, g - 1)
                for j in range(4):
                    mm = nc.tensor.transpose(PS[:, g % 2, j * P:(j + 1) * P], kb[:, j % 2, (2 * q + j // 2) * P:(2 * q + j // 2 + 1) * P],
                                             IDENT[:, :])
                mm.then_inc(yk_turned, 1)
            for q in range(4):
                turn_k(0, q)
            for quad in range(2):
                for i in range(4):
                    b = 4 * quad + i
                    pe.wait_ge(yk_taken, 4 * (b + 1))
                    if i == 0 and quad:
                        pe.wait_ge(yp_ready, quad)
                    for k in range(KB):
                        mm = nc.tensor.matmul(PS[32 * i:32 * i + 32, 2, 0:NMEM], cqx[:, k, b, :], ckT[b % 2][:, k, :],
                                              start=(k == 0), stop=(k == KB - 1), tile_position=(0, 32 * i))
                        if k == KB - 1:
                            mm.then_inc(ys_ready, 1)
                        if k % 2 and b + 1 < DB:
                            turn_k(b + 1, k // 2)
                pe.wait_ge(yn_ready, quad + 1)
                if quad:
                    pe.wait_ge(yt_taken, quad)
                for m in range(2):
                    mm = nc.tensor.transpose(PS[:, 3, m * P:(m + 1) * P], yl[:, m * P:(m + 1) * P], IDENT[:, :])
                mm.then_inc(yt_ready, 1)
                pe.wait_ge(yt_taken, quad + 1)
                pe.wait_ge(cv_landed[quad], 64)
                if quad:
                    pe.wait_ge(yo_taken, quad)
                for i in range(4):
                    vb = cv[:, i, :].rearrange("p (t n) -> p t n", n=D)
                    rows = slice(32 * i, 32 * i + 32)
                    for half in range(2):
                        for m in range(2):
                            mm = nc.tensor.matmul(PS[rows, 4 + half, :], ypt[:, m, rows], vb[:, m, 512 * half:512 * half + 512],
                                                  start=(m == 0), stop=(m == 1), tile_position=(0, 32 * i))
                    mm.then_inc(yo_ready, 1)
                pe.wait_ge(yv_taken, quad + 1)
                for k in range(KB):
                    mm = nc.tensor.transpose(PS[:, 6 + k // 4, (k % 4) * P:(k % 4 + 1) * P], yo[:, k * P:(k + 1) * P], IDENT[:, :])
                mm.then_inc(yo_turned, 1)

        yv_taken, yo_turned, yo_high = sem("yv_taken"), sem("yo_turned"), sem("yo_high")

        def sample_out(quad, k, x):
            src = PS[:, 6 + k // 4, (k % 4) * P:(k % 4 + 1) * P].rearrange("p (b c) -> p b c", b=4)
            return (x[:, k, SEQ + quad * 32:SEQ + quad * 32 + 32].rearrange("p (b t) -> p b t", b=4),
                    src[:, :, DT * (k // 2):DT * (k // 2) + DT])

        def xsample_scalar(act):
            act.wait_ge(out_stored, 16 * mark["mkv"])
            def take_k(b):
                for q in range(4):
                    g = 4 * b + q
                    act.wait_ge(yk_turned, g + 1)
                    if q == 0 and b >= 2:
                        act.wait_ge(ys_ready, b - 1)
                    nc.scalar.activation(ckT[b % 2][:, 2 * q:2 * q + 2, :], PS[:, g % 2, :].rearrange("p (a b) -> p a b", a=2), ACT.Copy)\
                        .then_inc(yk_taken, 1)
            take_k(0)
            for quad in range(2):
                for i in range(4):
                    if 4 * quad + i + 1 < DB:
                        take_k(4 * quad + i + 1)
                act.wait_ge(ym_ready, quad + 1)
                nc.scalar.activation(yl[:, :], PS[:, 2, 0:NMEM], ACT.Exp, bias=xmax[:, 0:1], accum_out=xsum[:, 0:1]).then_inc(yp_ready, 1)
                act.wait_ge(yt_ready, quad + 1)
                if quad:
                    act.wait_ge(yo_ready, 4 * quad)
                nc.scalar.activation(ypt[:, :, :], PS[:, 3, 0:2 * P].rearrange("p (a b) -> p a b", a=2), ACT.Copy).then_inc(yt_taken, 1)
                act.wait_ge(yo_ready, 4 * quad + 4)
                nc.scalar.activation(yo, PS[:, 4:6, :].rearrange("p a b -> p (a b)"), ACT.Copy).then_inc(yv_taken, 1)
                act.wait_ge(yo_turned, quad + 1)
                for k in range(KB):
                    out, src = sample_out(quad, k, xhi)
                    last = nc.scalar.activation(out, src, ACT.Copy)
                last.then_inc(yo_high, 1)

        def xsample_vector(dve):
            for quad in range(2):
                dve.wait_ge(ys_ready, 4 * quad + 4)
                if quad:
                    dve.wait_ge(yt_ready, quad)
                nc.vector.tensor_reduce(xmax[:, 0:1], PS[:, 2, 0:NMEM], AX_X, ALU.max, negate=True).then_inc(ym_ready, 1)
                dve.wait_ge(yp_ready, quad + 1)
                chains["dve"](nc.vector.reciprocal(xrec[:, 0:1], xsum[:, 0:1]))
                nc.vector.tensor_scalar(yl[:, :], yl[:, :], xrec[:, 0:1], None, ALU.mult).then_inc(yn_ready, 1)
                dve.wait_ge(yo_high, quad + 1)
                for k in range(KB):
                    (hi, src), (lo, _) = sample_out(quad, k, xhi), sample_out(quad, k, xlo)
                    last = nc.vector.tensor_tensor(lo, src, hi.bitcast(F32), ALU.subtract)
                last.then_inc(yo_taken, 1)

        gate_taken, up_taken, h_high, h_low = sem("gate_taken"), sem("up_taken"), sem("hidden_high"), sem("hidden_low")

        def ffn_tensor(pe, nb, n0, q0, others, before_first=lambda k: None):
            def pair(i, first, before=lambda k: None):
                for s in range(2):
                    pe.wait_ge(w_split, i * 2 + (n0 + s + 1))
                    if first:
                        pe.wait_ge(z_taken, others + s - 1)
                    else:
                        pe.wait_ge((gate_taken, up_taken)[s], i + q0)
                    products(s, (xhi, xlo), KB, CHUNKS, before).then_inc(z_ready, 1)
            pair(0, True, before_first)
            with pe.Fori(1, nb) as i:
                pair(i, False)

        def down_tensor(pe, nb, n0, q0):
            pe.wait_ge(gate_taken, q0 + nb)
            proj_tensor(pe, (ghi, glo), KB, n0, nk=nb, ffn_blocks=2 * (q0 + nb), before_first=lambda k: pe.wait_ge(h_low, q0 + k + 1))

        def ffn_scalar(act, nb, n0, q0):
            def pair(i, s, first):
                act.wait_ge(z_ready, i * 4 + (n0 + 2 * s + 1))
                if not first:
                    act.wait_ge(h_low, i * 2 + (q0 + s - 1))
                for c, (t0, w) in enumerate(CHUNKS):
                    last = nc.scalar.activation(silu_g[:, s, t0:t0 + w], PS[:, c, 0:w], ACT.Silu)
                last.then_inc(gate_taken, 1)
                act.wait_ge(up_taken, i * 2 + (q0 + s + 1))
                nc.scalar.activation(ghi[:, bass.ds(i * 2 + s, 1), :], silu_g[:, s:s + 1, :], ACT.Copy).then_inc(h_high, 1)
            if q0 == 0:
                pair(0, 0, True)
                pair(0, 1, True)
            with act.Fori(1 if q0 == 0 else 0, nb // 2) as i:
                pair(i, 0, False)
                pair(i, 1, False)

        def ffn_vector(dve, nb, n0, q0):
            def split_pair(i, s):
                for which in range(2):
                    split_block(dve, i * 2, which, n0 + 2 * s, KB)

            def combine(i, s):
                dve.wait_ge(z_ready, i * 4 + (n0 + 2 * s + 2))
                dve.wait_ge(gate_taken, i * 2 + (q0 + s + 1))
                for c, (t0, w) in enumerate(CHUNKS):
                    last = nc.vector.tensor_tensor(silu_g[:, s, t0:t0 + w], PS[:, 3 + c, 0:w], silu_g[:, s, t0:t0 + w], ALU.mult)
                last.then_inc(up_taken, 1)
                dve.wait_ge(h_high, i * 2 + (q0 + s + 1))
                nc.vector.tensor_tensor(glo[:, bass.ds(i * 2 + s, 1), :], silu_g[:, s:s + 1, :],
                                        ghi[:, bass.ds(i * 2 + s, 1), :].bitcast(F32), ALU.subtract).then_inc(h_low, 1)
            with dve.Fori(0, nb // 2 - 1) as i:
                split_pair(i, 1)
                combine(i, 0)
                split_pair(i + 1, 0)
                combine(i, 1)
            split_pair(nb // 2 - 1, 1)
            combine(nb // 2 - 1, 0)
            split_first(dve, n0 + 2 * nb, nb)
            combine(nb // 2 - 1, 1)

        yst = cut(HB, 0, 4, D)
        y_turned, y_taken = sem("y_turned"), sem("y_taken")
        y_stored = [sem(f"y_stored{i}") for i in range(4)]

        def out_tensor(pe):
            for g in range(2 * TT):
                t, half = g // 2, g % 2
                n = P if t < TT - 1 else NS
                if g >= 4:
                    pe.wait_ge(y_taken, g - 3)
                for j in range(4):
                    mm = nc.tensor.transpose(PS[0:n, g % 4, j * P:(j + 1) * P], xn[:, 4 * half + j, t * P:t * P + n], IDENT[:, :])
                mm.then_inc(y_turned, 1)

        def out_scalar(act):
            for g in range(2 * TT):
                t, half = g // 2, g % 2
                n = P if t < TT - 1 else NS
                act.wait_ge(y_turned, g + 1)
                if t >= 4:
                    act.wait_ge(y_stored[t % 4], 16 * (t // 4))
                nc.scalar.activation(yst[0:n, t % 4, 512 * half:512 * half + 512], PS[0:n, g % 4, :], ACT.Copy).then_inc(y_taken, 1)

        def out_store(sp):
            yp = O["y_p"][0].rearrange("(t p) d -> p t d", p=P)
            for t in range(TT):
                sp.wait_ge(y_taken, 2 * t + 2)
                if t < TT - 1:
                    sp.dma_start(yp[:, t, :], yst[:, t % 4, :]).then_inc(y_stored[t % 4], 16)
                else:
                    sp.dma_start(O["y_s"].rearrange("b t d -> (b t) d"), yst[0:NS, t % 4, :]).then_inc(y_stored[t % 4], 16)
            for s in range(4):
                sp.wait_ge(y_stored[s], 16 * len(range(s, TT, 4)))

        order = ["turn", "att_proj", "kv", "att", "ml_proj", "conv_state", "conv", "gates", "chunks", "sample",
                 "win", "out", "mem_turn", "mem_proj", "mkv", "cq", "cross", "xsample", "co",
                 "ffn_down", "final_norm", "end"]
        PH = {name: i + 1 for i, name in enumerate(order)}
        groups = [(n, sum(FGROUPS[:g])) for g, n in enumerate(FGROUPS)]
        NB = {}
        count = 0
        for name, blocks in (("aq", 4), ("akv", 8), ("qk", 8), ("mv", 4), ("mo", 4), ("out", 8), ("mk", 8), ("mv2", 8), ("cq", 8),
                             ("co", 8), *((f"{x}{g}", 2 * n if x == "ffn" else KB) for g, n in enumerate(FGROUPS) for x in ("ffn", "down"))):
            NB[name] = count
            count += blocks
        MCH = ((0, NMEM),)
        J = {}
        j = 0
        for r, (name, nb) in enumerate((("x", 8), ("att", 4), ("ml", 4), ("mem", 8), ("cross", 8), ("ffn", 8), ("final", 8))):
            J[name] = (j, r, j)
            j += nb
        chains = {}

        block = ctx.enter_context(nc.Block())

        @block.sync
        def _(sp):
            load_inputs(sp)
            win = A["w_in"]
            proj_load(sp, [w_view(win, 0)], 4, NB["aq"])
            sp.wait_ge(phase_done, 4 * PH["turn"])
            sp.dma_start(XT_DRAM, XT0[:, :]).then_inc(xt_stored, 16)
            proj_load(sp, [w_view(win, AW)], 8, NB["akv"])
            sp.wait_ge(phase_done, 4 * PH["att_proj"])
            kv_store(sp)
            sp.wait_ge(phase_done, 4 * PH["kv"])
            att_load(sp)
            ml_loads(sp)
            sp.wait_ge(phase_done, 4 * PH["att"])
            proj_load(sp, [w_view(win, 3 * AW)], 8, NB["qk"])
            proj_load(sp, [w_view(win, 5 * AW)], 4, NB["mv"])
            proj_load(sp, [w_view(win, 6 * AW)], 4, NB["mo"])
            ml_tables(sp)
            conv_store(sp)
            m_store(sp)
            sp.wait_ge(phase_done, 4 * PH["gates"])
            sample_state_load(sp)
            win_load_first(sp)
            state_store(sp)
            win_load(sp)
            sp.wait_ge(phase_done, 4 * PH["win"])
            sp.dma_start(XTF[:, :], XT_DRAM).then_inc(xt_back, 16)
            proj_load(sp, [w_view(A["w_out"])], 8, NB["out"])
            mem_load(sp)
            proj_load(sp, [w_view(A["w_ck"])], 8, NB["mk"])
            proj_load(sp, [w_view(A["w_cv"])], 8, NB["mv2"])
            mkv_store(sp)
            proj_load(sp, [w_view(A["w_cq"])], 8, NB["cq"])
            xsample_load(sp)
            proj_load(sp, [w_view(A["w_co"])], 8, NB["co"])
            for g, (nb, q0) in enumerate(groups):
                proj_load(sp, [w_view(A[w], q0 * P) for w in ("w_gate", "w_up")], 2 * nb, NB[f"ffn{g}"])
                proj_load(sp, [w_view(A["w_down"], 0, q0 * P, nb)], KB, NB[f"down{g}"], nb)
            out_store(sp)
            sp.wait_ge(out_stored, 16 * stores[0])
            sp.wait_ge(cache_stored, 16 * 2 * DB)

        @block.tensor
        def _(pe):
            c = chains["pe"] = Chain(pe, None)
            turn_tensor(pe)
            c.meet()
            norm_tensor(pe, KB, N, *J["x"])
            proj_tensor(pe, (xhi, xlo), 4, NB["aq"], before_first=normed(pe, *J["x"][1:]))
            proj_tensor(pe, (xhi, xlo), 8, NB["akv"])
            c.meet()
            kv_turn_tensor(pe)
            c.meet()
            att_tensor(pe)
            pe.wait_ge(o_taken, len(UNITS))
            att_turn_tensor(pe)
            c.meet()
            gates_tensor(pe)
            pe.wait_ge(gates_read, 1)
            proj_tensor(pe, (xhi, xlo), 8, NB["qk"])
            proj_tensor(pe, (xhi, xlo), 4, NB["mv"])
            proj_tensor(pe, (xhi, xlo), 4, NB["mo"])
            c.meet()
            conv_state_tensor(pe)
            c.meet()
            c.meet()
            k_turn_tensor(pe)
            pe.wait_ge(kt_taken, TT)
            gate_tensor(pe)
            c.meet()
            chunk_tensor(pe)
            c.meet()
            sample_tensor(pe)
            c.meet()
            win_tensor(pe)
            c.meet()
            norm_tensor(pe, 4, N, *J["att"])
            norm_tensor(pe, 4, N, *J["ml"])
            proj_tensor(pe, (xhi, xlo), 8, NB["out"], before_first=normed(pe, J["ml"][1], J["att"][2]))
            c.meet()
            mem_turn_tensor(pe)
            c.meet()
            norm_tensor(pe, KB, NMEM, *J["mem"])
            proj_tensor(pe, (mhi, mlo), 8, NB["mk"], MCH, before_first=normed(pe, *J["mem"][1:]))
            proj_tensor(pe, (mhi, mlo), 8, NB["mv2"], MCH)
            c.meet()
            mkv_turn_tensor(pe)
            c.meet()
            norm_tensor(pe, KB, N, *J["cross"])
            proj_tensor(pe, (xhi, xlo), 8, NB["cq"], before_first=normed(pe, *J["cross"][1:]))
            c.meet()
            cross_tensor(pe)
            c.meet()
            xsample_tensor(pe)
            c.meet()
            proj_tensor(pe, (xhi, xlo), 8, NB["co"])
            c.meet()
            norm_tensor(pe, KB, N, *J["ffn"])
            for g, (nb, q0) in enumerate(groups):
                ffn_tensor(pe, nb, NB[f"ffn{g}"], q0, NB["ffn0"] + g * KB,
                           (lambda k: None) if g else normed(pe, *J["ffn"][1:]))
                down_tensor(pe, nb, NB[f"down{g}"], q0)
            c.meet()
            norm_tensor(pe, KB, N, *J["final"])
            c.meet()
            out_tensor(pe)
            c.meet()

        @block.scalar
        def _(act):
            c = chains["act"] = Chain(act, act_step)
            c.meet()
            norm_scalar(act, x0, xhi, KB, N, *J["x"])
            proj_evac(act, aq, 4, NB["aq"], HD ** -0.5)
            proj_evac(act, akv, 8, NB["akv"])
            c.meet()
            kv_turn_scalar(act)
            c.meet()
            att_scalar(act)
            att_turn_scalar(act)
            c.meet()
            proj_evac(act, qk, 8, NB["qk"])
            for j in range(2 * NP):
                evac_block(act, (mv, sig_o)[j // NP], j % NP // 2, j % 2, NB[("mv", "mo")[j // NP]])
                conv_silu(act, j)
            c.meet()
            conv_state_scalar(act)
            c.meet()
            conv_scalar(act)
            c.meet()
            gate_scalar(act)
            c.meet()
            chunk_scalar(act, range(NC))
            c.meet()
            chunk_scalar(act, [NC])
            c.meet()
            win_scalar(act)
            c.meet()
            norm_scalar(act, cat, xhi, 4, N, *J["att"])
            norm_scalar(act, cat[:, NP:, :], xhi[:, NP:, :], 4, N, *J["ml"])
            c.meet()
            c.meet()
            norm_scalar(act, mem_T, mhi, KB, NMEM, *J["mem"])
            proj_evac(act, mkT, 8, NB["mk"], chunks=MCH)
            proj_evac(act, mvT, 8, NB["mv2"], chunks=MCH)
            c.meet()
            mkv_turn_scalar(act)
            c.meet()
            norm_scalar(act, XT, xhi, KB, N, *J["cross"])
            proj_evac(act, cq, 8, NB["cq"], XD ** -0.5)
            c.meet()
            cross_scalar(act)
            c.meet()
            xsample_scalar(act)
            c.meet()
            c.meet()
            norm_scalar(act, XT, xhi, KB, N, *J["ffn"])
            for g, (nb, q0) in enumerate(groups):
                ffn_scalar(act, nb, NB[f"ffn{g}"], q0)
            c.meet()
            norm_scalar(act, XT, None, KB, N, *J["final"])
            c.meet()
            out_scalar(act)
            c.meet()

        @block.vector
        def _(dve):
            c = chains["dve"] = Chain(dve, dve_step)
            turn_vector(dve)
            c.meet()
            norm_vector(dve, x0, (xhi, xlo), KB, N, G_MIX, *J["x"], lambda: split_first(dve, NB["aq"]))
            proj_split(dve, 4, NB["aq"], 1)
            proj_split(dve, 8, NB["akv"])
            c.meet()
            c.meet()
            att_vector(dve)
            c.meet()
            nc.vector.memset(gate_w[:, :, :], 0.0).then_inc(gw_zeroed, 1)
            gates_split(dve)
            gates_vector(dve)
            proj_split(dve, 8, NB["qk"])
            for j in range(2 * NP):
                split_block(dve, j // 2, j % 2, NB["mv"], KB)
                conv_block(dve, j)
            c.meet()
            gate_bias_vector(dve)
            c.meet()
            conv_vector(dve)
            c.meet()
            k_turn_vector(dve)
            gate_vector(dve)
            c.meet()
            chunk_vector(dve)
            c.meet()
            sample_vector(dve)
            c.meet()
            win_vector(dve)
            c.meet()
            norm_vector(dve, cat, (xhi, xlo), 4, N, G_ATT, *J["att"])
            norm_vector(dve, cat[:, NP:, :], (xhi[:, NP:, :], xlo[:, NP:, :]), 4, N, G_ML, *J["ml"],
                        lambda: split_first(dve, NB["out"]))
            dve.wait_ge(xt_back, 16)
            proj_split_add(dve, XT, 8, NB["out"])
            c.meet()
            mem_turn_vector(dve)
            c.meet()
            norm_vector(dve, mem_T, (mhi, mlo), KB, NMEM, G_MEM, *J["mem"], lambda: split_first(dve, NB["mk"]))
            proj_split(dve, 8, NB["mk"], 1)
            proj_split(dve, 8, NB["mv2"])
            c.meet()
            c.meet()
            norm_vector(dve, XT, (xhi, xlo), KB, N, G_CROSS, *J["cross"], lambda: split_first(dve, NB["cq"]))
            proj_split(dve, 8, NB["cq"], 1)
            c.meet()
            cross_vector(dve)
            c.meet()
            xsample_vector(dve)
            c.meet()
            split_first(dve, NB["co"])
            proj_split_add(dve, XT, 8, NB["co"])
            c.meet()
            norm_vector(dve, XT, (xhi, xlo), KB, N, G_FFN, *J["ffn"], lambda: split_first(dve, NB["ffn0"]))
            for g, (nb, q0) in enumerate(groups):
                ffn_vector(dve, nb, NB[f"ffn{g}"], q0)

                def split_next():
                    if g + 1 < len(groups):
                        split_first(dve, NB[f"ffn{g + 1}"])
                proj_split_add(dve, XT, KB, NB[f"down{g}"], nb, split_next)
            c.meet()
            norm_vector(dve, XT, xn, KB, N, G_FINAL, *J["final"])
            c.meet()
            c.meet()

        @block.gpsimd
        def _(pool):
            c = chains["pool"] = Chain(pool, pool_step)
            for name in order:
                if name == "kv":
                    q_wide_pool(pool)
                elif name == "att":
                    att_pool(pool)
                elif name == "conv_state":
                    conv_state_pool(pool)
                elif name == "gates":
                    q_zero_pool(pool)
                    q_pad_pool(pool, 0)
                    q_pad_pool(pool, 1)
                elif name == "chunks":
                    sample_pool(pool)
                    chunk_pool(pool, range(NC))
                elif name == "sample":
                    q_mask_pool(pool)
                    chunk_pool(pool, [NC])
                elif name == "cross":
                    xsample_pool(pool)
                c.meet()


_INS = ['x_prompt', 'x_sample', 'mem_prompt', 'cache_win_k', 'cache_win_v', 'cache_mem_k', 'cache_mem_v', 'state_conv',
        'state_mlstm_C', 'state_mlstm_n', 'state_mlstm_m', 'g_mix', 'w_in', 'conv_w', 'conv_b', 'b_ig', 'b_fg', 'b_og',
        'g_attn_out', 'g_mlstm_out', 'w_out', 'g_cross', 'g_mem', 'w_cq', 'w_ck', 'w_cv', 'w_co', 'g_ffn', 'w_gate', 'w_up',
        'w_down', 'g_final']
_OUTS = [('y_p', (1, SEQ, D)), ('y_s', (DB, DT, D)), ('win_k_p', (1, SEQ, H, HD)), ('win_v_p', (1, SEQ, H, HD)),
         ('conv_p', (1, 3, D)), ('C_p', (1, H, HD, HD)), ('n_p', (1, H, HD)), ('m_p', (1, H)),
         ('mem_k', (1, NMEM, XH, XD)), ('mem_v', (1, NMEM, XH, XD)), ('win_k_s', (DB, PAST + DT, H, HD)),
         ('win_v_s', (DB, PAST + DT, H, HD)), ('conv_s', (DB, 3, D)), ('C_s', (DB, H, HD, HD)), ('n_s', (DB, H, HD)),
         ('m_s', (DB, H))]


def kernel(**inputs):
    import concourse.bacc as _bacc
    from concourse.bass_utils import run_bass_kernel_spmd as _run

    nc = _bacc.Bacc("TRN2", target_bir_lowering=False, num_devices=1)
    arrays, ins, outs = {}, {}, {}
    given = {name: np.ascontiguousarray(inputs[name]) for name in _INS}
    given.update(constants())
    for name, a in given.items():
        arrays[f"in_{name}_dram"] = a
        ins[name] = nc.dram_tensor(f"in_{name}_dram", a.shape, F32, kind="ExternalInput").ap()
    for name, shape in _OUTS:
        outs[name] = nc.dram_tensor(f"out_{name}_dram", shape, F32, kind="ExternalOutput").ap()
    build(nc, ins, outs)
    r = _run(nc, [arrays], core_ids=[0])
    return tuple(r.results[0][f"out_{name}_dram"] for name, _ in _OUTS)
```
